# Optimizing a Trainium2 kernel written in Bass

```python
import jax, jax.numpy as jnp
from jax import lax
import numpy as np

D_MODEL = 2048
BATCH = 1
SEQ = 256
DEPTH = 1

N_MEM = 256
D_MIX = D_MODEL
D_DELTA = D_MIX // 2
D_CONV = D_MIX - D_DELTA
DN_HEADS = 8
DN_HEAD_DIM = D_DELTA // DN_HEADS
DN_CONV_W = 4
DN_CHUNK = 64
CF_CONV_W = 31
XA_HEADS = 4
XA_HEAD_DIM = D_MODEL // XA_HEADS
D_FF = 4 * D_MODEL
EPS = 1e-6
D_IN = 4 * D_DELTA + 2 * DN_HEADS + 2 * D_CONV


def rms_norm(x, g):
    xf = x.astype(jnp.float32)
    y = xf * lax.rsqrt(jnp.mean(xf * xf, axis=-1, keepdims=True) + EPS)
    return (y * g.astype(jnp.float32)).astype(x.dtype)

def layer_norm(x, g, b):
    xf = x.astype(jnp.float32)
    mu = jnp.mean(xf, axis=-1, keepdims=True)
    xc = xf - mu
    var = jnp.mean(xc * xc, axis=-1, keepdims=True)
    y = xc * lax.rsqrt(var + EPS) * g.astype(jnp.float32) + b.astype(jnp.float32)
    return y.astype(x.dtype)

def l2_normalize(x):
    xf = x.astype(jnp.float32)
    return xf * lax.rsqrt(jnp.sum(xf * xf, axis=-1, keepdims=True) + EPS)

def causal_depthwise_conv(x, w):
    width, ch = w.shape
    return lax.conv_general_dilated(
        x, w[:, None, :].astype(x.dtype), window_strides=(1,), padding=[(width - 1, 0)],
        dimension_numbers=("NWC", "WIO", "NWC"), feature_group_count=ch)

def chunk_gated_delta_rule(q, k, v, g, beta):
    B, T, H, Dk = q.shape
    Dv = v.shape[-1]
    C = DN_CHUNK
    N = T // C

    def to_chunks(t):
        t = t.reshape((B, N, C, H) + t.shape[3:])
        return jnp.moveaxis(t, 3, 1)

    q, k, v, g, beta = (to_chunks(t) for t in (q, k, v, g, beta))
    q = q * (Dk ** -0.5)
    g = jnp.cumsum(g, axis=-1)
    causal = jnp.tril(jnp.ones((C, C), dtype=bool))
    strict = jnp.tril(jnp.ones((C, C), dtype=bool), -1)
    decay = jnp.exp(jnp.where(causal, g[..., :, None] - g[..., None, :], -jnp.inf))

    k_beta = k * beta[..., None]
    v_beta = v * beta[..., None]
    a = jnp.einsum("bhncd,bhnsd->bhncs", k_beta, k) * decay
    t_mat = jnp.eye(C, dtype=jnp.float32) + jnp.where(strict, a, 0.0)
    rhs = jnp.concatenate([v_beta, k_beta * jnp.exp(g)[..., None]], axis=-1)
    sol = lax.linalg.triangular_solve(t_mat, rhs, left_side=True, lower=True, unit_diagonal=True)
    u, w = sol[..., :Dv], sol[..., Dv:]

    attn = jnp.einsum("bhncd,bhnsd->bhncs", q, k) * decay
    q_dec = q * jnp.exp(g)[..., None]
    g_last = g[..., -1]
    k_dec = k * jnp.exp(g_last[..., None] - g)[..., None]

    def step(S, xs):
        q_c, k_c, u_c, w_c, attn_c, gl = xs
        v_new = u_c - jnp.einsum("bhcd,bhde->bhce", w_c, S)
        o = jnp.einsum("bhcd,bhde->bhce", q_c, S) + jnp.einsum("bhcs,bhse->bhce", attn_c, v_new)
        S = S * jnp.exp(gl)[..., None, None] + jnp.einsum("bhcd,bhce->bhde", k_c, v_new)
        return S, o

    xs = tuple(jnp.moveaxis(t, 2, 0) for t in (q_dec, k_dec, u, w, attn, g_last))
    S0 = jnp.zeros((B, H, Dk, Dv), dtype=jnp.float32)
    _, o = lax.scan(step, S0, xs)
    return jnp.transpose(o, (1, 0, 3, 2, 4)).reshape(B, T, H, Dv)

def hybrid_mixer(xn, w_in, dn_conv_w, dn_a_log, dn_dt_bias, dn_norm_g,
                 cf_dw_w, cf_dw_b, cf_ln_g, cf_ln_b, w_out):
    B, T, _ = xn.shape
    proj = xn @ w_in
    qkv, z, b_raw, a_raw, glu = jnp.split(
        proj, [3 * D_DELTA, 4 * D_DELTA, 4 * D_DELTA + DN_HEADS, 4 * D_DELTA + 2 * DN_HEADS], axis=-1)

    qkv = jax.nn.silu(causal_depthwise_conv(qkv, dn_conv_w))
    q, k, v = jnp.split(qkv, 3, axis=-1)
    hd = (B, T, DN_HEADS, DN_HEAD_DIM)
    q = l2_normalize(q.reshape(hd))
    k = l2_normalize(k.reshape(hd))
    v = v.reshape(hd).astype(jnp.float32)
    beta = jax.nn.sigmoid(b_raw.astype(jnp.float32))
    g = -jnp.exp(dn_a_log.astype(jnp.float32)) * jax.nn.softplus(
        a_raw.astype(jnp.float32) + dn_dt_bias.astype(jnp.float32))
    o = chunk_gated_delta_rule(q, k, v, g, beta)
    o = rms_norm(o, dn_norm_g) * jax.nn.silu(z.reshape(hd).astype(jnp.float32))
    o = o.reshape(B, T, D_DELTA).astype(xn.dtype)

    c = glu[..., :D_CONV] * jax.nn.sigmoid(glu[..., D_CONV:])
    c = causal_depthwise_conv(c, cf_dw_w) + cf_dw_b
    c = jax.nn.silu(layer_norm(c, cf_ln_g, cf_ln_b))

    return jnp.concatenate([o, c], axis=-1) @ w_out

def memory_cross_attention(hn, mem_n, w_q, w_k, w_v, w_o):
    B, T, _ = hn.shape
    M = mem_n.shape[1]
    q = (hn @ w_q).reshape(B, T, XA_HEADS, XA_HEAD_DIM)
    k = (mem_n @ w_k).reshape(B, M, XA_HEADS, XA_HEAD_DIM)
    v = (mem_n @ w_v).reshape(B, M, XA_HEADS, XA_HEAD_DIM)
    s = jnp.einsum("bthd,bmhd->bhtm", q, k).astype(jnp.float32) * (XA_HEAD_DIM ** -0.5)
    p = jax.nn.softmax(s, axis=-1).astype(v.dtype)
    o = jnp.einsum("bhtm,bmhd->bthd", p, v).reshape(B, T, D_MODEL)
    return o @ w_o

def squared_relu_mlp(hn, w1, w2):
    return jnp.square(jax.nn.relu(hn @ w1)) @ w2

def first_inputs(seed: int = 0) -> dict:
    key = jax.random.key(seed)
    ks = jax.random.split(key, 24)
    f32 = jnp.float32
    L = DEPTH

    def dense(k, fan_in, fan_out):
        return jax.random.normal(k, (L, fan_in, fan_out), f32) * fan_in ** -0.5

    def gain(k, n):
        return 1.0 + 0.02 * jax.random.normal(k, (L, n), f32)

    dt = jnp.exp(jax.random.uniform(ks[6], (L, DN_HEADS), f32, np.log(1e-3), np.log(1e-1)))
    return {
        "x": jax.random.normal(ks[0], (BATCH, SEQ, D_MODEL), f32),
        "mem": jax.random.normal(ks[1], (BATCH, N_MEM, D_MODEL), f32),
        "norm_mix_g": gain(ks[2], D_MODEL),
        "w_in": dense(ks[3], D_MODEL, D_IN),
        "dn_conv_w": jax.random.normal(ks[4], (L, DN_CONV_W, 3 * D_DELTA), f32) * DN_CONV_W ** -0.5,
        "dn_a_log": jnp.log(jax.random.uniform(ks[5], (L, DN_HEADS), f32, 1.0, 16.0)),
        "dn_dt_bias": dt + jnp.log(-jnp.expm1(-dt)),
        "dn_norm_g": gain(ks[7], DN_HEAD_DIM),
        "cf_dw_w": jax.random.normal(ks[8], (L, CF_CONV_W, D_CONV), f32) * CF_CONV_W ** -0.5,
        "cf_dw_b": 0.02 * jax.random.normal(ks[9], (L, D_CONV), f32),
        "cf_ln_g": gain(ks[10], D_CONV),
        "cf_ln_b": 0.02 * jax.random.normal(ks[11], (L, D_CONV), f32),
        "w_out": dense(ks[12], D_MIX, D_MODEL),
        "norm_xa_g": gain(ks[13], D_MODEL),
        "norm_mem_g": gain(ks[14], D_MODEL),
        "xa_wq": dense(ks[15], D_MODEL, D_MODEL),
        "xa_wk": dense(ks[16], D_MODEL, D_MODEL),
        "xa_wv": dense(ks[17], D_MODEL, D_MODEL),
        "xa_wo": dense(ks[18], D_MODEL, D_MODEL),
        "norm_mlp_g": gain(ks[19], D_MODEL),
        "mlp_w1": dense(ks[20], D_MODEL, D_FF),
        "mlp_w2": dense(ks[21], D_FF, D_MODEL),
        "norm_final_g": 1.0 + 0.02 * jax.random.normal(ks[22], (D_MODEL,), f32),
    }

def first_block(x, mem, norm_mix_g, w_in, dn_conv_w, dn_a_log, dn_dt_bias, dn_norm_g,
              cf_dw_w, cf_dw_b, cf_ln_g, cf_ln_b, w_out, norm_xa_g, norm_mem_g,
              xa_wq, xa_wk, xa_wv, xa_wo, norm_mlp_g, mlp_w1, mlp_w2, norm_final_g):
    h = x
    for i in range(DEPTH):
        h = h + hybrid_mixer(rms_norm(h, norm_mix_g[i]), w_in[i], dn_conv_w[i], dn_a_log[i],
                             dn_dt_bias[i], dn_norm_g[i], cf_dw_w[i], cf_dw_b[i],
                             cf_ln_g[i], cf_ln_b[i], w_out[i])
        h = h + memory_cross_attention(rms_norm(h, norm_xa_g[i]), rms_norm(mem, norm_mem_g[i]),
                                       xa_wq[i], xa_wk[i], xa_wv[i], xa_wo[i])
        h = h + squared_relu_mlp(rms_norm(h, norm_mlp_g[i]), mlp_w1[i], mlp_w2[i])
    return rms_norm(h, norm_final_g)


GRID_W = 64
CTX_LEN = 256

MLA_HEADS = 8
MLA_NOPE = 128
MLA_ROPE = 64
MLA_V = 128
MLA_Q_RANK = 512
MLA_KV_RANK = 512
MLA_SCALE = (MLA_NOPE + MLA_ROPE) ** -0.5
ROPE_BASE = 10000.0

NA_HEADS = 4
NA_HEAD_DIM = 128
NA_KH = 8
NA_KW = 16
NA_SCALE = NA_HEAD_DIM ** -0.5

FN_GROUPS = 4
FN_CH = 128

MLA_WIDTH = MLA_HEADS * MLA_V
NA_WIDTH = NA_HEADS * NA_HEAD_DIM
FN_WIDTH = FN_GROUPS * FN_CH
MIX_WIDTH = MLA_WIDTH + NA_WIDTH + FN_WIDTH
IN_SPLITS = (MLA_Q_RANK, MLA_KV_RANK, MLA_ROPE, NA_WIDTH, NA_WIDTH, NA_WIDTH, FN_WIDTH)
IN_COLS = sum(IN_SPLITS)

D_FF_2 = 5632
CONV_W = 3
Q_BLOCK = 128


def rmsnorm(x, g):
    xf = x.astype(jnp.float32)
    y = xf * lax.rsqrt(jnp.mean(xf * xf, axis=-1, keepdims=True) + EPS)
    return (y * g.astype(jnp.float32)).astype(x.dtype)

def split_columns(u):
    offs = np.cumsum(IN_SPLITS)[:-1].tolist()
    return jnp.split(u, offs, axis=-1)

def axial_angles(rows, cols):
    n = MLA_ROPE // 4
    freqs = ROPE_BASE ** (-jnp.arange(n, dtype=jnp.float32) / n)
    ang_r = rows.astype(jnp.float32)[:, None, None] * freqs
    ang_c = cols.astype(jnp.float32)[:, None, None] * freqs
    return ang_r, ang_c

def rotate(x, ang):
    n = x.shape[-1] // 2
    x1, x2 = x[..., :n], x[..., n:]
    cos, sin = jnp.cos(ang).astype(x.dtype), jnp.sin(ang).astype(x.dtype)
    return jnp.concatenate([x1 * cos - x2 * sin, x2 * cos + x1 * sin], axis=-1)

def axial_rope(x, ang_r, ang_c):
    h = x.shape[-1] // 2
    return jnp.concatenate([rotate(x[..., :h], ang_r), rotate(x[..., h:], ang_c)], axis=-1)

def mla_qkv(c_q, c_kv, k_r, g_q, w_uq, g_kv, w_ukv, angles):
    B, L, _ = c_q.shape
    q = (rmsnorm(c_q, g_q) @ w_uq).reshape(B, L, MLA_HEADS, MLA_NOPE + MLA_ROPE)
    kv = (rmsnorm(c_kv, g_kv) @ w_ukv).reshape(B, L, MLA_HEADS, MLA_NOPE + MLA_V)
    q_nope, q_rope = q[..., :MLA_NOPE], q[..., MLA_NOPE:]
    k_nope, v = kv[..., :MLA_NOPE], kv[..., MLA_NOPE:]
    k_rope = k_r[:, :, None, :]
    if angles is not None:
        q_rope = axial_rope(q_rope, *angles)
        k_rope = axial_rope(k_rope, *angles)
    q = jnp.concatenate([q_nope, q_rope], axis=-1)
    k = jnp.concatenate([k_nope, jnp.broadcast_to(k_rope, (B, L, MLA_HEADS, MLA_ROPE))], axis=-1)
    return q, k, v

def blocked_attention(q, k, v, scale):
    B, L, H, dq = q.shape
    dv = v.shape[-1]
    nb = L // Q_BLOCK
    qb = q.reshape(B, nb, Q_BLOCK, H, dq).transpose(1, 0, 2, 3, 4)

    def one_block(qi):
        s = jnp.einsum('bqhd,bkhd->bhqk', qi, k, preferred_element_type=jnp.float32) * scale
        p = jax.nn.softmax(s, axis=-1).astype(v.dtype)
        return jnp.einsum('bhqk,bkhd->bqhd', p, v)

    o = lax.map(one_block, qb)
    return o.transpose(1, 0, 2, 3, 4).reshape(B, L, H * dv)

def neighborhood_attention(q, k, v, k_ctx, v_ctx, rpb):
    B, S, H, d = q.shape
    rows = S // GRID_W
    kh = min(NA_KH, rows)
    qg = q.reshape(B, rows, GRID_W, H, d)
    kg = k.reshape(B, rows, GRID_W, H, d)
    vg = v.reshape(B, rows, GRID_W, H, d)
    w_idx = jnp.arange(GRID_W)
    col_start = jnp.clip(w_idx - NA_KW // 2, 0, GRID_W - NA_KW)
    col_idx = col_start[:, None] + jnp.arange(NA_KW)
    rel_col = col_idx - w_idx[:, None] + (NA_KW - 1)
    nwin = kh * NA_KW

    def one_row(r):
        rs = jnp.clip(r - kh // 2, 0, rows - kh)
        q_r = lax.dynamic_index_in_dim(qg, r, axis=1, keepdims=False)
        k_rows = lax.dynamic_slice_in_dim(kg, rs, kh, axis=1)
        v_rows = lax.dynamic_slice_in_dim(vg, rs, kh, axis=1)
        k_win = k_rows[:, :, col_idx]
        v_win = v_rows[:, :, col_idx]
        rel_row = rs + jnp.arange(kh) - r + (NA_KH - 1)
        bias = rpb[:, rel_row[None, :, None], rel_col[:, None, :]]
        s_win = jnp.einsum('bwhd,bawjhd->bhwaj', q_r, k_win, preferred_element_type=jnp.float32) * NA_SCALE
        s_win = s_win + bias.astype(jnp.float32)
        s_ctx = jnp.einsum('bwhd,bchd->bhwc', q_r, k_ctx, preferred_element_type=jnp.float32) * NA_SCALE
        s = jnp.concatenate([s_win.reshape(B, H, GRID_W, nwin), s_ctx], axis=-1)
        p = jax.nn.softmax(s, axis=-1).astype(v.dtype)
        p_win = p[..., :nwin].reshape(B, H, GRID_W, kh, NA_KW)
        p_ctx = p[..., nwin:]
        return (jnp.einsum('bhwaj,bawjhd->bwhd', p_win, v_win)
                + jnp.einsum('bhwc,bchd->bwhd', p_ctx, v_ctx))

    o = lax.map(one_row, jnp.arange(rows))
    return o.transpose(1, 0, 2, 3, 4).reshape(B, S, H * d)

def fourier_mix(f, w_fnet):
    B, L, _ = f.shape
    fg = f.reshape(B, L, FN_GROUPS, FN_CH).astype(jnp.float32)
    spec = jnp.fft.fft2(fg, axes=(1, 3), norm='ortho').real.astype(f.dtype)
    return jnp.einsum('blgc,gcd->blgd', spec, w_fnet).reshape(B, L, FN_WIDTH)

def conv_ffn(h, w_up, conv_w, conv_b, w_down):
    L = h.shape[1]
    u = h @ w_up
    up = jnp.pad(u, ((0, 0), (CONV_W // 2, CONV_W // 2), (0, 0)))
    u = sum(up[:, j:j + L] * conv_w[j] for j in range(CONV_W)) + conv_b
    gate, val = jnp.split(u, 2, axis=-1)
    return (jax.nn.silu(gate) * val) @ w_down

def heads(t, n_heads):
    B, L, _ = t.shape
    return t.reshape(B, L, n_heads, -1)

def second_inputs(seed: int = 0) -> dict:
    key = jax.random.key(seed)
    ks = jax.random.split(key, 24)
    D = D_MODEL

    def nrm(k, shape, scale):
        return jax.random.normal(k, shape, jnp.float32) * scale

    return {
        'x': nrm(ks[0], (BATCH, SEQ, D), 1.0),
        'c': nrm(ks[1], (BATCH, D), 1.0),
        'ctx': nrm(ks[2], (BATCH, CTX_LEN, D), 1.0),
        'c_ctx': nrm(ks[3], (D,), 1.0),
        'w_mod': nrm(ks[4], (DEPTH, D, 6 * D), D ** -0.5),
        'b_mod': nrm(ks[5], (DEPTH, 6 * D), 0.02),
        'g_attn': 1.0 + nrm(ks[6], (DEPTH, D), 0.02),
        'g_ffn': 1.0 + nrm(ks[7], (DEPTH, D), 0.02),
        'w_in': nrm(ks[8], (DEPTH, D, IN_COLS), D ** -0.5),
        'g_q': 1.0 + nrm(ks[9], (DEPTH, MLA_Q_RANK), 0.02),
        'w_uq': nrm(ks[10], (DEPTH, MLA_Q_RANK, MLA_HEADS * (MLA_NOPE + MLA_ROPE)), MLA_Q_RANK ** -0.5),
        'g_kv': 1.0 + nrm(ks[11], (DEPTH, MLA_KV_RANK), 0.02),
        'w_ukv': nrm(ks[12], (DEPTH, MLA_KV_RANK, MLA_HEADS * (MLA_NOPE + MLA_V)), MLA_KV_RANK ** -0.5),
        'na_rpb': nrm(ks[13], (DEPTH, NA_HEADS, 2 * NA_KH - 1, 2 * NA_KW - 1), 0.1),
        'w_fnet': nrm(ks[14], (DEPTH, FN_GROUPS, FN_CH, FN_CH), FN_CH ** -0.5),
        'w_out': nrm(ks[15], (DEPTH, MIX_WIDTH, D), MIX_WIDTH ** -0.5),
        'w_up': nrm(ks[16], (DEPTH, D, 2 * D_FF_2), D ** -0.5),
        'conv_w': nrm(ks[17], (DEPTH, CONV_W, 2 * D_FF_2), CONV_W ** -0.5),
        'conv_b': nrm(ks[18], (DEPTH, 2 * D_FF_2), 0.02),
        'w_down': nrm(ks[19], (DEPTH, D_FF_2, D), D_FF_2 ** -0.5),
        'g_final': 1.0 + nrm(ks[20], (D,), 0.02),
    }

def second_block(x, c, ctx, c_ctx, w_mod, b_mod, g_attn, g_ffn, w_in, g_q, w_uq, g_kv, w_ukv,
              na_rpb, w_fnet, w_out, w_up, conv_w, conv_b, w_down, g_final):
    S = x.shape[1]
    pos = jnp.arange(S)
    angles = axial_angles(pos // GRID_W, pos % GRID_W)
    xc = ctx
    mod_in = jax.nn.silu(c)
    modc_in = jax.nn.silu(c_ctx)

    for l in range(DEPTH):
        ctx_out = l < DEPTH - 1
        sh1, sc1, gt1, sh2, sc2, gt2 = jnp.split((mod_in @ w_mod[l] + b_mod[l])[:, None, :], 6, axis=-1)
        csh1, csc1, cgt1, csh2, csc2, cgt2 = jnp.split(modc_in @ w_mod[l] + b_mod[l], 6, axis=-1)

        h = rmsnorm(x, g_attn[l]) * (1 + sc1) + sh1
        hc = rmsnorm(xc, g_attn[l]) * (1 + csc1) + csh1
        cq, ckv, kr, qn, kn, vn, f = split_columns(h @ w_in[l])
        cq_c, ckv_c, kr_c, qn_c, kn_c, vn_c, f_c = split_columns(hc @ w_in[l])

        q_m, k_m, v_m = mla_qkv(cq, ckv, kr, g_q[l], w_uq[l], g_kv[l], w_ukv[l], angles)
        q_mc, k_mc, v_mc = mla_qkv(cq_c, ckv_c, kr_c, g_q[l], w_uq[l], g_kv[l], w_ukv[l], None)
        o_mla = blocked_attention(q_m, jnp.concatenate([k_m, k_mc], axis=1),
                                  jnp.concatenate([v_m, v_mc], axis=1), MLA_SCALE)
        kn_c, vn_c = heads(kn_c, NA_HEADS), heads(vn_c, NA_HEADS)
        o_na = neighborhood_attention(heads(qn, NA_HEADS), heads(kn, NA_HEADS), heads(vn, NA_HEADS),
                                      kn_c, vn_c, na_rpb[l])
        o_fn = fourier_mix(f, w_fnet[l])
        x = x + gt1 * (jnp.concatenate([o_mla, o_na, o_fn], axis=-1) @ w_out[l])

        if ctx_out:
            o_mla_c = blocked_attention(q_mc, k_mc, v_mc, MLA_SCALE)
            o_na_c = blocked_attention(heads(qn_c, NA_HEADS), kn_c, vn_c, NA_SCALE)
            o_fn_c = fourier_mix(f_c, w_fnet[l])
            xc = xc + cgt1 * (jnp.concatenate([o_mla_c, o_na_c, o_fn_c], axis=-1) @ w_out[l])

        h2 = rmsnorm(x, g_ffn[l]) * (1 + sc2) + sh2
        x = x + gt2 * conv_ffn(h2, w_up[l], conv_w[l], conv_b[l], w_down[l])
        if ctx_out:
            h2c = rmsnorm(xc, g_ffn[l]) * (1 + csc2) + csh2
            xc = xc + cgt2 * conv_ffn(h2c, w_up[l], conv_w[l], conv_b[l], w_down[l])

    return rmsnorm(x, g_final)


def setup_inputs(seed=0):
    out = dict(first_inputs(seed))
    for name, value in second_inputs(seed + 1).items():
        if name != "x":
            out[name + "_2"] = value
    return out


def reference(
    x, mem, norm_mix_g, w_in, dn_conv_w, dn_a_log, dn_dt_bias, dn_norm_g, cf_dw_w, cf_dw_b,
    cf_ln_g, cf_ln_b, w_out, norm_xa_g, norm_mem_g, xa_wq, xa_wk, xa_wv, xa_wo, norm_mlp_g,
    mlp_w1, mlp_w2, norm_final_g, c_2, ctx_2, c_ctx_2, w_mod_2, b_mod_2, g_attn_2, g_ffn_2,
    w_in_2, g_q_2, w_uq_2, g_kv_2, w_ukv_2, na_rpb_2, w_fnet_2, w_out_2, w_up_2, conv_w_2,
    conv_b_2, w_down_2, g_final_2,
):
    x = first_block(
        x, mem, norm_mix_g, w_in, dn_conv_w, dn_a_log, dn_dt_bias, dn_norm_g, cf_dw_w, cf_dw_b,
        cf_ln_g, cf_ln_b, w_out, norm_xa_g, norm_mem_g, xa_wq, xa_wk, xa_wv, xa_wo, norm_mlp_g,
        mlp_w1, mlp_w2, norm_final_g,
    )
    return second_block(
        x, c_2, ctx_2, c_ctx_2, w_mod_2, b_mod_2, g_attn_2, g_ffn_2, w_in_2, g_q_2, w_uq_2,
        g_kv_2, w_ukv_2, na_rpb_2, w_fnet_2, w_out_2, w_up_2, conv_w_2, conv_b_2, w_down_2,
        g_final_2,
    )


_drawn_inputs = setup_inputs


def setup_inputs(seed=0):
    import zlib

    import numpy as np

    out = dict(_drawn_inputs(seed))
    spreads = {}
    factors = {'norm_mix_g': 3.246,
     'dn_norm_g': 6.69,
     'cf_dw_b': 3.19,
     'cf_ln_g': 5.701,
     'cf_ln_b': 6.518,
     'norm_xa_g': 8.0,
     'norm_mem_g': 8.0,
     'norm_mlp_g': 3.243,
     'g_attn_2': 8.0,
     'g_ffn_2': 4.246,
     'g_q_2': 8.0,
     'g_kv_2': 8.0,
     'na_rpb_2': 8.0,
     'conv_b_2': 4.895,
     'g_final_2': 2.783}
    for name, (base, spread) in spreads.items():
        noise = np.random.default_rng([zlib.crc32(name.encode()), seed]).standard_normal(out[name].shape)
        drawn = base * np.exp(spread * noise) if base else spread * noise
        out[name] = __import__('jax').numpy.asarray(drawn.astype(out[name].dtype))
    for name, factor in factors.items():
        out[name] = (out[name] * factor).astype(out[name].dtype)
    return out
```

```python
import numpy as np
from contextlib import ExitStack

import concourse.bass as bass
from concourse import mybir
from concourse.alu_op_type import AluOpType as ALU

F32 = mybir.dt.float32
F32R = mybir.dt.float32r
ACT = mybir.ActivationFunctionType
AX = mybir.AxisListType
ds = bass.ds

P = 128
D = 2048
T = 256
DC = D // P
TT = T // P
EPS = 1e-6
D_DELTA, D_CONV = 1024, 1024
DN_H, DN_TAPS, CF_TAPS = 8, 4, 31
XA_H = 4
XA_CH = DC // XA_H
XA_SCALE = float(512) ** -0.5
D_FF1, D_FF2 = 8192, 5632
MLA_H, NOPE, ROPE, LAT = 8, 128, 64, 512
LC = LAT // P
MLA_SCALE = float(NOPE + ROPE) ** -0.5
NA_H, NA_KH, NA_KW, GRID_W = 4, 8, 16, 64
NA_SCALE = float(P) ** -0.5
FN_G = 4
FN_SCALE = float(T * P) ** -0.5
NEG = -1e30

SLOT = 1024
RAW_N, SPL_N, MOD_N = 8, 4, 2
NCOL = 256
LAG = 3


class Phase:

    def __init__(self, name, nblocks, chunks, per_body=2, per_slot=4, ncol=NCOL, flip=False, mod=0):
        self.name, self.nblocks, self.chunks, self.flip, self.mod = name, nblocks, chunks, flip, mod
        self.K, self.per_slot, self.ncol = per_body, per_slot, ncol
        self.iters = nblocks // per_body
        self.slots_per_block = -(-chunks // per_slot)
        self.S = self.slots_per_block * per_body
        self.slots = self.slots_per_block * nblocks


FF1_ROUNDS = 4
FF2_ROUNDS = (16, 16, 12)


def phases():
    out = [
        Phase("glu", 8, DC), Phase("qkv", 12, DC), Phase("z", 4, DC),
        Phase("wout", 8, DC),
        Phase("memk", 8, DC, mod=2), Phase("memv", 8, DC, flip=True, mod=2),
        Phase("wq", 8, DC, mod=2), Phase("wo", 8, DC, mod=2),
    ]
    for r in range(FF1_ROUNDS):
        out += [Phase(f"w1_{r}", 8, DC, mod=1), Phase(f"w2_{r}", 8, DC, mod=1)]
    for who in ("c", "x"):
        out += [Phase("ckv_" + who, 2, DC), Phase("nak_" + who, 2, DC), Phase("nav_" + who, 2, DC, flip=True)]
        if who == "x":
            out += [Phase("cq", 2, DC), Phase("naq", 2, DC), Phase("fn", 2, DC)]
        out += [Phase("kr_" + who, 1, DC, per_body=1, per_slot=8, ncol=P)]
    for who in ("c", "x"):
        out += [Phase("kn_" + who, 4, LC, per_body=4), Phase("v_" + who, 4, LC, per_body=4, flip=True)]
    out += [Phase("qn", 4, LC, per_body=4), Phase("qr", 2, LC, per_body=2)]
    out += [Phase("wout2", 8, DC)]
    for r, n in enumerate(FF2_ROUNDS):
        out += [Phase(f"up_{r}", n, DC, per_body=2 if n % 2 == 0 else 1)]
        out += [Phase(f"down_{r}", 8, n, per_body=2 if n == 16 else 8)]
    slot = block = mod = 0
    mod_block = {1: MOD_CTX, 2: 0}
    for ph in out:
        ph.slot0, ph.block0 = slot, block
        ph.mod0 = mod
        if ph.mod:
            ph.mod_block0 = mod_block[ph.mod]
            mod_block[ph.mod] += ph.iters
        slot += ph.slots
        block += ph.nblocks
        mod += ph.iters if ph.mod else 0
        assert ph.iters == 1 or (ph.S % RAW_N == 0 and ph.K % 2 == 0), ph.name
    return {ph.name: ph for ph in out}, slot


MOD_BODIES = 48
MOD_CTX = 16
MOD_AT = ((0, 1, 2), (3, 4, 5), (6, 7, 8), (9, 10, 11), (12, 13), (14, 15))
PRE = 3
PH, N_SLOTS = phases()
MOD_BLOCKS = [ph.mod_block0 + i for ph in PH.values() if ph.mod for i in range(ph.iters)]


def columns(parts):
    at, out = 0, {}
    for name, n in parts:
        out[name] = (at, at + n)
        at += n
    return out, at


PV, N_PV = columns([
    ("norm_mix", DC), ("norm_mem", DC), ("norm_xa", DC), ("norm_mlp", DC), ("norm_final", DC),
    ("g_attn", DC), ("g_ffn", DC), ("g_final", DC), ("g_q", LC), ("g_kv", LC), ("dn_norm", 1),
    ("cf_b", 8), ("ln_g", 8), ("ln_b", 8), ("dn_conv", 24 * DN_TAPS), ("cf_conv", 8 * CF_TAPS),
    ("ff_conv", 88 * 3), ("ff_b", 88), ("b_mod", 96), ("c", DC), ("c_ctx", DC), ("a_log", 8), ("dt", 8),
])
CM, N_CM = columns([
    ("levels", 7 * P), ("upper", P), ("below", P), ("w_ba", DC * 16)])
CA, N_CA = columns([
    ("dft_ch", 2 * P), ("dft_cos", TT * T), ("dft_sin", TT * T), ("cos", T), ("sin", T), ("swap", P),
    ("w_fnet", FN_G * P)])
N_CZ = max(N_CM, N_CA)



def build(nc, x_t, mem_t, ctx_t, stream, mods, pvec, eye, cmix, catt, na_bias, na_mask, out_t):
    es = ExitStack()
    with es:
        def sb(name, shape, dt=F32, stack=None):
            return (stack or es).enter_context(nc.sbuf_tensor(name, shape, dt))

        def sem(name):
            return es.enter_context(nc.semaphore(name))

        raw = sb("raw", [P, RAW_N, SLOT])
        whi = sb("whi", [P, SPL_N, SLOT], F32R)
        wlo = sb("wlo", [P, SPL_N, SLOT], F32R)
        act = sb("act", [P, 2, DC, T], F32R)
        h = sb("h", [P, DC, T])
        tmp = sb("tmp", [P, DC, T])
        pv = sb("pv", [P, N_PV])
        cz = sb("cz", [P, N_CZ])
        ident = sb("ident", [P, P])
        ones = sb("ones", [P, P])
        stat = sb("stat", [P, 2, 512])
        modt = sb("modt", [P, P])
        small = sb("small", [P, 256])
        gt = sb("gt", [P, 12, 16])
        ev = sb("ev", [P, 2, 512])
        with ExitStack() as first:
            modraw = sb("modraw", [P, MOD_N, SLOT], stack=first)
            modacc = sb("modacc", [P, 4, NCOL], stack=first)
            with ExitStack() as mixer:
                qkvT = sb("qkvT", [P, 24, T], stack=mixer)
                zT = sb("zT", [P, 8, T], stack=mixer)
                cin = sb("cin", [P, 8, T + CF_TAPS - 1], stack=mixer)
            with ExitStack() as cross:
                memK = sb("memK", [P, DC, T], stack=cross)
                memV = sb("memV", [P, TT, D], stack=cross)
            with ExitStack() as mlp:
                hid = sb("hid", [P, 2, DC, T], F32R, stack=mlp)
        with ExitStack() as second:
            cq = sb("cq", [P, LC, T], stack=second)
            ckv = sb("ckv", [P, 2, LC, T], stack=second)
            kr = sb("kr", [P, 2, T], stack=second)
            with ExitStack() as local:
                naK = sb("naK", [P, NA_H, 2, T], stack=local)
                naV = sb("naV", [P, 2, TT, NA_H * P], stack=local)
                naQ = sb("naQ", [P, NA_H, T], stack=local)
                fT = sb("fT", [P, FN_G, T], stack=local)
                bias = sb("bias", [P, NA_H, TT, T], stack=local)
                mask = sb("mask", [P, TT, T], stack=local)
            with ExitStack() as latent:
                kN = sb("kN", [P, MLA_H, 2, T], stack=latent)
                mlaV = sb("mlaV", [P, 2, TT, MLA_H * P], stack=latent)
                qR = sb("qR", [P, MLA_H // 2, T], stack=latent)
        qN = tmp[:, 8:16, :]

        def tiles(t, n):
            flat = t.rearrange("p a b -> p (a b)") if len(t.shape) == 3 else t
            return [flat[:, 512 * k:512 * k + 512].rearrange("p (a b) -> p a b", a=4) for k in range(n)]
        T_TMP, T_CIN, T_EV = tiles(tmp[:, :, :], 8), tiles(cin[:, :, :], 4), tiles(ev[:, :, :], 2)
        T_STAT, T_MOD = tiles(stat[:, :, :], 2), tiles(modraw[:, :, :], 4)
        X, XT, Y, MT = ([T_TMP[4 * hg + k] for hg in range(2)] for k in range(4))
        AT, ATT = ([T_CIN[2 * hg + k] for hg in range(2)] for k in range(2))
        VB, ST = T_EV, T_STAT
        KW, QDT = ([T_MOD[2 * hg + k] for hg in range(2)] for k in range(2))
        KBT, EG, DT = X, Y, MT
        U_, VN, WT = AT, MT, Y

        bank = [es.enter_context(nc.psum_tensor(f"bank{i}", [P, 512], F32)) for i in range(8)]

        def b2(k):
            return bank[k][:, :].rearrange("p (a b) -> p a b", a=2)

        def b4(k):
            return bank[k][:, :].rearrange("p (a b) -> p a b", a=4)

        def par(name, k=0, n=1):
            return pv[:, PV[name][0] + k:PV[name][0] + k + n] if isinstance(k, int) else pv[:, ds(k + PV[name][0], n)]

        def cc(table, name):
            return cz[:, table[name][0]:table[name][1]]

        raw_in = [sem(f"raw_in{k}") for k in range(RAW_N)]
        mod_in = [sem(f"mod_in{k}") for k in range(MOD_N)]
        mod_used = sem("mod_used")
        mod_out = sem("mod_out")
        hi_done = sem("hi_done")
        split_done = sem("split_done")
        slot_used = sem("slot_used")
        block_free = sem("block_free")
        ev_a = sem("ev_a")
        ev_v = sem("ev_v")
        act_step = sem("act_step")
        dve_step = sem("dve_step")
        params_in = sem("params_in")
        late_in = sem("late_in")
        src_in = sem("src_in")
        squares = sem("squares")
        sums = sem("sums")
        var = sem("var")
        std = sem("std")
        normed = sem("normed")
        norm_hi = sem("norm_hi")
        act_ready = sem("act_ready")
        gate_pe, gate_act, gate_dve = sem("gate_pe"), sem("gate_act"), sem("gate_dve")
        l2_pe, l2_act, l2_dve, l2_sq = sem("l2_pe"), sem("l2_act"), sem("l2_dve"), sem("l2_sq")
        cf_pe, cf_act, cf_dve = sem("cf_pe"), sem("cf_act"), sem("cf_dve")
        dl_pe, dl_act, dl_dve = ([sem(f"dl_{e}{hg}") for hg in range(2)] for e in ("pe", "act", "dve"))
        on_pe, on_act, on_dve = sem("on_pe"), sem("on_act"), sem("on_dve")
        scores, maxes, exps, probs = sem("scores"), sem("maxes"), sem("exps"), sem("probs")
        probs_t, probs_c, heads, head_hi = sem("probs_t"), sem("probs_c"), sem("heads"), sem("head_hi")
        fn_pe, fn_act = sem("fn_pe"), sem("fn_act")
        ctx_in, bias_in, mem_in = sem("ctx_in"), sem("bias_in"), sem("mem_in")
        mixed = sem("mixed")
        rope_pe, rope_dve = sem("rope_pe"), sem("rope_dve")
        mod_ready = sem("mod_ready")
        bias_ready = sem("bias_ready")
        out_ready, stored = sem("out_ready"), sem("stored")
        EV0 = 1
        EV_UP = 1
        FREE = 2

        class Counts:

            def __init__(self, eng):
                self.eng, self.base = eng, {}

            def at(self, s, n):
                v = n + self.base.get(s.name, 0)
                if not isinstance(v, int) or v > 0:
                    self.eng.wait_ge(s, v)

            def end(self, s, n):
                self.base[s.name] = self.base.get(s.name, 0) + n

        class Chain:

            def __init__(self, eng, s):
                self.eng, self.s, self.n, self.i, self.per = eng, s, 0, 0, 0

            def __call__(self, ins):
                ins.then_inc(self.s, 1)
                self.n += 1
                self.eng.wait_ge(self.s, self.i * self.per + self.n)

            def tick(self, ins):
                ins.then_inc(self.s, 1)
                self.n += 1

            def now(self):
                return self.i * self.per + self.n

            def loop(self, i, per):
                self.n, self.i, self.per, self.mark = self.n - per, i, per, self.n

            def end(self, iters):
                assert self.n == self.mark, (self.n, self.mark)
                self.n, self.i, self.per = self.n + self.per * (iters - 1), 0, 0

        block = es.enter_context(nc.Block())

        def over(eng, ph, slot_of, evac_fn, chain, links, extra=None):
            ends = [(k + 1) * ph.slots_per_block - 1 + LAG for k in range(ph.K)]
            order = list(PH.values())
            n = order.index(ph)
            slot_fn = slot_of(ph)

            def body(i, first, done):
                for j in range(ph.S):
                    if j >= done:
                        slot_fn(i, j)
                    if extra:
                        extra(i, j)
                    for k, t in enumerate(ends):
                        if t == j:
                            evac_fn(i * ph.K + k, (ph.block0 + k) % 2)
                        elif t - ph.S == j and not first:
                            evac_fn((i - 1) * ph.K + k, (ph.block0 + k) % 2)

            body(0, True, min(PRE, ph.S) if n else 0)
            if ph.iters > 1:
                with eng.Fori(1, ph.iters) as i:
                    chain.loop(i, links)
                    body(i, False, 0)
                chain.end(ph.iters)
            after = order[n + 1] if n + 1 < len(order) else None
            for j in range(LAG):
                if after and j < min(PRE, after.S):
                    slot_of(after)(0, j)
                for k, t in enumerate(ends):
                    if t - ph.S == j:
                        evac_fn((ph.iters - 1) * ph.K + k, (ph.block0 + k) % 2)

        @block.sync
        def _(sp):
            def load(body, j):
                sp.wait_ge(split_done, body * RAW_N + (j + 1))
                sp.dma_start(raw[:, j, :], stream[ds(body * RAW_N + j, 1), :, :].rearrange("a p n -> (a p) n")
                             ).then_inc(raw_in[j], 16)

            def load_mod(body, q):
                sp.wait_ge(mod_used, body * 4 + (q + 1))
                sp.dma_start(modraw[:, q % MOD_N, :], mods[ds(body * 4 + q, 1), :, :].rearrange("a p n -> (a p) n")
                             ).then_inc(mod_in[q % MOD_N], 16)

            def bodies(first, last, mod=False):
                with sp.Fori(first, last) as b:
                    for j in range(RAW_N):
                        load(b, j)
                        if mod and j % 2:
                            load_mod(b - first, j // 2)

            with_mod = PH["memk"].slot0 // RAW_N
            bodies(0, with_mod)
            bodies(with_mod, with_mod + MOD_BODIES, True)
            bodies(with_mod + MOD_BODIES, N_SLOTS // RAW_N)
            for j in range(N_SLOTS % RAW_N):
                load(N_SLOTS // RAW_N, j)
            sp.wait_ge(out_ready, 1)
            sp.dma_start(out_t, tmp[:, :, :]).then_inc(stored, 16)
            sp.wait_ge(stored, 16)

        @block.gpsimd
        def _(pool):
            for dst, src in ((pv, pvec), (ident, eye[:, 0:P]), (ones, eye[:, P:2 * P]), (cz[:, 0:N_CM], cmix)):
                pool.dma_start(dst[:, :] if dst is not cz else dst, src).then_inc(params_in, 16)
            pool.dma_start(h[:, :, :], x_t).then_inc(src_in, 16)
            pool.wait_ge(mixed, 1)
            pool.dma_start(memV[:, :, :].rearrange("p a b -> p (a b)"), mem_t).then_inc(mem_in, 16)
            pool.dma_start(cz[:, 0:N_CA], catt).then_inc(late_in, 16)
            last = PH["w2_3"]
            pool.wait_ge(block_free, FREE + last.block0 + last.nblocks)
            pool.dma_start(kN[:, :, :, :].rearrange("p a b c -> p (a b c)"), ctx_t).then_inc(ctx_in, 16)
            pool.dma_start(bias[:, :, :, :].rearrange("p a b c -> p (a b c)"), na_bias).then_inc(bias_in, 16)
            pool.dma_start(mask[:, :, :].rearrange("p a b -> p (a b)"), na_mask).then_inc(bias_in, 16)

        BETA, A1, LN1, EA, G, GC, NGC, EGC, BEG, KDL, KDS = range(11)
        C_SILU, GAIN_X, GAIN_C, GAIN_F, SM = 0, 32, 48, 64, 96

        def gtc(row, ch, hd, n=1):
            return gt[:, row, ch * 8 + hd:ch * 8 + hd + n]

        LEVELS = 7
        GROUPS, CHUNKS = range(2), range(TT)
        PE_SIG = [["bc", "tr", "aa"] + [f"{a}{l}" for l in range(LEVELS) for a in "yz"] + ["uw"] + ["ws"] * ch + ["o"]
                  for ch in CHUNKS]
        ACT_SIG = [["eg"] * ch + ["dtx"] + ["kds"] * (1 - ch) + ["tok"] + [f"y{l}" for l in range(LEVELS)] + ["uc", "oc"]
                   for ch in CHUNKS]
        DVE_SIG = [["dta"] + ["kdl"] * (1 - ch) + ["kb", "vb", "aat", "m0"] + [a for l in range(LEVELS)
                   for a in ([f"m{l + 1}"] if l + 1 < LEVELS else []) + [f"x{l}"]] + ["vn"] * ch for ch in CHUNKS]

        def step(table, ch, name):
            return sum(len(table[k]) for k in range(ch)) + table[ch].index(name) + 1

        def bk(hg, k):
            return b4(4 * hg + k)

        def attention_units(kind):
            return [(hd, mt) for hd in range({"cross": XA_H, "mla": MLA_H, "na": NA_H}[kind]) for mt in range(TT)]

        def key_tiles(kind):
            return TT if kind == "cross" else 2 * TT

        @block.tensor
        def _(pe):
            c = Counts(pe)

            def phase(ph, src, c0=0):
                def body(i):
                    for k in range(ph.K):
                        b = bank[(ph.block0 + k) % 2]
                        pe.wait_ge(block_free, i * ph.K + (ph.block0 + k + 1))
                        for sl in range(ph.slots_per_block):
                            j = k * ph.slots_per_block + sl
                            pe.wait_ge(split_done, i * ph.S + (ph.slot0 + j + 1 + RAW_N))
                            buf = (ph.slot0 + j) % SPL_N
                            for ci in range(ph.per_slot):
                                kc = sl * ph.per_slot + ci
                                for hf in range(ph.ncol // P if not ph.flip else TT):
                                    for n, (wx, ax) in enumerate(((whi, 0), (whi, 1), (wlo, 0))):
                                        if ph.flip:
                                            lhs = src[:, ax, c0 + kc, hf * P:(hf + 1) * P]
                                            rhs = wx[:, buf, ci * NCOL:(ci + 1) * NCOL]
                                        else:
                                            lhs = wx[:, buf, ci * ph.ncol + hf * P:ci * ph.ncol + (hf + 1) * P]
                                            rhs = src[:, ax, c0 + kc, :]
                                        mm = pe.matmul(b[:, hf * T:(hf + 1) * T], lhs, rhs,
                                                       start=(kc == 0 and hf == 0 and n == 0),
                                                       stop=(kc == ph.chunks - 1 and n == 2), skip_group_check=True)
                            mm.then_inc(slot_used, 1)
                            if ph.mod and j == 6:
                                mod_matmuls(ph, i)
                if ph.iters > 1:
                    with pe.Fori(0, ph.iters) as i:
                        body(i)
                else:
                    body(0)

            def mod_matmuls(ph, i):
                mb = i + ph.mod0
                pe.wait_ge(mod_used, mb * 4 + (4 + MOD_N))
                for w in range(ph.mod):
                    for hf in range(2):
                        for e in range(2):
                            mm = pe.matmul(bank[2][:, ds(i * 2 + (2 * ph.mod_block0 + 96 * w + hf), 1)], modacc[:, 2 * w + e, hf * P:(hf + 1) * P],
                                           ones[:, 0:1], start=(e == 0), stop=(e == 1), skip_group_check=True)
                mm.then_inc(mod_out, 1)

            def norm(chunks=DC):
                for q in range(chunks // 4):
                    c.at(squares, q + 1)
                    for k in range(4 * q, 4 * q + 4):
                        mm = pe.matmul(bank[3][:, 0:T], ones[:, :], tmp[:, k, :], start=(k == 0), stop=(k == chunks - 1))
                mm.then_inc(sums, 1)
                c.end(squares, chunks // 4)

            def act_in(n):
                c.at(act_ready, n)
                c.end(act_ready, n)

            def phase_out(ph):
                pe.wait_ge(block_free, FREE + ph.block0 + ph.nblocks)

            pe.wait_ge(params_in, 64)
            norm()
            act_in(4)
            for mt in range(TT):
                for k in range(DC):
                    mm = pe.matmul(bank[3][:, 16 * mt:16 * mt + 16], tmp[:, k, mt * P:(mt + 1) * P],
                                   cc(CM, "w_ba")[:, 16 * k:16 * k + 16], start=(k == 0), stop=(k == DC - 1))
            mm.then_inc(gate_pe, 1)
            for name in ("glu", "qkv", "z"):
                phase(PH[name], act)
            def channel_sums(c0, s_, n):
                c.at(s_, n)
                for k in range(8):
                    mm = pe.matmul(bank[2][:, 0:T], ones[:, :], tmp[:, c0 + k, :], start=(k == 0), stop=(k == 7))
                mm.then_inc(cf_pe, 1)
            channel_sums(0, cf_dve, 1)
            c.at(gate_dve, 2)
            for mt in range(TT):
                mm = pe.matmul(bank[3][:, 32 + 8 * mt:40 + 8 * mt], cc(CM, "upper"), gtc(G, mt, 0, 8), start=True, stop=True)
            mm.then_inc(gate_pe, 1)
            for p in range(8):
                c.at(l2_sq, p + 1)
                if p >= 4:
                    c.at(l2_dve, p - 3)
                pe.matmul(bank[4 + p % 4][:, :], ones[:, :], ev[:, p % 2, :], start=True, stop=True).then_inc(l2_pe, 1)
                if p == 1:
                    channel_sums(8, cf_act, 1)
            c.at(cf_dve, 7)
            for ch in CHUNKS:
                tok = slice(ch * P, (ch + 1) * P)

                def a(hg, name):
                    c.at(dl_act[hg], step(ACT_SIG, ch, name))

                def v(hg, name):
                    c.at(dl_dve[hg], step(DVE_SIG, ch, name))
                for hg in GROUPS:
                    if ch:
                        c.at(dl_act[hg], step(ACT_SIG, ch - 1, "oc"))
                    for n in range(4):
                        pe.matmul(bk(hg, 0)[:, n, :], gtc(G, ch, 4 * hg + n).to_broadcast([P, P]), cc(CM, "upper"), start=True, stop=True)
                    for n in range(4):
                        mm = pe.matmul(bk(hg, 1)[:, n, :], gtc(BETA, ch, 4 * hg + n).to_broadcast([P, P]), ident[:, :], start=True, stop=True)
                    mm.then_inc(dl_pe[hg], 1)
                    for n in range(4):
                        pe.transpose(bk(hg, 2)[:, n, :], qkvT[:, 8 + 4 * hg + n, tok], ident[:, :])
                    for n in range(4):
                        mm = pe.transpose(bk(hg, 3)[:, n, :], qkvT[:, 16 + 4 * hg + n, tok], ident[:, :])
                    mm.then_inc(dl_pe[hg], 1)
                for hg in GROUPS:
                    v(hg, "kb")
                    for n in range(4):
                        pe.matmul(bk(hg, 0)[:, n, :], qkvT[:, 8 + 4 * hg + n, tok], KBT[hg][:, n, :], start=True, stop=True)
                    for n in range(4):
                        mm = pe.matmul(bk(hg, 1)[:, n, :], qkvT[:, 8 + 4 * hg + n, tok], qkvT[:, 4 * hg + n, tok], start=True, stop=True)
                    mm.then_inc(dl_pe[hg], 1)
                for lv in range(LEVELS):
                    for hg in GROUPS:
                        v(hg, f"m{lv}")
                        if lv:
                            v(hg, f"x{lv - 1}")
                        for n in range(4):
                            mm = pe.matmul(bk(hg, 0)[:, n, :], MT[hg][:, n, :], X[hg][:, n, :], start=True, stop=True)
                        mm.then_inc(dl_pe[hg], 1)
                    for hg in GROUPS:
                        a(hg, f"y{lv}")
                        if lv + 1 < LEVELS:
                            for n in range(4):
                                pe.matmul(bk(hg, 2)[:, n, :], XT[hg][:, n, :], Y[hg][:, n, :], start=True, stop=True)
                        for n in range(4):
                            mm = pe.matmul(bk(hg, 3)[:, n, :], Y[hg][:, n, :], XT[hg][:, n, :], start=True, stop=True)
                        mm.then_inc(dl_pe[hg], 1)
                for hg in GROUPS:
                    v(hg, f"x{LEVELS - 1}")
                    for n in range(4):
                        mm = pe.matmul(bk(hg, 1)[:, n, :], XT[hg][:, n, :], VB[hg][:, n, :], start=True, stop=True)
                    if ch:
                        for n in range(4):
                            mm = pe.matmul(bk(hg, 2)[:, n, :], KW[hg][:, n, :], XT[hg][:, n, :], start=True, stop=True)
                    mm.then_inc(dl_pe[hg], 1)
                if ch:
                    for hg in GROUPS:
                        a(hg, "uc")
                        for n in range(4):
                            mm = pe.matmul(bk(hg, 0)[:, n, :], WT[hg][:, n, :], ST[hg][:, n, :], start=True, stop=True)
                        mm.then_inc(dl_pe[hg], 1)
                for hg in GROUPS:
                    if ch:
                        v(hg, "vn")
                    else:
                        a(hg, "uc")
                    for n in range(4):
                        if ch:
                            pe.matmul(bk(hg, 3)[:, n, :], ST[hg][:, n, :], QDT[hg][:, n, :], start=True, stop=False)
                        mm = pe.matmul(bk(hg, 3)[:, n, :], VN[hg][:, n, :], ATT[hg][:, n, :], start=not ch, stop=True)
                    if not ch:
                        for n in range(4):
                            mm = pe.matmul(bk(hg, 2)[:, n, :], KW[hg][:, n, :], VN[hg][:, n, :], start=True, stop=True)
                    mm.then_inc(dl_pe[hg], 1)
            for p in range(4):
                c.at(on_act, p // 2 + 1)
                pe.matmul(bank[4 + p][:, :], ones[:, :], tmp[:, 2 * p:2 * p + 2, :], start=True, stop=True).then_inc(on_pe, 1)
            act_in(2 + 4)
            phase(PH["wout"], act)

            norm()
            act_in(4)
            phase(PH["memk"], act)
            phase(PH["memv"], act)
            norm()
            act_in(4)
            phase(PH["wq"], act)

            def attention(kind):
                units = attention_units(kind)
                kt = key_tiles(kind)
                for u in range(len(units) + 2):
                    if u < len(units):
                        hd, mt = units[u]
                        tok = slice(mt * P, (mt + 1) * P)
                        b = bank[3 + u % 2]
                        if kind == "cross":
                            for k in range(XA_CH):
                                mm = pe.matmul(b[:, 0:T], tmp[:, XA_CH * hd + k, tok], memK[:, XA_CH * hd + k, :],
                                               start=(k == 0), stop=(k == XA_CH - 1))
                        elif kind == "na":
                            mm = pe.matmul(b[:, :], naQ[:, hd, tok], naK[:, hd, :, :], start=True, stop=True)
                        else:
                            lo = ROPE * (hd % 2)
                            pe.matmul(b[:, :], qN[:, hd, tok], kN[:, hd, :, :], start=True, stop=False)
                            mm = pe.matmul(b[:, :], qR[lo:lo + ROPE, hd // 2, tok], kr[lo:lo + ROPE, :, :], start=False, stop=True)
                        mm.then_inc(scores, 1)
                    if 1 <= u <= len(units):
                        w = u - 1
                        c.at(probs, w + 1)
                        if w >= 2:
                            c.at(probs_c, w - 1)
                        for k in range(kt):
                            mm = pe.transpose(b4(5 + w % 2)[:, k, :], stat[:, w % 2, k * P:(k + 1) * P], ident[:, :])
                        mm.then_inc(probs_t, 1)
                    if u >= 3 and u % 2 == 1:
                        hd = (u - 3) // 2
                        c.at(probs_c, u - 1)
                        if hd:
                            c.at(act_ready, hd)
                        pt = ev[:, :, :].rearrange("p a (b t) -> p (a b) t", b=2)
                        for cd in range(XA_CH if kind == "cross" else 1):
                            b = bank[cd // 2 if kind == "cross" else 0]
                            for k in range(kt):
                                if kind == "cross":
                                    val = memV[:, k, (XA_CH * hd + cd) * P:(XA_CH * hd + cd + 1) * P]
                                elif kind == "na":
                                    val = naV[:, k // 2, k % 2, hd * P:(hd + 1) * P]
                                else:
                                    val = mlaV[:, k // 2, k % 2, hd * P:(hd + 1) * P]
                                mm = pe.matmul(b[:, T * (cd % 2):T * (cd % 2) + T], val, pt[:, k, :],
                                               start=(k == 0), stop=(k == kt - 1))
                        mm.then_inc(heads, 1)
                c.end(probs, len(units))
                c.end(probs_c, len(units))

            phase_out(PH["wq"])
            attention("cross")
            act_in(XA_H)
            phase(PH["wo"], act)

            norm()
            act_in(4)
            for r in range(FF1_ROUNDS):
                phase(PH[f"w1_{r}"], act)
                c.at(ev_v, PH[f"w1_{r}"].nblocks * (r + 1) + EV0)
                phase(PH[f"w2_{r}"], hid)
            c.end(ev_v, PH["w1_0"].nblocks * FF1_ROUNDS)
            norm()

            norm()
            act_in(4)
            for name in ("ckv_c", "nak_c", "nav_c", "kr_c"):
                phase(PH[name], act)
            norm()
            act_in(4)
            for name in ("ckv_x", "nak_x", "nav_x", "cq", "naq", "fn", "kr_x"):
                phase(PH[name], act)
            phase_out(PH["kr_x"])
            attention("na")
            act_in(NA_H)
            for g in range(FN_G):
                if g:
                    c.at(fn_act, 2 * g)
                for mt in range(TT):
                    mm = pe.matmul(bank[3][:, mt * T:(mt + 1) * T], fT[:, g, mt * P:(mt + 1) * P], cc(CA, "dft_ch"), start=True, stop=True)
                mm.then_inc(fn_pe, 1)
                c.at(fn_act, 2 * g + 1)
                for n in range(2 * TT):
                    mt, part = n // 2, n % 2
                    mm = pe.matmul(bank[4][:, 0:T], stat[:, 0, mt * T + part * P:mt * T + (part + 1) * P],
                                   cc(CA, ("dft_cos", "dft_sin")[part])[:, mt * T:(mt + 1) * T], start=(n == 0), stop=(n == 3))
                mm.then_inc(fn_pe, 1)
                c.at(fn_act, 2 * g + 2)
                if g:
                    c.at(act_ready, g)
                pe.matmul(bank[0][:, 0:T], cc(CA, "w_fnet")[:, g * P:(g + 1) * P], stat[:, 1, 0:T], start=True, stop=True).then_inc(heads, 1)
            act_in(FN_G)
            norm(LC)
            act_in(1)
            phase(PH["kn_c"], act)
            phase(PH["v_c"], act)
            norm(LC)
            act_in(1)
            phase(PH["kn_x"], act, 4)
            phase(PH["v_x"], act, 4)
            norm(LC)
            act_in(1)
            phase(PH["qn"], act)
            phase(PH["qr"], act)
            phase_out(PH["qr"])
            for n in range(1 + MLA_H // 2):
                src = kr[:, 0, :] if n == 0 else qR[:, n - 1, :]
                pe.matmul(bank[3 + n][:, 0:T], cc(CA, "swap"), src, start=True, stop=True).then_inc(rope_pe, 1)
            c.at(rope_dve, 1 + MLA_H // 2)
            attention("mla")
            act_in(MLA_H)
            phase(PH["wout2"], act)

            norm()
            act_in(4)
            done = 0
            for r, n in enumerate(FF2_ROUNDS):
                phase(PH[f"up_{r}"], act)
                done += n
                c.at(ev_v, EV_UP * done + EV0)
                phase(PH[f"down_{r}"], hid)
            norm()

        @block.scalar
        def _(sc):
            c = Counts(sc)
            chain = Chain(sc, act_step)

            def slot(ph):
                def f(i, j):
                    at = ph.slot0 + j
                    sc.wait_ge(raw_in[at % RAW_N], i * (16 * (ph.S // RAW_N)) + 16 * (at // RAW_N + 1))
                    sc.wait_ge(slot_used, i * ph.S + (at + 1))
                    sc.activation(whi[:, at % SPL_N, :], raw[:, at % RAW_N, :], ACT.Copy).then_inc(hi_done, 1)
                return f

            def done(ph, n):
                sc.wait_ge(slot_used, n * ph.slots_per_block + (ph.slot0 + ph.slots_per_block + SPL_N))

            def to(dst, flip=False, func=ACT.Copy):
                def make(ph):
                    def f(n, b):
                        done(ph, n)
                        o = dst[:, 0:TT, ds(n * NCOL, NCOL)] if flip else dst[:, ds(n * 2, 2), :]
                        sc.activation(o, b2(b), func).then_inc(block_free, 1)
                    return f
                return make

            def one(dst):
                def make(ph):
                    def f(n, b):
                        done(ph, n)
                        sc.activation(dst, bank[b][:, 0:T], ACT.Copy).then_inc(block_free, 1)
                    return f
                return make

            def nothing(ph):
                return lambda n, b: None

            def conv4(ph):
                def f(n, b):
                    done(ph, n)
                    sc.wait_ge(block_free, n + (FREE + ph.block0))
                    for hf in range(2):
                        ins = sc.activation(ev[:, 0, hf * T:(hf + 1) * T], b2(b)[:, hf, :], ACT.Copy,
                                            scale=par("dn_conv", n * 8 + (4 * hf + 3)))
                    ins.then_inc(ev_a, 1)
                    sc.wait_ge(block_free, n + (FREE + ph.block0 + 1))
                    chain(sc.activation(qkvT[:, ds(n * 2, 2), :], ev[:, 0, :].rearrange("p (a b) -> p a b", a=2), ACT.Silu))
                return f

            def glu(ph):
                def f(n, b):
                    done(ph, n)
                    sc.wait_ge(block_free, n + (FREE + ph.block0))
                    sc.activation(ev[:, 0, 0:T], b2(b)[:, 1, :], ACT.Sigmoid).then_inc(ev_a, 1)
                return f

            def relu2(ph):
                def f(n, b):
                    done(ph, n)
                    c.at(ev_v, n + EV0)
                    sc.activation(ev[:, 0, :], bank[b][:, :], ACT.Relu).then_inc(block_free, 1)
                    sc.wait_ge(block_free, n + (FREE + ph.block0 + 1))
                    chain(sc.activation(ev[:, 1, :], ev[:, 0, :], ACT.Square))
                    sc.activation(hid[:, 0, ds(n * 2, 2), :], ev[:, 1, :].rearrange("p (a b) -> p a b", a=2),
                                  ACT.Copy).then_inc(ev_a, 1)
                return f

            def gated(first):
                def make(ph):
                    def f(n, b):
                        done(ph, n)
                        c.at(ev_v, n * EV_UP + EV0)
                        for hf in range(2):
                            ins = sc.activation(ev[:, 0, hf * T:(hf + 1) * T], b2(b)[:, hf, :], ACT.Identity,
                                                scale=par("ff_conv", n * 6 + (6 * first + 3 * hf + 1)),
                                                bias=par("ff_b", n * 2 + (2 * first + hf)))
                        ins.then_inc(ev_a, 1)
                        sc.wait_ge(block_free, n + (FREE + ph.block0 + 1))
                        sc.activation(ev[:, 1, 0:T], ev[:, 0, 0:T], ACT.Silu).then_inc(ev_a, 1)
                    return f
                return make

            def phase(name, evac, links=0):
                over(sc, PH[name], slot, evac(PH[name]), chain, links)

            def before(name):
                sc.wait_ge(block_free, FREE + PH[name].block0)

            def norm(src, chunks=DC, c0=0, shift=None, split=True, at=0):
                for q in range(chunks // 4):
                    sc.activation(tmp[:, 4 * q:4 * q + 4, :], src[:, 4 * q:4 * q + 4, :], ACT.Square).then_inc(squares, 1)
                c.at(var, 1)
                sc.activation(stat[:, 0, T:2 * T], stat[:, 0, 0:T], ACT.Sqrt).then_inc(std, 1)
                c.end(var, 1)
                if split:
                    for q in range(chunks // 4):
                        c.at(normed, q + 1)
                        if shift is None:
                            ins = sc.activation(act[:, 0, c0 + 4 * q:c0 + 4 * q + 4, :], tmp[:, 4 * q:4 * q + 4, :], ACT.Copy)
                        else:
                            for k in range(4 * q, 4 * q + 4):
                                ins = sc.activation(act[:, 0, k, :], tmp[:, k, :], ACT.Identity, bias=modt[:, shift + k:shift + k + 1])
                        ins.then_inc(norm_hi, 1)
                    c.end(normed, chunks // 4)

            sc.wait_ge(params_in, 64)
            sc.activation(small[:, C_SILU:C_SILU + 2 * DC], pv[:, PV["c"][0]:PV["c_ctx"][1]], ACT.Silu).then_inc(mod_ready, 1)
            sc.wait_ge(src_in, 16)
            norm(h)
            phase("glu", glu)
            phase("qkv", conv4, 2)
            phase("z", to(zT, func=ACT.Silu))

            def row(r):
                return gt[:, r, :]
            c.at(gate_dve, 1)
            sc.activation(row(BETA).rearrange("p (a b) -> p a b", a=2),
                          bank[3][:, 0:32].rearrange("p (a b) -> p a b", a=2)[:, :, 0:8], ACT.Sigmoid)
            sc.activation(gt[:, EA, 0:8], par("a_log", 0, 8), ACT.Exp)
            chain(sc.activation(row(LN1), row(A1), ACT.Abs))
            chain(sc.activation(row(LN1), row(LN1), ACT.Exp, scale=-1.0))
            sc.activation(row(LN1), row(LN1), ACT.Ln, bias=1.0).then_inc(gate_act, 1)

            def square(p):
                sc.activation(ev[:, p % 2, :].rearrange("p (a b) -> p a b", a=2), qkvT[:, 2 * p:2 * p + 2, :], ACT.Square).then_inc(l2_sq, 1)
            sc.wait_ge(act_step, chain.n)
            square(0)
            square(1)
            c.at(gate_pe, 2)
            gc = bank[3][:, 32:48]
            sc.activation(row(GC), gc, ACT.Copy)
            sc.activation(row(NGC), gc, ACT.Copy, scale=-1.0)
            sc.activation(row(EGC), gc, ACT.Exp).then_inc(gate_act, 1)
            c.at(cf_dve, 3)
            sc.activation(tmp[:, 8:16, :], tmp[:, 0:8, :], ACT.Square).then_inc(cf_act, 1)
            for p in range(8):
                c.at(l2_dve, p + 1)
                sc.activation(stat[:, p % 2, :], stat[:, p % 2, :], ACT.Sqrt).then_inc(l2_act, 1)
                if p + 2 < 8:
                    c.at(l2_pe, p + 1)
                    square(p + 2)
            c.at(cf_dve, 4)
            sc.activation(stat[:, 0, T:2 * T], stat[:, 0, 0:T], ACT.Sqrt).then_inc(cf_act, 1)
            for q in range(2):
                c.at(cf_dve, 5 + q)
                for k in range(4 * q, 4 * q + 4):
                    ins = sc.activation(tmp[:, 8 + k, :], tmp[:, k, :], ACT.Silu, bias=par("ln_b", k))
                chain(ins)
                sc.activation(act[:, 0, 8 + 4 * q:12 + 4 * q, :], tmp[:, 8 + 4 * q:12 + 4 * q, :], ACT.Copy).then_inc(cf_act, 1)
            c.at(cf_dve, 7)
            for ch in CHUNKS:
                tok = slice(ch * P, (ch + 1) * P)

                def p_(hg, name):
                    c.at(dl_pe[hg], step(PE_SIG, ch, name))

                def v(hg, name):
                    c.at(dl_dve[hg], step(DVE_SIG, ch, name))
                if ch:
                    for hg in GROUPS:
                        p_(hg, "bc")
                        sc.activation(EG[hg], bk(hg, 0), ACT.Exp).then_inc(dl_act[hg], 1)
                for hg in GROUPS:
                    v(hg, "dta")
                    for n in range(4):
                        ins = sc.activation(DT[hg][:, n, :], DT[hg][:, n, :], ACT.Exp, bias=gtc(NGC, ch, 4 * hg + n))
                    ins.then_inc(dl_act[hg], 1)
                    if not ch:
                        v(hg, "kdl")
                        kds = gt[:, KDS, 4 * hg:4 * hg + 4]
                        sc.activation(kds, gt[:, KDL, 4 * hg:4 * hg + 4], ACT.Exp).then_inc(dl_act[hg], 1)
                        c.at(dl_act[hg], step(ACT_SIG, ch, "kds"))
                    p_(hg, "tr")
                    for n in range(4):
                        w = gtc(BEG, ch, 4 * hg + n) if ch else gt[:, KDS, 4 * hg + n:4 * hg + n + 1]
                        ins = sc.activation(KW[hg][:, n, :], bk(hg, 2)[:, n, :], ACT.Copy, scale=w)
                    ins.then_inc(dl_act[hg], 1)
                for lv in range(LEVELS):
                    for hg in GROUPS:
                        p_(hg, f"y{lv}")
                        sc.activation(Y[hg], bk(hg, 0), ACT.Copy).then_inc(dl_act[hg], 1)
                for hg in GROUPS:
                    p_(hg, "uw")
                    if ch:
                        sc.activation(U_[hg], bk(hg, 1), ACT.Copy)
                        sc.activation(WT[hg], bk(hg, 2), ACT.Copy).then_inc(dl_act[hg], 1)
                    else:
                        sc.activation(VN[hg], bk(hg, 1), ACT.Copy).then_inc(dl_act[hg], 1)
                for hg in GROUPS:
                    p_(hg, "o")
                    ins = sc.activation(qkvT[:, 16 + 4 * hg:20 + 4 * hg, tok], bk(hg, 3), ACT.Copy)
                    if not ch:
                        ins = sc.activation(ST[hg], bk(hg, 2), ACT.Copy)
                    ins.then_inc(dl_act[hg], 1)
            for hg in GROUPS:
                c.at(dl_act[hg], step(ACT_SIG, TT - 1, "oc"))
            for q in range(2):
                sc.activation(tmp[:, 4 * q:4 * q + 4, :], qkvT[:, 16 + 4 * q:20 + 4 * q, :], ACT.Square).then_inc(on_act, 1)
            for p in range(4):
                c.at(on_dve, 2 * p + 1)
                sc.activation(stat[:, p % 2, :], stat[:, p % 2, :], ACT.Sqrt).then_inc(on_act, 1)
                c.at(on_dve, 2 * p + 2)
                sc.activation(act[:, 0, 2 * p:2 * p + 2, :], qkvT[:, 16 + 2 * p:18 + 2 * p, :], ACT.Copy).then_inc(on_act, 1)
            phase("wout", nothing)

            before("memk")
            sc.wait_ge(mem_in, 16)
            norm(memV[:, :, :].rearrange("p a (b t) -> p (a b) t", t=T))
            phase("memk", to(memK))
            phase("memv", to(memV, flip=True))
            before("wq")
            norm(h)
            phase("wq", to(tmp))

            def attention(kind, c0=0):
                units = attention_units(kind)
                kt = key_tiles(kind)
                nk = kt * P
                scale = {"cross": XA_SCALE, "mla": MLA_SCALE, "na": 1.0}[kind]
                for u in range(len(units) + 2):
                    if u < len(units):
                        pb = stat[:, u % 2, 0:nk]
                        c.at(maxes, u + 1)
                        sc.activation(pb, pb if kind == "na" else bank[3 + u % 2][:, 0:nk], ACT.Exp, scale=scale,
                                      bias=small[:, SM + 4 * (u % 2) + 1:SM + 4 * (u % 2) + 2],
                                      accum_out=small[:, SM + 4 * (u % 2) + 2:SM + 4 * (u % 2) + 3]).then_inc(exps, 1)
                    if 1 <= u <= len(units):
                        w = u - 1
                        hd, mt = units[w]
                        c.at(probs_t, w + 1)
                        if mt == 0 and hd:
                            c.at(heads, hd)
                        sc.activation(ev[:, :, :].rearrange("p a (b t) -> p (a b) t", b=2)[:, 0:kt, mt * P:(mt + 1) * P],
                                      b4(5 + w % 2)[:, 0:kt, :], ACT.Copy).then_inc(probs_c, 1)
                    if u >= 3 and u % 2 == 1:
                        hd = (u - 3) // 2
                        c.at(heads, hd + 1)
                        if kind == "cross":
                            for k in range(2):
                                ins = sc.activation(act[:, 0, XA_CH * hd + 2 * k:XA_CH * hd + 2 * k + 2, :], b2(k), ACT.Copy)
                        else:
                            ins = sc.activation(act[:, 0, c0 + hd, :], bank[0][:, 0:T], ACT.Copy)
                        ins.then_inc(head_hi, 1)
                c.end(maxes, len(units))
                c.end(probs_t, len(units))
                c.end(heads, len(units) // 2)

            before("wo")
            attention("cross")
            phase("wo", nothing)

            before("w1_0")
            norm(h)
            for r in range(FF1_ROUNDS):
                phase(f"w1_{r}", relu2, 2)
                c.end(ev_v, PH["w1_0"].nblocks)
                phase(f"w2_{r}", nothing)
            before("ckv_c")
            norm(h, split=False)

            sc.wait_ge(ctx_in, 16)
            norm(kN[:, :, :, :].rearrange("p a b t -> p (a b) t"), shift=96)
            phase("ckv_c", to(ckv[:, 1, :, :]))
            phase("nak_c", to(naK[:, :, 1, :]))
            phase("nav_c", to(naV[:, 1, :, :], flip=True))
            phase("kr_c", one(kr[:, 1, :]))
            norm(h, shift=0)
            phase("ckv_x", to(ckv[:, 0, :, :]))
            phase("nak_x", to(naK[:, :, 0, :]))
            phase("nav_x", to(naV[:, 0, :, :], flip=True))
            phase("cq", to(cq))
            phase("naq", to(naQ))
            phase("fn", to(fT))
            phase("kr_x", one(kr[:, 0, :]))
            attention("na", 8)
            for g in range(FN_G):
                c.at(fn_pe, 2 * g + 1)
                if g:
                    c.at(heads, g)
                sc.activation(stat[:, 0, :], bank[3][:, :], ACT.Copy).then_inc(fn_act, 1)
                c.at(fn_pe, 2 * g + 2)
                sc.activation(stat[:, 1, 0:T], bank[4][:, 0:T], ACT.Copy, scale=FN_SCALE).then_inc(fn_act, 1)
                c.at(heads, g + 1)
                sc.activation(act[:, 0, 12 + g, :], bank[0][:, 0:T], ACT.Copy).then_inc(head_hi, 1)
            c.end(heads, FN_G)
            norm(ckv[:, 1, :, :], LC)
            phase("kn_c", to(kN[:, :, 1, :]))
            phase("v_c", to(mlaV[:, 1, :, :], flip=True))
            norm(ckv[:, 0, :, :], LC, 4)
            phase("kn_x", to(kN[:, :, 0, :]))
            phase("v_x", to(mlaV[:, 0, :, :], flip=True))
            norm(cq, LC)
            phase("qn", to(qN))
            phase("qr", to(qR))
            attention("mla")
            phase("wout2", nothing)

            before("up_0")
            norm(h, shift=48)
            first = 0
            for r, n in enumerate(FF2_ROUNDS):
                phase(f"up_{r}", gated(first))
                c.end(ev_v, n * EV_UP)
                first += n
                phase(f"down_{r}", nothing)
            sc.wait_ge(block_free, FREE + PH["down_2"].block0 + PH["down_2"].nblocks)
            norm(h, split=False)

        @block.vector
        def _(ve):
            c = Counts(ve)
            chain = Chain(ve, dve_step)
            ve.memset(cin[:, :, 0:CF_TAPS - 1], 0.0).then_inc(split_done, RAW_N)
            ve.memset(small[:, 120:121], 0.0).then_inc(slot_used, SPL_N)
            ve.memset(small[:, 122:123], 0.0).then_inc(block_free, FREE)
            ve.memset(small[:, 123:124], 0.0).then_inc(ev_v, EV0)

            mod_mark = {}

            def mod_chunk(ph, i, k):
                mb = i + ph.mod0
                q = k // 4
                if k % 4 == 0:
                    ve.wait_ge(mod_in[q % MOD_N], mb * 32 + 16 * (q // MOD_N + 1))
                if k == 0 and not (isinstance(mb, int) and mb == 0):
                    ve.wait_ge(mod_out, mb)
                if k >= 2:
                    if (k - 2) % 4 == 3:
                        ve.wait_ge(mod_used, mb * 4 + ((k - 2) // 4 + 1 + MOD_N))
                    else:
                        ve.wait_ge(dve_step, mod_mark[k - 2])
                for w in range(ph.mod):
                    wt = modraw[:, q % MOD_N, (k % 4) * NCOL:(k % 4 + 1) * NCOL]
                    col = small[:, C_SILU + DC * w + k:C_SILU + DC * w + k + 1]
                    acc = modacc[:, 2 * w + k % 2, :]
                    if k < 2:
                        ins = ve.tensor_scalar(acc, wt, col, None, ALU.mult)
                    else:
                        ins = ve.scalar_tensor_tensor(acc, wt, col, acc, ALU.mult, ALU.add)
                if k % 4 == 3:
                    ins.then_inc(mod_used, 1)
                else:
                    chain.tick(ins)
                    mod_mark[k] = chain.now()

            def slot(ph):
                def f(i, j):
                    at = ph.slot0 + j
                    ks = MOD_AT[j] if ph.mod and j < len(MOD_AT) else ()
                    for k in ks[:1]:
                        mod_chunk(ph, i, k)
                    ve.wait_ge(hi_done, i * ph.S + (at + 1))
                    ve.tensor_tensor(wlo[:, at % SPL_N, :], raw[:, at % RAW_N, :], whi[:, at % SPL_N, :].bitcast(F32),
                                     ALU.subtract).then_inc(split_done, 1)
                    for k in ks[1:]:
                        mod_chunk(ph, i, k)
                return f

            def done(ph, n):
                ve.wait_ge(slot_used, n * ph.slots_per_block + (ph.slot0 + ph.slots_per_block + SPL_N))

            def nothing(ph):
                return lambda n, b: None

            def conv4(ph):
                def f(n, b):
                    c.at(ev_a, n + 1)
                    for j in range(1, DN_TAPS):
                        for hf in range(2):
                            o = ev[:, 0, hf * T + j:(hf + 1) * T]
                            ins = ve.scalar_tensor_tensor(o, b2(b)[:, hf, 0:T - j], par("dn_conv", n * 8 + (4 * hf + 3 - j)), o,
                                                          ALU.mult, ALU.add)
                            if j == DN_TAPS - 1 and hf:
                                ins.then_inc(block_free, 1)
                            else:
                                ins.then_inc(dve_step, 1)
                                chain.n += 1
                        if j < DN_TAPS - 1:
                            ve.wait_ge(dve_step, chain.i * chain.per + chain.n)
                return f

            def glu(ph):
                def f(n, b):
                    c.at(ev_a, n + 1)
                    ve.tensor_tensor(cin[:, ds(n, 1), CF_TAPS - 1:CF_TAPS - 1 + T], b2(b)[:, 0:1, :],
                                     ev[:, 0, 0:T].rearrange("p (a b) -> p a b", a=1), ALU.mult).then_inc(block_free, 1)
                return f

            def resid(gate=None):
                def make(ph):
                    def f(n, b):
                        done(ph, n)
                        if gate is None:
                            ve.tensor_tensor(h[:, ds(n * 2, 2), :], b2(b), h[:, ds(n * 2, 2), :], ALU.add).then_inc(block_free, 1)
                        else:
                            for hf in range(2):
                                o = h[:, ds(n * 2 + hf, 1), :]
                                ins = ve.scalar_tensor_tensor(o, b2(b)[:, hf:hf + 1, :], modt[:, ds(n * 2 + (gate + hf), 1)], o,
                                                              ALU.mult, ALU.add)
                            ins.then_inc(block_free, 1)
                    return f
                return make

            def relu2(ph):
                def f(n, b):
                    c.at(ev_a, n + 1)
                    o = hid[:, 0, ds(n * 2, 2), :]
                    ve.tensor_tensor(hid[:, 1, ds(n * 2, 2), :], ev[:, 1, :].rearrange("p (a b) -> p a b", a=2), o.bitcast(F32),
                                     ALU.subtract).then_inc(ev_v, 1)
                return f

            def gated(first):
                def make(ph):
                    def f(n, b):
                        c.at(ev_a, n * 2 + 1)
                        for j, so, do in ((0, slice(0, T - 1), slice(1, T)), (2, slice(1, T), slice(0, T - 1))):
                            for hf in range(2):
                                o = ev[:, 0, hf * T + do.start:hf * T + do.stop]
                                ins = ve.scalar_tensor_tensor(o, b2(b)[:, hf, so], par("ff_conv", n * 6 + (6 * first + 3 * hf + j)), o,
                                                              ALU.mult, ALU.add)
                                if j == 2 and hf:
                                    ins.then_inc(block_free, 1)
                                else:
                                    ins.then_inc(dve_step, 1)
                                    chain.n += 1
                            if j == 0:
                                ve.wait_ge(dve_step, chain.i * chain.per + chain.n)
                        c.at(ev_a, n * 2 + 2)
                        chain(ve.tensor_tensor(ev[:, 1, T:2 * T], ev[:, 1, 0:T], ev[:, 0, T:2 * T], ALU.mult))
                        t = ev[:, 1:2, T:2 * T]
                        chain(ve.tensor_copy(hid[:, 0, ds(n, 1), :], t))
                        ve.tensor_tensor(hid[:, 1, ds(n, 1), :], t, hid[:, 0, ds(n, 1), :].bitcast(F32), ALU.subtract).then_inc(ev_v, 1)
                    return f
                return make

            def phase(name, evac, links=0, extra=None):
                ph = PH[name]
                over(ve, ph, slot, evac(ph), chain, links + (12 if ph.mod else 0), extra)

            def norm(src, gain, chunks=DC, c0=0, shift=None, into=None):
                c.at(sums, 1)
                ve.tensor_scalar(stat[:, 0, 0:T], bank[3][:, 0:T], 1.0 / (chunks * P), EPS, ALU.mult, ALU.add).then_inc(var, 1)
                c.at(std, 1)
                chain(ve.reciprocal(stat[:, 1, 0:T], stat[:, 0, T:2 * T]))
                c.end(sums, 1)
                c.end(std, 1)
                dst = tmp if into is None else into

                def lower(q):
                    c.at(norm_hi, q + 1)
                    if shift is None:
                        ks = slice(4 * q, 4 * q + 4)
                        ins = ve.tensor_tensor(act[:, 1, c0 + 4 * q:c0 + 4 * q + 4, :], tmp[:, ks, :],
                                               act[:, 0, c0 + 4 * q:c0 + 4 * q + 4, :].bitcast(F32), ALU.subtract)
                    else:
                        for k in range(4 * q, 4 * q + 4):
                            ins = ve.scalar_tensor_tensor(act[:, 1, k, :], tmp[:, k, :], modt[:, shift + k:shift + k + 1],
                                                          act[:, 0, k, :].bitcast(F32), ALU.add, ALU.subtract)
                    ins.then_inc(act_ready, 1)

                for q in range(chunks // 4):
                    for k in range(4 * q, 4 * q + 4):
                        ins = ve.scalar_tensor_tensor(dst[:, k, :], src[:, k, :], gain(k), stat[:, 1, 0:T], ALU.mult, ALU.mult)
                    if into is None:
                        ins.then_inc(normed, 1)
                        if q:
                            lower(q - 1)
                if into is None:
                    lower(chunks // 4 - 1)
                    c.end(norm_hi, chunks // 4)
                return ins

            def g(name):
                return lambda k: par(name, k)

            ve.wait_ge(params_in, 64)
            ve.wait_ge(mod_ready, 1)
            ve.wait_ge(src_in, 16)
            norm(h, g("norm_mix"))
            phase("glu", glu)
            c.end(ev_a, 8)
            c.at(gate_pe, 1)

            def conv31(i0):
                def f(i, j):
                    o = tmp[:, ds(i + i0, 1), :]
                    for t in range(4 * j, min(4 * j + 4, CF_TAPS)):
                        x_ = cin[:, ds(i + i0, 1), t:t + T]
                        w = par("cf_conv", i * CF_TAPS + (CF_TAPS * i0 + t))
                        if t == 0:
                            chain(ve.tensor_scalar(o, x_, w, par("cf_b", i + i0), ALU.mult, ALU.add))
                        else:
                            chain(ve.scalar_tensor_tensor(o, x_, w, o, ALU.mult, ALU.add))
                return f
            phase("qkv", conv4, 2 * 5 + CF_TAPS, conv31(0))
            c.end(ev_a, 12)
            phase("z", nothing, CF_TAPS, conv31(PH["qkv"].iters))
            assert PH["qkv"].iters + PH["z"].iters == 8

            ve.memset(small[:, 125:126], 0.0).then_inc(cf_dve, 1)
            for mt in range(TT):
                ins = ve.tensor_tensor(gt[:, A1, 8 * mt:8 * mt + 8], bank[3][:, 16 * mt + 8:16 * mt + 16], par("dt", 0, 8), ALU.add)
            ins.then_inc(gate_dve, 1)
            c.at(gate_act, 1)
            chain(ve.scalar_tensor_tensor(gt[:, GC, :], gt[:, A1, :], 0.0, gt[:, LN1, :], ALU.max, ALU.add))
            for mt in range(TT):
                r = slice(8 * mt, 8 * mt + 8)
                ins = ve.scalar_tensor_tensor(gt[:, G, r], gt[:, GC, r], -1.0, gt[:, EA, 0:8], ALU.mult, ALU.mult)
            ins.then_inc(gate_dve, 1)
            c.at(cf_pe, 1)
            ve.tensor_scalar(stat[:, 0, 0:T], bank[2][:, 0:T], 1.0 / D_CONV, None, ALU.mult).then_inc(cf_dve, 1)
            c.at(cf_dve, 2)
            ve.tensor_tensor(tmp[:, 0:8, :], tmp[:, 0:8, :], stat[:, 0:1, 0:T].to_broadcast([P, 8, T]), ALU.subtract).then_inc(cf_dve, 1)
            c.at(cf_dve, 3)
            for p in range(9):
                if p < 8:
                    c.at(l2_pe, p + 1)
                    ve.tensor_scalar(stat[:, p % 2, :], bank[4 + p % 4][:, :], 1.0, EPS, ALU.mult, ALU.add).then_inc(l2_dve, 1)
                if p:
                    q = p - 1
                    c.at(l2_act, q + 1)
                    chain(ve.reciprocal(stat[:, q % 2, :], stat[:, q % 2, :]))
                    o = qkvT[:, 2 * q:2 * q + 2, :]
                    chain(ve.scalar_tensor_tensor(o, o, float(P) ** -0.5 if q < 4 else 1.0,
                                                  stat[:, q % 2, :].rearrange("p (a b) -> p a b", a=2), ALU.mult, ALU.mult))
            c.at(gate_act, 2)
            ve.tensor_tensor(gt[:, BEG, :], gt[:, BETA, :], gt[:, EGC, :], ALU.mult)
            c.at(cf_pe, 2)
            ve.tensor_scalar(stat[:, 0, 0:T], bank[2][:, 0:T], 1.0 / D_CONV, EPS, ALU.mult, ALU.add).then_inc(cf_dve, 1)
            c.at(cf_act, 2)
            chain(ve.reciprocal(stat[:, 1, 0:T], stat[:, 0, T:2 * T]))
            for q in range(2):
                for k in range(4 * q, 4 * q + 4):
                    ins = ve.scalar_tensor_tensor(tmp[:, k, :], tmp[:, k, :], par("ln_g", k), stat[:, 1, 0:T], ALU.mult, ALU.mult)
                ins.then_inc(cf_dve, 1)
            for q in range(2):
                c.at(cf_act, 3 + q)
                ve.tensor_tensor(act[:, 1, 8 + 4 * q:12 + 4 * q, :], tmp[:, 8 + 4 * q:12 + 4 * q, :],
                                 act[:, 0, 8 + 4 * q:12 + 4 * q, :].bitcast(F32), ALU.subtract).then_inc(act_ready, 1)
            ve.memset(small[:, 127:128], 0.0).then_inc(cf_dve, 1)

            c.at(cf_dve, 7)

            def every(t):
                return t.rearrange("p (a b) -> p a b", a=1).to_broadcast([P, 4, P])
            for ch in CHUNKS:
                tok = slice(ch * P, (ch + 1) * P)

                def p_(hg, name):
                    c.at(dl_pe[hg], step(PE_SIG, ch, name))

                def a(hg, name):
                    c.at(dl_act[hg], step(ACT_SIG, ch, name))

                def mine(hg, name):
                    c.at(dl_dve[hg], step(DVE_SIG, ch, name))
                for hg in GROUPS:
                    if ch:
                        c.at(dl_act[hg], step(ACT_SIG, ch - 1, "oc"))
                        a(hg, "eg")
                    p_(hg, "bc")
                    ve.tensor_tensor(DT[hg], bk(hg, 0), every(cc(CM, "below")), ALU.add).then_inc(dl_dve[hg], 1)
                    if not ch:
                        ve.tensor_tensor(gt[:, KDL, 4 * hg:4 * hg + 4], bk(hg, 0)[:, :, P - 1], gtc(GC, ch, 4 * hg, 4),
                                         ALU.subtract).then_inc(dl_dve[hg], 1)
                    if ch:
                        ve.tensor_tensor(QDT[hg], qkvT[:, 4 * hg:4 * hg + 4, tok], EG[hg], ALU.mult)
                    ve.tensor_tensor(KBT[hg], qkvT[:, 8 + 4 * hg:12 + 4 * hg, tok], bk(hg, 1), ALU.mult).then_inc(dl_dve[hg], 1)
                for hg in GROUPS:
                    p_(hg, "tr")
                    for n in range(4):
                        ins = ve.tensor_scalar(VB[hg][:, n, :], bk(hg, 3)[:, n, :], gtc(BETA, ch, 4 * hg + n), None, ALU.mult)
                    ins.then_inc(dl_dve[hg], 1)
                    p_(hg, "aa")
                    a(hg, "dtx")
                    ve.tensor_copy(X[hg], every(ident[:, :]))
                    ve.tensor_copy(XT[hg], every(ident[:, :]))
                    ve.tensor_tensor(AT[hg], bk(hg, 0), DT[hg], ALU.mult)
                    ve.tensor_tensor(ATT[hg], bk(hg, 1), DT[hg], ALU.mult).then_inc(dl_dve[hg], 1)
                    mine(hg, "aat")

                def masked(hg, lv):
                    ve.tensor_tensor(MT[hg], AT[hg], every(cc(CM, "levels")[:, lv * P:(lv + 1) * P]), ALU.mult).then_inc(dl_dve[hg], 1)
                for hg in GROUPS:
                    masked(hg, 0)
                for lv in range(LEVELS):
                    if lv + 1 < LEVELS:
                        for hg in GROUPS:
                            p_(hg, f"y{lv}")
                            masked(hg, lv + 1)
                    for hg in GROUPS:
                        p_(hg, f"z{lv}")
                        if lv:
                            mine(hg, f"x{lv - 1}")
                        if lv + 1 < LEVELS:
                            ve.tensor_tensor(X[hg], X[hg], bk(hg, 2), ALU.subtract)
                        ve.tensor_tensor(XT[hg], XT[hg], bk(hg, 3), ALU.subtract).then_inc(dl_dve[hg], 1)
                if ch:
                    for hg in GROUPS:
                        p_(hg, "ws")
                        ve.tensor_tensor(VN[hg], U_[hg], bk(hg, 0), ALU.subtract).then_inc(dl_dve[hg], 1)
            for p in range(4):
                c.at(on_pe, p + 1)
                ve.tensor_scalar(stat[:, p % 2, :], bank[4 + p][:, :], 1.0 / P, EPS, ALU.mult, ALU.add).then_inc(on_dve, 1)
                c.at(on_act, 2 + 2 * p + 1)
                chain(ve.reciprocal(stat[:, p % 2, :], stat[:, p % 2, :]))
                o = qkvT[:, 16 + 2 * p:18 + 2 * p, :]
                chain(ve.scalar_tensor_tensor(o, o, par("dn_norm"), stat[:, p % 2, :].rearrange("p (a b) -> p a b", a=2), ALU.mult, ALU.mult))
                ve.tensor_tensor(o, o, zT[:, 2 * p:2 * p + 2, :], ALU.mult).then_inc(on_dve, 1)
                c.at(on_act, 2 + 2 * p + 2)
                ve.tensor_tensor(act[:, 1, 2 * p:2 * p + 2, :], o, act[:, 0, 2 * p:2 * p + 2, :].bitcast(F32),
                                 ALU.subtract).then_inc(act_ready, 1)
            ve.memset(small[:, 121:122], 0.0).then_inc(mod_used, MOD_N)
            ve.memset(small[:, 126:127], 0.0).then_inc(mixed, 1)
            phase("wout", resid())

            norm(memV[:, :, :].rearrange("p a (b t) -> p (a b) t", t=T), g("norm_mem"))
            phase("memk", nothing)
            phase("memv", nothing)
            norm(h, g("norm_xa"))
            phase("wq", nothing)

            def attention(kind, c0=0):
                units = attention_units(kind)
                nk = key_tiles(kind) * P
                scale = {"cross": XA_SCALE, "mla": MLA_SCALE, "na": 1.0}[kind]
                for u in range(len(units) + 2):
                    if u < len(units):
                        hd, mt = units[u]
                        pb = stat[:, u % 2, 0:nk]
                        b = bank[3 + u % 2]
                        m = SM + 4 * (u % 2)
                        c.at(scores, u + 1)
                        if u >= 2:
                            c.at(probs_t, u - 1)
                        src = b[:, 0:nk]
                        if kind == "na":
                            ve.scalar_tensor_tensor(pb[:, 0:T], b[:, 0:T], NA_SCALE, bias[:, hd, mt, :], ALU.mult, ALU.add)
                            chain(ve.tensor_scalar(pb[:, T:2 * T], b[:, T:2 * T], NA_SCALE, None, ALU.mult))
                            src = pb
                        chain(ve.tensor_reduce(small[:, m:m + 1], src, AX.X, ALU.max))
                        ve.tensor_scalar(small[:, m + 1:m + 2], small[:, m:m + 1], -scale, None, ALU.mult).then_inc(maxes, 1)
                        c.at(exps, u + 1)
                        chain(ve.reciprocal(small[:, m + 3:m + 4], small[:, m + 2:m + 3]))
                        ve.tensor_scalar(pb, pb, small[:, m + 3:m + 4], None, ALU.mult).then_inc(probs, 1)
                    if u >= 3 and u % 2 == 1:
                        hd = (u - 3) // 2
                        c.at(head_hi, hd + 1)
                        if kind == "cross":
                            for k in range(2):
                                ks = slice(XA_CH * hd + 2 * k, XA_CH * hd + 2 * k + 2)
                                ins = ve.tensor_tensor(act[:, 1, ks, :], b2(k), act[:, 0, ks, :].bitcast(F32), ALU.subtract)
                        else:
                            ins = ve.tensor_tensor(act[:, 1, c0 + hd, :], bank[0][:, 0:T], act[:, 0, c0 + hd, :].bitcast(F32),
                                                   ALU.subtract)
                        ins.then_inc(act_ready, 1)
                for s_ in (scores, exps, probs_t):
                    c.end(s_, len(units))
                c.end(head_hi, len(units) // 2)

            attention("cross")
            phase("wo", resid())

            norm(h, g("norm_mlp"))
            for r in range(FF1_ROUNDS):
                phase(f"w1_{r}", relu2)
                c.end(ev_a, PH["w1_0"].nblocks)
                phase(f"w2_{r}", resid())
            ve.wait_ge(mod_out, MOD_BODIES)
            ve.tensor_tensor(modt[:, 0:96], bank[2][:, 0:96], par("b_mod", 0, 96), ALU.add)
            chain(ve.tensor_tensor(modt[:, 96:128], bank[2][:, 96:128], par("b_mod", 0, 32), ALU.add))
            for to_, sc_at, name in ((GAIN_X, 16, "g_attn"), (GAIN_C, 112, "g_attn"), (GAIN_F, 64, "g_ffn")):
                chain(ve.scalar_tensor_tensor(small[:, to_:to_ + DC], modt[:, sc_at:sc_at + DC], 1.0, par(name, 0, DC), ALU.add, ALU.mult))

            def gs(at):
                return lambda k: small[:, at + k:at + k + 1]
            chain(norm(h, g("norm_final"), into=h))
            norm(kN[:, :, :, :].rearrange("p a b t -> p (a b) t"), gs(GAIN_C), shift=96)
            for name in ("ckv_c", "nak_c", "nav_c", "kr_c"):
                phase(name, nothing)
            norm(h, gs(GAIN_X), shift=0)
            for name in ("ckv_x", "nak_x", "nav_x", "cq", "naq", "fn", "kr_x"):
                phase(name, nothing)
            ve.wait_ge(bias_in, 32)
            for hd in range(NA_H):
                chain(ve.tensor_tensor(bias[:, hd, :, :], bias[:, hd, :, :], mask[:, :, :], ALU.add))
            attention("na", 8)
            for gg in range(FN_G):
                c.at(head_hi, gg + 1)
                ve.tensor_tensor(act[:, 1, 12 + gg, :], bank[0][:, 0:T], act[:, 0, 12 + gg, :].bitcast(F32), ALU.subtract).then_inc(act_ready, 1)
            c.end(head_hi, FN_G)
            norm(ckv[:, 1, :, :], g("g_kv"), LC)
            phase("kn_c", nothing)
            phase("v_c", nothing)
            norm(ckv[:, 0, :, :], g("g_kv"), LC, 4)
            phase("kn_x", nothing)
            phase("v_x", nothing)
            norm(cq, g("g_q"), LC)
            phase("qn", nothing)
            phase("qr", nothing)
            ve.wait_ge(block_free, FREE + PH["qr"].block0 + PH["qr"].nblocks)
            for n in range(1 + MLA_H // 2):
                x_ = kr[:, 0, :] if n == 0 else qR[:, n - 1, :]
                c.at(rope_pe, n + 1)
                if n:
                    c.at(rope_dve, n)
                ve.tensor_tensor(stat[:, 0, 0:T], x_, cc(CA, "cos"), ALU.mult)
                chain(ve.tensor_tensor(stat[:, 1, 0:T], bank[3 + n][:, 0:T], cc(CA, "sin"), ALU.mult))
                ve.tensor_tensor(x_, stat[:, 0, 0:T], stat[:, 1, 0:T], ALU.add).then_inc(rope_dve, 1)
            attention("mla")
            phase("wout2", resid(32))
            norm(h, gs(GAIN_F), shift=48)
            first = 0
            for r, n in enumerate(FF2_ROUNDS):
                phase(f"up_{r}", gated(first), 2 * 5)
                c.end(ev_a, 2 * n)
                first += n
                phase(f"down_{r}", resid(80))
            norm(h, g("g_final"), into=tmp).then_inc(out_ready, 1)


def slots_of(w, ph, cols=None):
    if cols is not None:
        w = np.concatenate([w[:, a:b] for a, b in cols], axis=1)
    n = ph.nblocks * ph.ncol
    assert w.shape == (ph.chunks * P, n), (ph.name, w.shape)
    w = w.reshape(ph.slots_per_block, ph.per_slot, P, ph.nblocks, ph.ncol)
    return w.transpose(3, 0, 2, 1, 4).reshape(ph.slots, P, SLOT)


def per_partition(v):
    return np.ascontiguousarray(v).reshape(-1, P).T


def feature_major(x):
    return x.reshape(T, -1, P).transpose(2, 1, 0).reshape(P, -1)


def kernel(**a):
    import concourse.bacc as bacc
    from concourse.bass_utils import run_bass_kernel_spmd

    a = {k: np.asarray(v) for k, v in a.items()}
    w_in, w_in2 = a["w_in"][0], a["w_in_2"][0]
    parts = {}
    parts["qkv"] = slots_of(w_in[:, 0:3072], PH["qkv"])
    parts["z"] = slots_of(w_in[:, 3072:4096], PH["z"])
    w_ba = w_in[:, 4096:4112]
    g0 = 4112
    parts["glu"] = slots_of(w_in, PH["glu"], [c for i in range(8) for c in (
        (g0 + P * i, g0 + P * (i + 1)), (g0 + 1024 + P * i, g0 + 1024 + P * (i + 1)))])
    parts["wout"] = slots_of(a["w_out"][0], PH["wout"])
    parts["memk"] = slots_of(a["xa_wk"][0], PH["memk"])
    parts["memv"] = slots_of(a["xa_wv"][0], PH["memv"])
    parts["wq"] = slots_of(a["xa_wq"][0], PH["wq"])
    parts["wo"] = slots_of(a["xa_wo"][0], PH["wo"])
    for r in range(FF1_ROUNDS):
        parts[f"w1_{r}"] = slots_of(a["mlp_w1"][0][:, D * r:D * (r + 1)], PH[f"w1_{r}"])
        parts[f"w2_{r}"] = slots_of(a["mlp_w2"][0][D * r:D * (r + 1), :], PH[f"w2_{r}"])
    at = {}
    o = 0
    for name, n in (("cq", LAT), ("ckv", LAT), ("kr", ROPE), ("naq", 512), ("nak", 512), ("nav", 512), ("fn", 512)):
        at[name] = (o, o + n)
        o += n
    for name in ("ckv", "nak", "nav"):
        for who in "cx":
            parts[f"{name}_{who}"] = slots_of(w_in2, PH[f"{name}_{who}"], [at[name]])
    for who in "cx":
        parts[f"kr_{who}"] = slots_of(w_in2, PH[f"kr_{who}"], [at["kr"], at["kr"]])
    for name in ("cq", "naq", "fn"):
        parts[name] = slots_of(w_in2, PH[name], [at[name]])
    ukv, uq = a["w_ukv_2"][0], a["w_uq_2"][0]
    for who in "cx":
        parts[f"kn_{who}"] = slots_of(ukv, PH[f"kn_{who}"], [(256 * i, 256 * i + 128) for i in range(MLA_H)])
        parts[f"v_{who}"] = slots_of(ukv, PH[f"v_{who}"], [(256 * i + 128, 256 * i + 256) for i in range(MLA_H)])
    parts["qn"] = slots_of(uq, PH["qn"], [(192 * i, 192 * i + 128) for i in range(MLA_H)])
    parts["qr"] = slots_of(uq, PH["qr"], [(192 * i + 128, 192 * i + 192) for i in range(MLA_H)])
    parts["wout2"] = slots_of(a["w_out_2"][0], PH["wout2"])
    first = 0
    for r, n in enumerate(FF2_ROUNDS):
        parts[f"up_{r}"] = slots_of(a["w_up_2"][0], PH[f"up_{r}"], [c for i in range(first, first + n) for c in (
            (P * i, P * (i + 1)), (D_FF2 + P * i, D_FF2 + P * (i + 1)))])
        parts[f"down_{r}"] = slots_of(a["w_down_2"][0][P * first:P * (first + n)], PH[f"down_{r}"])
        first += n
    stream = np.empty((N_SLOTS, P, SLOT), np.float32)
    for name, ph in PH.items():
        stream[ph.slot0:ph.slot0 + ph.slots] = parts.pop(name)
    mods = a["w_mod_2"][0].reshape(4, 4, P, MOD_BODIES, NCOL).transpose(3, 0, 2, 1, 4).reshape(-1, P, SLOT)

    def paired(v):
        v = v.reshape(v.shape[:-1] + (2, D_FF2 // P, P))
        return v.swapaxes(-3, -2).reshape(v.shape[:-3] + (88, P))

    vec = {
        "norm_mix": per_partition(a["norm_mix_g"]), "norm_mem": per_partition(a["norm_mem_g"]),
        "norm_xa": per_partition(a["norm_xa_g"]), "norm_mlp": per_partition(a["norm_mlp_g"]),
        "norm_final": per_partition(a["norm_final_g"]), "g_attn": per_partition(a["g_attn_2"]),
        "g_ffn": per_partition(a["g_ffn_2"]), "g_final": per_partition(a["g_final_2"]),
        "g_q": per_partition(a["g_q_2"]), "g_kv": per_partition(a["g_kv_2"]), "dn_norm": per_partition(a["dn_norm_g"]),
        "cf_b": per_partition(a["cf_dw_b"]), "ln_g": per_partition(a["cf_ln_g"]), "ln_b": per_partition(a["cf_ln_b"]),
        "dn_conv": a["dn_conv_w"][0].reshape(DN_TAPS, 24, P).transpose(2, 1, 0).reshape(P, -1),
        "cf_conv": a["cf_dw_w"][0].reshape(CF_TAPS, 8, P).transpose(2, 1, 0).reshape(P, -1),
        "ff_conv": paired(a["conv_w_2"][0]).transpose(2, 1, 0).reshape(P, -1),
        "ff_b": paired(a["conv_b_2"][0]).T, "b_mod": per_partition(a["b_mod_2"]),
        "c": per_partition(a["c_2"]), "c_ctx": per_partition(a["c_ctx_2"]),
        "a_log": np.broadcast_to(a["dn_a_log"][0], (P, 8)), "dt": np.broadcast_to(a["dn_dt_bias"][0], (P, 8)),
    }
    pvec = np.concatenate([vec[name] for name in PV], axis=1)
    eye = np.concatenate([np.eye(P), np.ones((P, P))], axis=1).astype(np.float32)
    i, j = np.arange(P)[:, None], np.arange(P)[None, :]
    levels = [((i // (2 * s) == j // (2 * s)) & (i % (2 * s) < s) & (j % (2 * s) >= s)).astype(np.float32) for s in (1, 2, 4, 8, 16, 32, 64)]
    upper = (i <= j).astype(np.float32)
    below = np.where(i <= j, 0.0, NEG).astype(np.float32)
    cmix = np.concatenate(levels + [upper, below, w_ba.reshape(DC, P, 16).transpose(1, 0, 2).reshape(P, -1)], axis=1)
    ang = 2 * np.pi * ((i * j) % P) / P
    dft_ch = np.concatenate([np.cos(ang), np.sin(ang)], axis=1)
    tt = np.arange(T)
    ang = 2 * np.pi * ((tt[:, None] * tt[None, :]) % T) / T

    def rows(m):
        return m.reshape(TT, P, T).transpose(1, 0, 2).reshape(P, -1)
    freqs = np.float32(10000.0) ** (-np.arange(16, dtype=np.float32) / 16)
    f = np.arange(P) % ROPE
    pos = np.where(f[:, None] < 32, tt[None, :] // GRID_W, tt[None, :] % GRID_W).astype(np.float32)
    angle = pos * freqs[f % 16][:, None]
    sign = np.where(f % 32 < 16, -1.0, 1.0)[:, None]
    swap = (i == (j ^ 16)).astype(np.float32)
    catt = np.concatenate([dft_ch, rows(np.cos(ang)), rows(-np.sin(ang)), np.cos(angle), sign * np.sin(angle), swap,
                           ], axis=1).astype(np.float32)
    catt = np.concatenate([catt, a["w_fnet_2"][0].transpose(1, 0, 2).reshape(P, -1)], axis=1)
    qr_, qw, kr_, kw = tt[:, None] // GRID_W, tt[:, None] % GRID_W, tt[None, :] // GRID_W, tt[None, :] % GRID_W
    start = np.clip(qw - NA_KW // 2, 0, GRID_W - NA_KW)
    inside = (kw >= start) & (kw < start + NA_KW)
    rel_col = np.clip(kw - qw + NA_KW - 1, 0, 2 * NA_KW - 2)
    table = a["na_rpb_2"][0][:, kr_ - qr_ + NA_KH - 1, rel_col]
    na_bias = table.reshape(NA_H, TT, P, T).transpose(2, 0, 1, 3).reshape(P, -1)
    na_mask = np.where(inside, 0.0, NEG).astype(np.float32).reshape(TT, P, T).transpose(1, 0, 2).reshape(P, -1)

    arrays = {
        "x_t": feature_major(a["x"][0]).reshape(P, DC, T), "mem_t": feature_major(a["mem"][0]), "ctx_t": feature_major(a["ctx_2"][0]),
        "stream": stream, "mods": mods, "pvec": pvec, "eye": eye, "cmix": cmix, "catt": catt, "na_bias": na_bias, "na_mask": na_mask,
    }
    nc = bacc.Bacc("TRN2", target_bir_lowering=False, num_devices=1)
    args = []
    for name, v in arrays.items():
        arrays[name] = np.ascontiguousarray(v)
        args.append(nc.dram_tensor(name, v.shape, mybir.dt.from_np(v.dtype), kind="ExternalInput").ap())
    args.append(nc.dram_tensor("out_t", (P, DC, T), F32, kind="ExternalOutput").ap())
    build(nc, *args)
    got = run_bass_kernel_spmd(nc, [arrays], core_ids=[0]).results[0]["out_t"]
    return got.transpose(2, 1, 0).reshape(1, T, D)
```

```python
import numpy as np
from contextlib import ExitStack

import concourse.bass as bass
from concourse import mybir
from concourse.alu_op_type import AluOpType as ALU

F32 = mybir.dt.float32
F32R = mybir.dt.float32r
ACT = mybir.ActivationFunctionType
AX = mybir.AxisListType
ds = bass.ds

P = 128
D = 2048
T = 256
DC = D // P
TT = T // P
EPS = 1e-6
D_DELTA, D_CONV = 1024, 1024
DN_H, DN_TAPS, CF_TAPS = 8, 4, 31
XA_H = 4
XA_CH = DC // XA_H
XA_SCALE = float(512) ** -0.5
D_FF1, D_FF2 = 8192, 5632
MLA_H, NOPE, ROPE, LAT = 8, 128, 64, 512
LC = LAT // P
MLA_SCALE = float(NOPE + ROPE) ** -0.5
NA_H, NA_KH, NA_KW, GRID_W = 4, 8, 16, 64
NA_SCALE = float(P) ** -0.5
FN_G = 4
FN_SCALE = float(T * P) ** -0.5
NEG = -1e30

SLOT = 1024
RAW_N, SPL_N, MOD_N = 8, 4, 2
NCOL = 256
LAG = 3


class Phase:

    def __init__(self, name, nblocks, chunks, per_body=2, per_slot=4, ncol=NCOL, flip=False, mod=0):
        self.name, self.nblocks, self.chunks, self.flip, self.mod = name, nblocks, chunks, flip, mod
        self.K, self.per_slot, self.ncol = per_body, per_slot, ncol
        self.iters = nblocks // per_body
        self.slots_per_block = -(-chunks // per_slot)
        self.S = self.slots_per_block * per_body
        self.slots = self.slots_per_block * nblocks


FF1_ROUNDS = 4
FF2_ROUNDS = (16, 16, 12)


def phases():
    out = [
        Phase("glu", 8, DC), Phase("qkv", 12, DC, per_body=4), Phase("z", 4, DC),
        Phase("wout", 8, DC),
        Phase("memk", 8, DC, mod=2), Phase("memv", 8, DC, flip=True, mod=2),
        Phase("wq", 8, DC, mod=2), Phase("wo", 8, DC, mod=2),
    ]
    for r in range(FF1_ROUNDS):
        out += [Phase(f"w1_{r}", 8, DC, mod=1), Phase(f"w2_{r}", 8, DC, mod=1)]
    for who in ("c", "x"):
        out += [Phase("ckv_" + who, 2, DC), Phase("nak_" + who, 2, DC), Phase("nav_" + who, 2, DC, flip=True)]
        if who == "x":
            out += [Phase("cq", 2, DC), Phase("naq", 2, DC), Phase("fn", 2, DC)]
        out += [Phase("kr_" + who, 1, DC, per_body=1, per_slot=8, ncol=P)]
    for who in ("c", "x"):
        out += [Phase("kn_" + who, 4, LC, per_body=4), Phase("v_" + who, 4, LC, per_body=4, flip=True)]
    out += [Phase("qn", 4, LC, per_body=4), Phase("qr", 2, LC, per_body=2)]
    out += [Phase("wout2", 8, DC)]
    for r, n in enumerate(FF2_ROUNDS):
        out += [Phase(f"up_{r}", n, DC, per_body=2 if n % 2 == 0 else 1)]
        out += [Phase(f"down_{r}", 8, n, per_body=2 if n == 16 else 8)]
    slot = block = mod = 0
    with_mod = [ph for ph in out if ph.mod]
    for ph in out:
        ph.slot0, ph.block0 = slot, block
        ph.mod0 = mod
        if ph.mod:
            n = with_mod.index(ph)
            ph.mod_half, ph.mod_block0 = n % 2, n // 2 * ph.iters
            assert (ph.mod == 2) == (ph.mod_block0 < MOD_CTX // 2)
        slot += ph.slots
        block += ph.nblocks
        mod += ph.iters if ph.mod else 0
        assert ph.iters == 1 or (ph.S % RAW_N == 0 and ph.K % 2 == 0), ph.name
    return {ph.name: ph for ph in out}, slot


MOD_COL = 512
MOD_BODIES = 48
MOD_CTX = 16
MOD_K = DC // 2
MOD_AT = ((0, 1), (2, 3), (4,), (5,), (6,), (7,))
MOD_OUT_AT = 4
PRE = 3
PH, N_SLOTS = phases()
MOD_ORDER = [(ph.mod_half, ph.mod_block0 + i) for ph in PH.values() if ph.mod for i in range(ph.iters)]


def columns(parts):
    at, out = 0, {}
    for name, n in parts:
        out[name] = (at, at + n)
        at += n
    return out, at


PV, N_PV = columns([
    ("norm_mix", DC), ("norm_mem", DC), ("norm_xa", DC), ("norm_mlp", DC), ("norm_final", DC),
    ("g_attn", DC), ("g_ffn", DC), ("g_final", DC), ("g_q", LC), ("g_kv", LC), ("dn_norm", 1),
    ("cf_b", 8), ("ln_g", 8), ("ln_b", 8), ("dn_conv", 24 * DN_TAPS), ("cf_conv", 8 * CF_TAPS),
    ("ff_conv", 88 * 3), ("ff_b", 88), ("b_mod", 96), ("c", DC), ("c_ctx", DC), ("a_log", 8), ("dt", 8),
])
CM, N_CM = columns([
    ("levels", 7 * P), ("upper", P), ("below", P), ("w_ba", DC * 16)])
CA, N_CA = columns([
    ("dft_ch", 2 * P), ("dft_cos", TT * T), ("dft_sin", TT * T), ("cos", T), ("sin", T), ("swap", P),
    ("w_fnet", FN_G * P)])
N_CZ = max(N_CM, N_CA)



def build(nc, x_t, mem_t, ctx_t, stream, mods, pvec, eye, cmix, catt, na_bias, na_mask, out_t):
    es = ExitStack()
    with es:
        def sb(name, shape, dt=F32, stack=None):
            return (stack or es).enter_context(nc.sbuf_tensor(name, shape, dt))

        def sem(name):
            return es.enter_context(nc.semaphore(name))

        raw = sb("raw", [P, RAW_N, SLOT])
        whi = sb("whi", [P, SPL_N, SLOT], F32R)
        wlo = sb("wlo", [P, SPL_N, SLOT], F32R)
        act = sb("act", [P, 2, DC, T], F32R)
        h = sb("h", [P, DC, T])
        tmp = sb("tmp", [P, DC, T])
        pv = sb("pv", [P, N_PV])
        cz = sb("cz", [P, N_CZ])
        ident = sb("ident", [P, P])
        ones = sb("ones", [P, P])
        stat = sb("stat", [P, 2, 512])
        modt = sb("modt", [P, P])
        msum = sb("msum", [P, 2, MOD_BODIES * 4])
        small = sb("small", [P, 256])
        gt = sb("gt", [P, 12, 16])
        ev = sb("ev", [P, 2, 512])
        with ExitStack() as first:
            modraw = sb("modraw", [P, MOD_N, SLOT], stack=first)
            modacc = sb("modacc", [P, 2, MOD_COL], stack=first)
            with ExitStack() as mixer:
                qkvT = sb("qkvT", [P, 24, T], stack=mixer)
                zT = sb("zT", [P, 8, T], stack=mixer)
                cin = sb("cin", [P, 8, T + CF_TAPS - 1], stack=mixer)
            with ExitStack() as cross:
                memK = sb("memK", [P, DC, T], stack=cross)
                memV = sb("memV", [P, TT, D], stack=cross)
            with ExitStack() as mlp:
                hid = sb("hid", [P, 2, DC, T], F32R, stack=mlp)
        with ExitStack() as second:
            cq = sb("cq", [P, LC, T], stack=second)
            ckv = sb("ckv", [P, 2, LC, T], stack=second)
            kr = sb("kr", [P, 2, T], stack=second)
            with ExitStack() as local:
                naK = sb("naK", [P, NA_H, 2, T], stack=local)
                naV = sb("naV", [P, 2, TT, NA_H * P], stack=local)
                naQ = sb("naQ", [P, NA_H, T], stack=local)
                fT = sb("fT", [P, FN_G, T], stack=local)
                bias = sb("bias", [P, NA_H, TT, T], stack=local)
                mask = sb("mask", [P, TT, T], stack=local)
            with ExitStack() as latent:
                kN = sb("kN", [P, MLA_H, 2, T], stack=latent)
                mlaV = sb("mlaV", [P, 2, TT, MLA_H * P], stack=latent)
                qR = sb("qR", [P, MLA_H // 2, T], stack=latent)
        qN = tmp[:, 8:16, :]
        memory = memV[:, :, :].rearrange("p a (b t) -> p (a b) t", t=T)

        def tiles(t, n):
            flat = t.rearrange("p a b -> p (a b)") if len(t.shape) == 3 else t
            return [flat[:, 512 * k:512 * k + 512].rearrange("p (a b) -> p a b", a=4) for k in range(n)]
        T_TMP, T_CIN, T_EV = tiles(tmp[:, :, :], 8), tiles(cin[:, :, :], 4), tiles(ev[:, :, :], 2)
        T_STAT, T_MOD = tiles(stat[:, :, :], 2), tiles(modraw[:, :, :], 4)
        X, XT, Y, MT = ([T_TMP[4 * hg + k] for hg in range(2)] for k in range(4))
        AT, ATT = ([T_CIN[2 * hg + k] for hg in range(2)] for k in range(2))
        VB, ST = T_EV, T_STAT
        KW, QDT = ([T_MOD[2 * hg + k] for hg in range(2)] for k in range(2))
        KBT, EG, DT = X, Y, MT
        U_, VN, WT = AT, MT, Y

        bank = [es.enter_context(nc.psum_tensor(f"bank{i}", [P, 512], F32)) for i in range(8)]


        def b2(k):
            return bank[k][:, :].rearrange("p (a b) -> p a b", a=2)

        def b4(k):
            return bank[k][:, :].rearrange("p (a b) -> p a b", a=4)

        def par(name, k=0, n=1):
            return pv[:, PV[name][0] + k:PV[name][0] + k + n] if isinstance(k, int) else pv[:, ds(k + PV[name][0], n)]

        def cc(table, name):
            return cz[:, table[name][0]:table[name][1]]

        raw_in = [sem(f"raw_in{k}") for k in range(RAW_N)]
        mod_in = [sem(f"mod_in{k}") for k in range(MOD_N)]
        mod_used = sem("mod_used")
        mod_out = sem("mod_out")
        hi_done = sem("hi_done")
        split_done = sem("split_done")
        slot_used = sem("slot_used")
        block_free = sem("block_free")
        ev_a = sem("ev_a")
        ev_v = sem("ev_v")
        act_step = sem("act_step")
        dve_step = sem("dve_step")
        params_in = sem("params_in")
        late_in = sem("late_in")
        src_in = sem("src_in")
        squares = sem("squares")
        sums = sem("sums")
        res_sq = sem("res_sq")
        res_sum = sem("res_sum")
        h_sums, h_var, h_std, h_root = sem("h_sums"), sem("h_var"), sem("h_std"), sem("h_root")
        mem_sq, mem_sum = sem("mem_sq"), sem("mem_sum")
        var = sem("var")
        root = sem("root")
        std = sem("std")
        spread = sem("spread")
        normed = sem("normed")
        norm_hi = sem("norm_hi")
        act_ready = sem("act_ready")
        gate_pe, gate_act, gate_dve = sem("gate_pe"), sem("gate_act"), sem("gate_dve")
        l2_pe, l2_act, l2_dve, l2_sq = sem("l2_pe"), sem("l2_act"), sem("l2_dve"), sem("l2_sq")
        cf_pe, cf_act, cf_dve = sem("cf_pe"), sem("cf_act"), sem("cf_dve")
        dl_pe, dl_act, dl_dve = ([sem(f"dl_{e}{hg}") for hg in range(2)] for e in ("pe", "act", "dve"))
        on_pe, on_act, on_dve = sem("on_pe"), sem("on_act"), sem("on_dve")
        scores, maxes, exps, probs = sem("scores"), sem("maxes"), sem("exps"), sem("probs")
        probs_t, probs_c, heads, head_hi = sem("probs_t"), sem("probs_c"), sem("heads"), sem("head_hi")
        fn_pe, fn_act = sem("fn_pe"), sem("fn_act")
        ctx_in, bias_in, mem_in = sem("ctx_in"), sem("bias_in"), sem("mem_in")
        mixed = sem("mixed")
        rope_pe, rope_dve = sem("rope_pe"), sem("rope_dve")
        mod_ready = sem("mod_ready")
        bias_ready = sem("bias_ready")
        out_ready, stored = sem("out_ready"), sem("stored")
        EV0 = 1
        EV_UP = 1
        FREE = 2

        class Counts:

            def __init__(self, eng):
                self.eng, self.base = eng, {}

            def at(self, s, n):
                v = n + self.base.get(s.name, 0)
                if not isinstance(v, int) or v > 0:
                    self.eng.wait_ge(s, v)

            def end(self, s, n):
                self.base[s.name] = self.base.get(s.name, 0) + n

        class Chain:

            def __init__(self, eng, s):
                self.eng, self.s, self.n, self.i, self.per = eng, s, 0, 0, 0

            def __call__(self, ins):
                ins.then_inc(self.s, 1)
                self.n += 1
                self.eng.wait_ge(self.s, self.i * self.per + self.n)

            def tick(self, ins):
                ins.then_inc(self.s, 1)
                self.n += 1

            def now(self):
                return self.i * self.per + self.n

            def loop(self, i, per):
                self.n, self.i, self.per, self.mark = self.n - per, i, per, self.n

            def end(self, iters):
                assert self.n == self.mark, (self.n, self.mark)
                self.n, self.i, self.per = self.n + self.per * (iters - 1), 0, 0

        block = es.enter_context(nc.Block())

        def over(eng, ph, slot_of, evac_fn, chain, links, extra=None):
            ends = [(k + 1) * ph.slots_per_block - 1 + LAG for k in range(ph.K)]
            order = list(PH.values())
            n = order.index(ph)
            slot_fn = slot_of(ph)

            def body(i, first, done):
                for j in range(ph.S):
                    if j >= done:
                        slot_fn(i, j)
                    if extra:
                        extra(i, j)
                    for k, t in enumerate(ends):
                        if t == j:
                            evac_fn(i * ph.K + k, (ph.block0 + k) % 2, k)
                        elif t - ph.S == j and not first:
                            evac_fn((i - 1) * ph.K + k, (ph.block0 + k) % 2, k)

            body(0, True, min(PRE, ph.S) if n else 0)
            if ph.iters > 1:
                with eng.Fori(1, ph.iters) as i:
                    chain.loop(i, links)
                    body(i, False, 0)
                chain.end(ph.iters)
            after = order[n + 1] if n + 1 < len(order) else None
            for j in range(LAG):
                if after and j < min(PRE, after.S):
                    slot_of(after)(0, j)
                for k, t in enumerate(ends):
                    if t - ph.S == j:
                        evac_fn((ph.iters - 1) * ph.K + k, (ph.block0 + k) % 2, k)

        @block.sync
        def _(sp):
            def load(body, j):
                sp.wait_ge(split_done, body * RAW_N + (j + 1))
                sp.dma_start(raw[:, j, :], stream[ds(body * RAW_N + j, 1), :, :].rearrange("a p n -> (a p) n")
                             ).then_inc(raw_in[j], 16)

            def load_mod(body, q):
                sp.wait_ge(mod_used, body * 4 + (q + 1))
                sp.dma_start(modraw[:, q % MOD_N, :], mods[ds(body * 4 + q, 1), :, :].rearrange("a p n -> (a p) n")
                             ).then_inc(mod_in[q % MOD_N], 16)

            def bodies(first, last, mod=False):
                with sp.Fori(first, last) as b:
                    for j in range(RAW_N):
                        load(b, j)
                        if mod and j % 2:
                            load_mod(b - first, j // 2)

            with_mod = PH["memk"].slot0 // RAW_N
            bodies(0, with_mod)
            bodies(with_mod, with_mod + MOD_BODIES, True)
            bodies(with_mod + MOD_BODIES, N_SLOTS // RAW_N)
            for j in range(N_SLOTS % RAW_N):
                load(N_SLOTS // RAW_N, j)
            sp.wait_ge(out_ready, 1)
            sp.dma_start(out_t, tmp[:, :, :]).then_inc(stored, 16)
            sp.wait_ge(stored, 16)

        @block.gpsimd
        def _(pool):
            for dst, src in ((pv, pvec), (ident, eye[:, 0:P]), (ones, eye[:, P:2 * P]), (cz[:, 0:N_CM], cmix)):
                pool.dma_start(dst[:, :] if dst is not cz else dst, src).then_inc(params_in, 16)
            pool.dma_start(h[:, :, :], x_t).then_inc(src_in, 16)
            pool.wait_ge(mixed, 1)
            pool.dma_start(memV[:, :, :].rearrange("p a b -> p (a b)"), mem_t).then_inc(mem_in, 16)
            pool.dma_start(cz[:, 0:N_CA], catt).then_inc(late_in, 16)
            last = PH["w2_3"]
            pool.wait_ge(block_free, FREE + last.block0 + last.nblocks)
            pool.dma_start(kN[:, :, :, :].rearrange("p a b c -> p (a b c)"), ctx_t).then_inc(ctx_in, 16)
            pool.dma_start(bias[:, :, :, :].rearrange("p a b c -> p (a b c)"), na_bias).then_inc(bias_in, 16)
            pool.dma_start(mask[:, :, :].rearrange("p a b -> p (a b)"), na_mask).then_inc(bias_in, 16)

        BETA, A1, LN1, EA, G, GC, NGC, EGC, BEG, KDL, KDS = range(11)
        C_SILU, GAIN_X, GAIN_C, GAIN_F, SM, ROOT, H_ROOT, L2, ON = 0, 32, 48, 64, 96, 112, 116, 128, 176

        def gtc(row, ch, hd, n=1):
            return gt[:, row, ch * 8 + hd:ch * 8 + hd + n]

        LEVELS = 7
        GROUPS, CHUNKS = range(2), range(TT)
        PE_SIG = [["bc", "tr", "aa"] + [f"{a}{l}" for l in range(LEVELS) for a in "yz"] + ["uw"] + ["ws"] * ch + ["o"]
                  for ch in CHUNKS]
        ACT_SIG = [["eg"] * ch + ["dtx"] + ["kds"] * (1 - ch) + ["tok"] + [f"y{l}" for l in range(LEVELS)] + ["uc", "oc"]
                   for ch in CHUNKS]
        DVE_SIG = [["dta"] + ["kdl"] * (1 - ch) + ["kb", "vb", "aat", "m0"] + [a for l in range(LEVELS)
                   for a in ([f"m{l + 1}"] if l + 1 < LEVELS else []) + [f"x{l}"]] + ["vn"] * ch for ch in CHUNKS]

        def step(table, ch, name):
            return sum(len(table[k]) for k in range(ch)) + table[ch].index(name) + 1

        def bk(hg, k):
            return b4(4 * hg + k)

        def attention_units(kind):
            return [(hd, mt) for hd in range({"cross": XA_H, "mla": MLA_H, "na": NA_H}[kind]) for mt in range(TT)]

        def key_tiles(kind):
            return TT if kind == "cross" else 2 * TT

        @block.tensor
        def _(pe):
            c = Counts(pe)

            def phase(ph, src, c0=0, after=None):
                def body(i):
                    for k in range(ph.K):
                        b = bank[(ph.block0 + k) % 2]
                        pe.wait_ge(block_free, i * ph.K + (ph.block0 + k + 1))
                        for sl in range(ph.slots_per_block):
                            j = k * ph.slots_per_block + sl
                            pe.wait_ge(split_done, i * ph.S + (ph.slot0 + j + 1 + RAW_N))
                            if after and k == 0:
                                c.at(after[0], after[1] + (sl + 1) * after[2])
                            buf = (ph.slot0 + j) % SPL_N
                            for ci in range(ph.per_slot):
                                kc = sl * ph.per_slot + ci
                                for hf in range(ph.ncol // P if not ph.flip else TT):
                                    for n, (wx, ax) in enumerate(((whi, 0), (whi, 1), (wlo, 0))):
                                        if ph.flip:
                                            lhs = src[:, ax, c0 + kc, hf * P:(hf + 1) * P]
                                            rhs = wx[:, buf, ci * NCOL:(ci + 1) * NCOL]
                                        else:
                                            lhs = wx[:, buf, ci * ph.ncol + hf * P:ci * ph.ncol + (hf + 1) * P]
                                            rhs = src[:, ax, c0 + kc, :]
                                        mm = pe.matmul(b[:, hf * T:(hf + 1) * T], lhs, rhs,
                                                       start=(kc == 0 and hf == 0 and n == 0),
                                                       stop=(kc == ph.chunks - 1 and n == 2), skip_group_check=True)
                            mm.then_inc(slot_used, 1)
                            if ph.mod and j == MOD_OUT_AT:
                                mod_matmuls(ph, i)
                if ph.iters > 1:
                    with pe.Fori(0, ph.iters) as i:
                        body(i)
                else:
                    body(0)

            def mod_matmuls(ph, i):
                mb = i + ph.mod0
                pe.wait_ge(mod_used, mb * 4 + (4 + MOD_N))
                for w in range(ph.mod):
                    for n in range(MOD_COL // P):
                        mm = pe.matmul(bank[2][:, 4 * w + n:4 * w + n + 1], modacc[:, w, n * P:(n + 1) * P],
                                       ones[:, 0:1], start=True, stop=True, skip_group_check=True)
                mm.then_inc(mod_out, 1)

            def row_sums(out, src, tok, start, stop):
                return pe.matmul(out, src[:, tok], ones[:, 0:1], start=start, stop=stop, skip_group_check=True)

            def over_features(out, col, n, start=True):
                return pe.matmul(out, small[:, col + n:col + n + 1].to_broadcast([P, P]), ident[:, :], start=start, stop=True,
                                 skip_group_check=True)

            def norm_root(b, col, s_):
                c.at(s_, 1)
                c.end(s_, 1)
                for mt in range(TT):
                    mm = over_features(bank[b][:, T + mt * P:T + (mt + 1) * P], col, mt, mt == 0)
                mm.then_inc(spread, 1)

            def norm(chunks=DC):
                for q in range(chunks // 4):
                    c.at(squares, q + 1)
                    for k in range(4 * q, 4 * q + 4):
                        for mt in range(TT):
                            mm = row_sums(bank[3][:, mt:mt + 1], tmp[:, k, :], slice(mt * P, (mt + 1) * P),
                                          k == 0 and mt == 0, k == chunks - 1)
                mm.then_inc(sums, 1)
                c.end(squares, chunks // 4)
                norm_root(3, ROOT, root)

            def residual_sums(b, s_):
                c.at(res_sum, 1)
                c.end(res_sum, 1)
                for hf in range(2):
                    for mt in range(TT):
                        mm = row_sums(bank[b][:, mt:mt + 1], stat[:, 1, :], slice(hf * T + mt * P, hf * T + (mt + 1) * P),
                                      hf == 0 and mt == 0, hf == 1)
                mm.then_inc(s_, 1)

            def act_in(n):
                c.at(act_ready, n)
                c.end(act_ready, n)

            def phase_in(name):
                phase(PH[name], act, after=(act_ready, 0, 1))
                c.end(act_ready, DC // 4)

            def phase_out(ph):
                pe.wait_ge(block_free, FREE + ph.block0 + ph.nblocks)

            pe.wait_ge(params_in, 64)
            norm()
            act_in(4)
            for mt in range(TT):
                for k in range(DC):
                    mm = pe.matmul(bank[3][:, 16 * mt:16 * mt + 16], tmp[:, k, mt * P:(mt + 1) * P],
                                   cc(CM, "w_ba")[:, 16 * k:16 * k + 16], start=(k == 0), stop=(k == DC - 1))
            mm.then_inc(gate_pe, 1)
            for name in ("glu", "qkv", "z"):
                phase(PH[name], act)
            c.at(cf_dve, 1)
            for k in range(8):
                mm = pe.matmul(bank[2][:, 0:T], ones[:, :], tmp[:, k, :], start=(k == 0), stop=(k == 7))
            mm.then_inc(cf_pe, 1)
            c.at(gate_dve, 2)
            for mt in range(TT):
                mm = pe.matmul(bank[3][:, 32 + 8 * mt:40 + 8 * mt], cc(CM, "upper"), gtc(G, mt, 0, 8), start=True, stop=True)
            mm.then_inc(gate_pe, 1)
            for p in range(8):
                c.at(l2_sq, p + 1)
                for n in range(4):
                    mm = row_sums(bank[4][:, 4 * p + n:4 * p + n + 1], ev[:, p % 2, :], slice(n * P, (n + 1) * P), True, True)
                mm.then_inc(l2_pe, 1)
            c.at(cf_act, 1)
            for mt in range(TT):
                for k in range(8):
                    mm = row_sums(bank[4][:, 32 + mt:33 + mt], tmp[:, 8 + k, :], slice(mt * P, (mt + 1) * P), k == 0, k == 7)
            mm.then_inc(cf_pe, 1)
            c.at(l2_dve, 2)
            for p in range(8):
                if p >= 4:
                    c.at(l2_dve, p - 1)
                for n in range(4):
                    mm = over_features(bank[4 + p % 4][:, n * P:(n + 1) * P], L2, 4 * p + n, n == 0)
                mm.then_inc(l2_pe, 1)
            for mt in range(TT):
                mm = over_features(bank[2][:, mt * P:(mt + 1) * P], L2, 32 + mt, mt == 0)
            mm.then_inc(cf_pe, 1)
            c.at(cf_dve, 6)
            for ch in CHUNKS:
                tok = slice(ch * P, (ch + 1) * P)

                def a(hg, name):
                    c.at(dl_act[hg], step(ACT_SIG, ch, name))

                def v(hg, name):
                    c.at(dl_dve[hg], step(DVE_SIG, ch, name))
                for hg in GROUPS:
                    if ch:
                        c.at(dl_act[hg], step(ACT_SIG, ch - 1, "oc"))
                    for n in range(4):
                        pe.matmul(bk(hg, 0)[:, n, :], gtc(G, ch, 4 * hg + n).to_broadcast([P, P]), cc(CM, "upper"), start=True, stop=True)
                    for n in range(4):
                        mm = pe.matmul(bk(hg, 1)[:, n, :], gtc(BETA, ch, 4 * hg + n).to_broadcast([P, P]), ident[:, :], start=True, stop=True)
                    mm.then_inc(dl_pe[hg], 1)
                    for n in range(4):
                        pe.transpose(bk(hg, 2)[:, n, :], qkvT[:, 8 + 4 * hg + n, tok], ident[:, :])
                    for n in range(4):
                        mm = pe.transpose(bk(hg, 3)[:, n, :], qkvT[:, 16 + 4 * hg + n, tok], ident[:, :])
                    mm.then_inc(dl_pe[hg], 1)
                for hg in GROUPS:
                    v(hg, "kb")
                    for n in range(4):
                        pe.matmul(bk(hg, 0)[:, n, :], qkvT[:, 8 + 4 * hg + n, tok], KBT[hg][:, n, :], start=True, stop=True)
                    for n in range(4):
                        mm = pe.matmul(bk(hg, 1)[:, n, :], qkvT[:, 8 + 4 * hg + n, tok], qkvT[:, 4 * hg + n, tok], start=True, stop=True)
                    mm.then_inc(dl_pe[hg], 1)
                for lv in range(LEVELS):
                    for hg in GROUPS:
                        v(hg, f"m{lv}")
                        if lv:
                            v(hg, f"x{lv - 1}")
                        for n in range(4):
                            mm = pe.matmul(bk(hg, 0)[:, n, :], MT[hg][:, n, :], X[hg][:, n, :], start=True, stop=True)
                        mm.then_inc(dl_pe[hg], 1)
                    for hg in GROUPS:
                        a(hg, f"y{lv}")
                        if lv + 1 < LEVELS:
                            for n in range(4):
                                pe.matmul(bk(hg, 2)[:, n, :], XT[hg][:, n, :], Y[hg][:, n, :], start=True, stop=True)
                        for n in range(4):
                            mm = pe.matmul(bk(hg, 3)[:, n, :], Y[hg][:, n, :], XT[hg][:, n, :], start=True, stop=True)
                        mm.then_inc(dl_pe[hg], 1)
                for hg in GROUPS:
                    v(hg, f"x{LEVELS - 1}")
                    for n in range(4):
                        mm = pe.matmul(bk(hg, 1)[:, n, :], XT[hg][:, n, :], VB[hg][:, n, :], start=True, stop=True)
                    if ch:
                        for n in range(4):
                            mm = pe.matmul(bk(hg, 2)[:, n, :], KW[hg][:, n, :], XT[hg][:, n, :], start=True, stop=True)
                    mm.then_inc(dl_pe[hg], 1)
                if ch:
                    for hg in GROUPS:
                        a(hg, "uc")
                        for n in range(4):
                            mm = pe.matmul(bk(hg, 0)[:, n, :], WT[hg][:, n, :], ST[hg][:, n, :], start=True, stop=True)
                        mm.then_inc(dl_pe[hg], 1)
                for hg in GROUPS:
                    if ch:
                        v(hg, "vn")
                    else:
                        a(hg, "uc")
                    for n in range(4):
                        if ch:
                            pe.matmul(bk(hg, 3)[:, n, :], ST[hg][:, n, :], QDT[hg][:, n, :], start=True, stop=False)
                        mm = pe.matmul(bk(hg, 3)[:, n, :], VN[hg][:, n, :], ATT[hg][:, n, :], start=not ch, stop=True)
                    if not ch:
                        for n in range(4):
                            mm = pe.matmul(bk(hg, 2)[:, n, :], KW[hg][:, n, :], VN[hg][:, n, :], start=True, stop=True)
                    mm.then_inc(dl_pe[hg], 1)
            for hd in range(DN_H):
                c.at(on_act, hd // 4 + 1)
                for mt in range(TT):
                    mm = row_sums(bank[4][:, 2 * hd + mt:2 * hd + mt + 1], tmp[:, hd, :], slice(mt * P, (mt + 1) * P), True, True)
            mm.then_inc(on_pe, 1)
            c.at(on_dve, 2)
            for p in range(4):
                for n in range(4):
                    mm = over_features(bank[4 + p][:, n * P:(n + 1) * P], ON, 4 * p + n, n == 0)
                mm.then_inc(on_pe, 1)
            act_in(2 + 4)
            phase(PH["wout"], act)
            pe.wait_ge(mem_sum, 1)
            for q in range(4):
                for mt in range(TT):
                    mm = row_sums(bank[3][:, mt:mt + 1], memK[:, q, :], slice(mt * P, (mt + 1) * P), q == 0 and mt == 0, q == 3)
            mm.then_inc(sums, 1)
            residual_sums(4, h_sums)
            norm_root(3, ROOT, root)
            phase_in("memk")
            norm_root(4, H_ROOT, h_root)
            phase(PH["memv"], act)
            phase_in("wq")

            def attention(kind):
                units = attention_units(kind)
                kt = key_tiles(kind)
                for u in range(len(units) + 2):
                    if u < len(units):
                        hd, mt = units[u]
                        tok = slice(mt * P, (mt + 1) * P)
                        b = bank[3 + u % 2]
                        if kind == "cross":
                            for k in range(XA_CH):
                                mm = pe.matmul(b[:, 0:T], tmp[:, XA_CH * hd + k, tok], memK[:, XA_CH * hd + k, :],
                                               start=(k == 0), stop=(k == XA_CH - 1))
                        elif kind == "na":
                            mm = pe.matmul(b[:, :], naQ[:, hd, tok], naK[:, hd, :, :], start=True, stop=True)
                        else:
                            lo = ROPE * (hd % 2)
                            pe.matmul(b[:, :], qN[:, hd, tok], kN[:, hd, :, :], start=True, stop=False)
                            mm = pe.matmul(b[:, :], qR[lo:lo + ROPE, hd // 2, tok], kr[lo:lo + ROPE, :, :], start=False, stop=True)
                        mm.then_inc(scores, 1)
                    if 1 <= u <= len(units):
                        w = u - 1
                        c.at(probs, w + 1)
                        if w >= 2:
                            c.at(probs_c, w - 1)
                        for k in range(kt):
                            mm = pe.transpose(b4(5 + w % 2)[:, k, :], stat[:, w % 2, k * P:(k + 1) * P], ident[:, :])
                        mm.then_inc(probs_t, 1)
                    if u >= 3 and u % 2 == 1:
                        hd = (u - 3) // 2
                        c.at(probs_c, u - 1)
                        if hd:
                            c.at(act_ready, hd)
                        pt = ev[:, :, :].rearrange("p a (b t) -> p (a b) t", b=2)
                        for cd in range(XA_CH if kind == "cross" else 1):
                            b = bank[cd // 2 if kind == "cross" else 0]
                            for k in range(kt):
                                if kind == "cross":
                                    val = memV[:, k, (XA_CH * hd + cd) * P:(XA_CH * hd + cd + 1) * P]
                                elif kind == "na":
                                    val = naV[:, k // 2, k % 2, hd * P:(hd + 1) * P]
                                else:
                                    val = mlaV[:, k // 2, k % 2, hd * P:(hd + 1) * P]
                                mm = pe.matmul(b[:, T * (cd % 2):T * (cd % 2) + T], val, pt[:, k, :],
                                               start=(k == 0), stop=(k == kt - 1))
                        mm.then_inc(heads, 1)
                c.end(probs, len(units))
                c.end(probs_c, len(units))

            phase_out(PH["wq"])
            attention("cross")
            act_in(XA_H)
            phase(PH["wo"], act)
            residual_sums(3, sums)
            norm_root(3, ROOT, root)
            for r in range(FF1_ROUNDS):
                if r:
                    phase(PH[f"w1_{r}"], act)
                else:
                    phase_in("w1_0")
                phase(PH[f"w2_{r}"], hid, after=(ev_v, PH[f"w1_{r}"].nblocks * r + EV0, 2))
            c.end(ev_v, PH["w1_0"].nblocks * FF1_ROUNDS)
            residual_sums(5, sums)
            norm_root(5, ROOT, root)

            norm()
            phase_in("ckv_c")
            for name in ("nak_c", "nav_c", "kr_c"):
                phase(PH[name], act)
            norm()
            phase_in("ckv_x")
            for name in ("nak_x", "nav_x", "cq", "naq", "fn", "kr_x"):
                phase(PH[name], act)
            phase_out(PH["kr_x"])
            attention("na")
            act_in(NA_H)
            for g in range(FN_G):
                if g:
                    c.at(fn_act, 2 * g)
                for mt in range(TT):
                    mm = pe.matmul(bank[3][:, mt * T:(mt + 1) * T], fT[:, g, mt * P:(mt + 1) * P], cc(CA, "dft_ch"), start=True, stop=True)
                mm.then_inc(fn_pe, 1)
                c.at(fn_act, 2 * g + 1)
                for n in range(2 * TT):
                    mt, part = n // 2, n % 2
                    mm = pe.matmul(bank[4][:, 0:T], stat[:, 0, mt * T + part * P:mt * T + (part + 1) * P],
                                   cc(CA, ("dft_cos", "dft_sin")[part])[:, mt * T:(mt + 1) * T], start=(n == 0), stop=(n == 3))
                mm.then_inc(fn_pe, 1)
                c.at(fn_act, 2 * g + 2)
                if g:
                    c.at(act_ready, g)
                pe.matmul(bank[0][:, 0:T], cc(CA, "w_fnet")[:, g * P:(g + 1) * P], stat[:, 1, 0:T], start=True, stop=True).then_inc(heads, 1)
            act_in(FN_G)
            norm(LC)
            act_in(1)
            phase(PH["kn_c"], act)
            phase(PH["v_c"], act)
            norm(LC)
            act_in(1)
            phase(PH["kn_x"], act, 4)
            phase(PH["v_x"], act, 4)
            norm(LC)
            act_in(1)
            phase(PH["qn"], act)
            phase(PH["qr"], act)
            phase_out(PH["qr"])
            for n in range(1 + MLA_H // 2):
                src = kr[:, 0, :] if n == 0 else qR[:, n - 1, :]
                pe.matmul(bank[3 + n][:, 0:T], cc(CA, "swap"), src, start=True, stop=True).then_inc(rope_pe, 1)
            c.at(rope_dve, 1 + MLA_H // 2)
            attention("mla")
            act_in(MLA_H)
            phase(PH["wout2"], act)
            residual_sums(3, sums)
            norm_root(3, ROOT, root)
            done = 0
            for r, n in enumerate(FF2_ROUNDS):
                if r:
                    phase(PH[f"up_{r}"], act)
                else:
                    phase_in("up_0")
                phase(PH[f"down_{r}"], hid, after=(ev_v, EV_UP * done + EV0, 4 * EV_UP))
                done += n
            residual_sums(3, sums)
            norm_root(3, ROOT, root)

        @block.scalar
        def _(sc):
            c = Counts(sc)
            chain = Chain(sc, act_step)

            def slot(ph):
                def f(i, j):
                    at = ph.slot0 + j
                    sc.wait_ge(raw_in[at % RAW_N], i * (16 * (ph.S // RAW_N)) + 16 * (at // RAW_N + 1))
                    sc.wait_ge(slot_used, i * ph.S + (at + 1))
                    sc.activation(whi[:, at % SPL_N, :], raw[:, at % RAW_N, :], ACT.Copy).then_inc(hi_done, 1)
                return f

            def done(ph, n):
                sc.wait_ge(slot_used, n * ph.slots_per_block + (ph.slot0 + ph.slots_per_block + SPL_N))

            def to(dst, flip=False, func=ACT.Copy):
                def make(ph):
                    def f(n, b, k):
                        done(ph, n)
                        o = dst[:, 0:TT, ds(n * NCOL, NCOL)] if flip else dst[:, ds(n * 2, 2), :]
                        sc.activation(o, b2(b), func).then_inc(block_free, 1)
                    return f
                return make

            def one(dst):
                def make(ph):
                    def f(n, b, k):
                        done(ph, n)
                        sc.activation(dst, bank[b][:, 0:T], ACT.Copy).then_inc(block_free, 1)
                    return f
                return make

            def nothing(ph):
                return lambda n, b, k: None

            def conv4(ph):
                def f(n, b, k):
                    done(ph, n)
                    sc.wait_ge(block_free, n + (FREE + ph.block0))
                    for hf in range(2):
                        ins = sc.activation(ev[:, 0, hf * T:(hf + 1) * T], b2(b)[:, hf, :], ACT.Copy,
                                            scale=par("dn_conv", n * 8 + (4 * hf + 3)))
                    ins.then_inc(ev_a, 1)
                    sc.wait_ge(block_free, n + (FREE + ph.block0 + 1))
                    chain(sc.activation(qkvT[:, ds(n * 2, 2), :], ev[:, 0, :].rearrange("p (a b) -> p a b", a=2), ACT.Silu))
                return f

            def glu(ph):
                def f(n, b, k):
                    done(ph, n)
                    sc.wait_ge(block_free, n + (FREE + ph.block0))
                    sc.activation(ev[:, 0, 0:T], b2(b)[:, 1, :], ACT.Sigmoid).then_inc(ev_a, 1)
                return f

            def relu2(ph):
                def f(n, b, k):
                    done(ph, n)
                    c.at(ev_v, n + EV0)
                    sc.activation(ev[:, 0, :], bank[b][:, :], ACT.Relu).then_inc(block_free, 1)
                    sc.wait_ge(block_free, n + (FREE + ph.block0 + 1))
                    chain(sc.activation(ev[:, 1, :], ev[:, 0, :], ACT.Square))
                    sc.activation(hid[:, 0, ds(n * 2, 2), :], ev[:, 1, :].rearrange("p (a b) -> p a b", a=2),
                                  ACT.Copy).then_inc(ev_a, 1)
                return f

            def gated(first):
                def make(ph):
                    def f(n, b, k):
                        done(ph, n)
                        c.at(ev_v, n * EV_UP + EV0)
                        for hf in range(2):
                            ins = sc.activation(ev[:, 0, hf * T:(hf + 1) * T], b2(b)[:, hf, :], ACT.Identity,
                                                scale=par("ff_conv", n * 6 + (6 * first + 3 * hf + 1)),
                                                bias=par("ff_b", n * 2 + (2 * first + hf)))
                        ins.then_inc(ev_a, 1)
                        sc.wait_ge(block_free, n + (FREE + ph.block0 + 1))
                        sc.activation(ev[:, 1, 0:T], ev[:, 0, 0:T], ACT.Silu).then_inc(ev_a, 1)
                    return f
                return make

            def squared(ph):
                def f(n, b, k):
                    sc.wait_ge(block_free, n + (FREE + ph.block0 + 1))
                    sc.activation(ev[:, k % 2, :].rearrange("p (a b) -> p a b", a=2), h[:, ds(n * 2, 2), :], ACT.Square).then_inc(res_sq, 1)
                return f

            def phase(name, evac, links=0, extra=None):
                over(sc, PH[name], slot, evac(PH[name]), chain, links, extra)

            def before(name):
                sc.wait_ge(block_free, FREE + PH[name].block0)

            def norm(src, chunks=DC, c0=0, shift=None, split=True, rooted=False):
                for q in range(chunks // 4 if src is not None else 0):
                    sc.activation(tmp[:, 4 * q:4 * q + 4, :], src[:, 4 * q:4 * q + 4, :], ACT.Square).then_inc(squares, 1)
                if not rooted:
                    c.at(var, 1)
                    sc.activation(small[:, ROOT:ROOT + TT], small[:, ROOT:ROOT + TT], ACT.Sqrt).then_inc(std, 1)
                    c.end(var, 1)
                if split:
                    for q in range(chunks // 4):
                        c.at(normed, q + 1)
                        if shift is None:
                            ins = sc.activation(act[:, 0, c0 + 4 * q:c0 + 4 * q + 4, :], tmp[:, 4 * q:4 * q + 4, :], ACT.Copy)
                        else:
                            for k in range(4 * q, 4 * q + 4):
                                ins = sc.activation(act[:, 0, k, :], tmp[:, k, :], ACT.Identity, bias=modt[:, shift + k:shift + k + 1])
                        ins.then_inc(norm_hi, 1)
                    c.end(normed, chunks // 4)

            sc.wait_ge(params_in, 64)
            sc.activation(small[:, C_SILU:C_SILU + 2 * DC], pv[:, PV["c"][0]:PV["c_ctx"][1]], ACT.Silu).then_inc(mod_ready, 1)
            sc.wait_ge(src_in, 16)
            norm(h)
            phase("glu", glu)
            phase("qkv", conv4, PH["qkv"].K)
            phase("z", to(zT, func=ACT.Silu))

            def row(r):
                return gt[:, r, :]
            c.at(gate_dve, 1)
            sc.activation(row(BETA).rearrange("p (a b) -> p a b", a=2),
                          bank[3][:, 0:32].rearrange("p (a b) -> p a b", a=2)[:, :, 0:8], ACT.Sigmoid)
            sc.activation(gt[:, EA, 0:8], par("a_log", 0, 8), ACT.Exp)
            chain(sc.activation(row(LN1), row(A1), ACT.Abs))
            chain(sc.activation(row(LN1), row(LN1), ACT.Exp, scale=-1.0))
            sc.activation(row(LN1), row(LN1), ACT.Ln, bias=1.0).then_inc(gate_act, 1)

            def square(p):
                sc.activation(ev[:, p % 2, :].rearrange("p (a b) -> p a b", a=2), qkvT[:, 2 * p:2 * p + 2, :], ACT.Square).then_inc(l2_sq, 1)
            sc.wait_ge(act_step, chain.n)
            square(0)
            square(1)
            c.at(gate_pe, 2)
            gc = bank[3][:, 32:48]
            sc.activation(row(GC), gc, ACT.Copy)
            sc.activation(row(NGC), gc, ACT.Copy, scale=-1.0)
            sc.activation(row(EGC), gc, ACT.Exp).then_inc(gate_act, 1)
            for p in range(2, 8):
                c.at(l2_pe, p - 1)
                square(p)
            c.at(cf_dve, 3)
            sc.activation(tmp[:, 8:16, :], tmp[:, 0:8, :], ACT.Square).then_inc(cf_act, 1)
            c.at(l2_dve, 1)
            sc.activation(small[:, L2:L2 + 34], small[:, L2:L2 + 34], ACT.Sqrt).then_inc(l2_act, 1)
            for q in range(2):
                c.at(cf_dve, 4 + q)
                for k in range(4 * q, 4 * q + 4):
                    ins = sc.activation(tmp[:, 8 + k, :], tmp[:, k, :], ACT.Silu, bias=par("ln_b", k))
                chain(ins)
                sc.activation(act[:, 0, 8 + 4 * q:12 + 4 * q, :], tmp[:, 8 + 4 * q:12 + 4 * q, :], ACT.Copy).then_inc(cf_act, 1)
            c.at(cf_dve, 6)
            for ch in CHUNKS:
                tok = slice(ch * P, (ch + 1) * P)

                def p_(hg, name):
                    c.at(dl_pe[hg], step(PE_SIG, ch, name))

                def v(hg, name):
                    c.at(dl_dve[hg], step(DVE_SIG, ch, name))
                if ch:
                    for hg in GROUPS:
                        p_(hg, "bc")
                        sc.activation(EG[hg], bk(hg, 0), ACT.Exp).then_inc(dl_act[hg], 1)
                for hg in GROUPS:
                    v(hg, "dta")
                    for n in range(4):
                        ins = sc.activation(DT[hg][:, n, :], DT[hg][:, n, :], ACT.Exp, bias=gtc(NGC, ch, 4 * hg + n))
                    ins.then_inc(dl_act[hg], 1)
                    if not ch:
                        v(hg, "kdl")
                        kds = gt[:, KDS, 4 * hg:4 * hg + 4]
                        sc.activation(kds, gt[:, KDL, 4 * hg:4 * hg + 4], ACT.Exp).then_inc(dl_act[hg], 1)
                        c.at(dl_act[hg], step(ACT_SIG, ch, "kds"))
                    p_(hg, "tr")
                    for n in range(4):
                        w = gtc(BEG, ch, 4 * hg + n) if ch else gt[:, KDS, 4 * hg + n:4 * hg + n + 1]
                        ins = sc.activation(KW[hg][:, n, :], bk(hg, 2)[:, n, :], ACT.Copy, scale=w)
                    ins.then_inc(dl_act[hg], 1)
                for lv in range(LEVELS):
                    for hg in GROUPS:
                        p_(hg, f"y{lv}")
                        sc.activation(Y[hg], bk(hg, 0), ACT.Copy).then_inc(dl_act[hg], 1)
                for hg in GROUPS:
                    p_(hg, "uw")
                    if ch:
                        sc.activation(U_[hg], bk(hg, 1), ACT.Copy)
                        sc.activation(WT[hg], bk(hg, 2), ACT.Copy).then_inc(dl_act[hg], 1)
                    else:
                        sc.activation(VN[hg], bk(hg, 1), ACT.Copy).then_inc(dl_act[hg], 1)
                for hg in GROUPS:
                    p_(hg, "o")
                    ins = sc.activation(qkvT[:, 16 + 4 * hg:20 + 4 * hg, tok], bk(hg, 3), ACT.Copy)
                    if not ch:
                        ins = sc.activation(ST[hg], bk(hg, 2), ACT.Copy)
                    ins.then_inc(dl_act[hg], 1)
            for hg in GROUPS:
                c.at(dl_act[hg], step(ACT_SIG, TT - 1, "oc"))
            for q in range(2):
                sc.activation(tmp[:, 4 * q:4 * q + 4, :], qkvT[:, 16 + 4 * q:20 + 4 * q, :], ACT.Square).then_inc(on_act, 1)
            c.at(on_dve, 1)
            sc.activation(small[:, ON:ON + 16], small[:, ON:ON + 16], ACT.Sqrt).then_inc(on_act, 1)
            for p in range(4):
                c.at(on_dve, p + 3)
                sc.activation(act[:, 0, 2 * p:2 * p + 2, :], qkvT[:, 16 + 2 * p:18 + 2 * p, :], ACT.Copy).then_inc(on_act, 1)
            def memory_squares(i, j):
                if isinstance(i, int) and j == LAG + 1:
                    sc.wait_ge(mem_in, 16)
                    for q in range(4):
                        sc.activation(tmp[:, 4 * q:4 * q + 4, :], memory[:, 4 * q:4 * q + 4, :], ACT.Square).then_inc(mem_sq, 1)

            def h_sqrt(at):
                def f(i, j):
                    if isinstance(i, int) and j == at:
                        c.at(h_var, 1)
                        sc.activation(small[:, H_ROOT:H_ROOT + TT], small[:, H_ROOT:H_ROOT + TT], ACT.Sqrt).then_inc(h_std, 1)
                        c.end(h_var, 1)
                return f
            phase("wout", squared, 0, memory_squares)
            before("memk")
            norm(None)
            phase("memk", to(memK), 0, h_sqrt(6))
            phase("memv", to(memV, flip=True))
            before("wq")
            norm(None, rooted=True)
            phase("wq", to(tmp))

            def attention(kind, c0=0):
                units = attention_units(kind)
                kt = key_tiles(kind)
                nk = kt * P
                scale = {"cross": XA_SCALE, "mla": MLA_SCALE, "na": 1.0}[kind]
                for u in range(len(units) + 2):
                    if u < len(units):
                        pb = stat[:, u % 2, 0:nk]
                        c.at(maxes, u + 1)
                        sc.activation(pb, pb if kind == "na" else bank[3 + u % 2][:, 0:nk], ACT.Exp, scale=scale,
                                      bias=small[:, SM + 4 * (u % 2) + 1:SM + 4 * (u % 2) + 2],
                                      accum_out=small[:, SM + 4 * (u % 2) + 2:SM + 4 * (u % 2) + 3]).then_inc(exps, 1)
                    if 1 <= u <= len(units):
                        w = u - 1
                        hd, mt = units[w]
                        c.at(probs_t, w + 1)
                        if mt == 0 and hd:
                            c.at(heads, hd)
                        sc.activation(ev[:, :, :].rearrange("p a (b t) -> p (a b) t", b=2)[:, 0:kt, mt * P:(mt + 1) * P],
                                      b4(5 + w % 2)[:, 0:kt, :], ACT.Copy).then_inc(probs_c, 1)
                    if u >= 3 and u % 2 == 1:
                        hd = (u - 3) // 2
                        c.at(heads, hd + 1)
                        if kind == "cross":
                            for k in range(2):
                                ins = sc.activation(act[:, 0, XA_CH * hd + 2 * k:XA_CH * hd + 2 * k + 2, :], b2(k), ACT.Copy)
                        else:
                            ins = sc.activation(act[:, 0, c0 + hd, :], bank[0][:, 0:T], ACT.Copy)
                        ins.then_inc(head_hi, 1)
                c.end(maxes, len(units))
                c.end(probs_t, len(units))
                c.end(heads, len(units) // 2)

            before("wo")
            attention("cross")
            phase("wo", squared)
            before("w1_0")
            norm(None)
            for r in range(FF1_ROUNDS):
                phase(f"w1_{r}", relu2, 2)
                c.end(ev_v, PH["w1_0"].nblocks)
                phase(f"w2_{r}", squared if r == FF1_ROUNDS - 1 else nothing)
            before("ckv_c")
            norm(None, split=False)

            sc.wait_ge(ctx_in, 16)
            norm(kN[:, :, :, :].rearrange("p a b t -> p (a b) t"), shift=96)
            phase("ckv_c", to(ckv[:, 1, :, :]))
            phase("nak_c", to(naK[:, :, 1, :]))
            phase("nav_c", to(naV[:, 1, :, :], flip=True))
            phase("kr_c", one(kr[:, 1, :]))
            norm(h, shift=0)
            phase("ckv_x", to(ckv[:, 0, :, :]))
            phase("nak_x", to(naK[:, :, 0, :]))
            phase("nav_x", to(naV[:, 0, :, :], flip=True))
            phase("cq", to(cq))
            phase("naq", to(naQ))
            phase("fn", to(fT))
            phase("kr_x", one(kr[:, 0, :]))
            attention("na", 8)
            for g in range(FN_G):
                c.at(fn_pe, 2 * g + 1)
                if g:
                    c.at(heads, g)
                sc.activation(stat[:, 0, :], bank[3][:, :], ACT.Copy).then_inc(fn_act, 1)
                c.at(fn_pe, 2 * g + 2)
                sc.activation(stat[:, 1, 0:T], bank[4][:, 0:T], ACT.Copy, scale=FN_SCALE).then_inc(fn_act, 1)
                c.at(heads, g + 1)
                sc.activation(act[:, 0, 12 + g, :], bank[0][:, 0:T], ACT.Copy).then_inc(head_hi, 1)
            c.end(heads, FN_G)
            norm(ckv[:, 1, :, :], LC)
            phase("kn_c", to(kN[:, :, 1, :]))
            phase("v_c", to(mlaV[:, 1, :, :], flip=True))
            norm(ckv[:, 0, :, :], LC, 4)
            phase("kn_x", to(kN[:, :, 0, :]))
            phase("v_x", to(mlaV[:, 0, :, :], flip=True))
            norm(cq, LC)
            phase("qn", to(qN))
            phase("qr", to(qR))
            attention("mla")
            phase("wout2", squared)
            before("up_0")
            norm(None, shift=48)
            first = 0
            for r, n in enumerate(FF2_ROUNDS):
                phase(f"up_{r}", gated(first))
                c.end(ev_v, n * EV_UP)
                first += n
                phase(f"down_{r}", squared if r == len(FF2_ROUNDS) - 1 else nothing)
            norm(None, split=False)

        @block.vector
        def _(ve):
            c = Counts(ve)
            chain = Chain(ve, dve_step)
            ve.memset(cin[:, :, 0:CF_TAPS - 1], 0.0).then_inc(split_done, RAW_N)
            ve.memset(small[:, 120:121], 0.0).then_inc(slot_used, SPL_N)
            ve.memset(small[:, 122:123], 0.0).then_inc(block_free, FREE)
            ve.memset(small[:, 123:124], 0.0).then_inc(ev_v, EV0)

            mod_mark = {}

            def mod_store(n, both):
                ve.wait_ge(mod_out, n)
                return ve.tensor_copy(msum[:, 0:both, ds(n * 4 - 4, 4)], bank[2][:, 0:4 * both].rearrange("p (a b) -> p a b", a=both))

            def mod_chunk(ph, i, k):
                mb = i + ph.mod0
                q = k // 2
                if k % 2 == 0:
                    ve.wait_ge(mod_in[q % MOD_N], mb * 32 + 16 * (q // MOD_N + 1))
                if k == 0:
                    if not isinstance(mb, int):
                        mod_store(mb, ph.mod)
                    elif mb:
                        mod_store(mb, 2 if mb <= MOD_CTX else 1)
                elif k % 2 == 0:
                    ve.wait_ge(mod_used, mb * 4 + (k // 2 + MOD_N))
                else:
                    ve.wait_ge(dve_step, mod_mark[k - 1])
                for w in range(ph.mod):
                    wt = modraw[:, q % MOD_N, (k % 2) * MOD_COL:(k % 2 + 1) * MOD_COL]
                    at = C_SILU + DC * w + MOD_K * ph.mod_half + k
                    col = small[:, at:at + 1]
                    acc = modacc[:, w, :]
                    if k == 0:
                        ins = ve.tensor_scalar(acc, wt, col, None, ALU.mult)
                    else:
                        ins = ve.scalar_tensor_tensor(acc, wt, col, acc, ALU.mult, ALU.add)
                if k % 2:
                    ins.then_inc(mod_used, 1)
                else:
                    chain.tick(ins)
                    mod_mark[k] = chain.now()

            def slot(ph):
                def f(i, j):
                    at = ph.slot0 + j
                    ks = MOD_AT[j] if ph.mod and j < len(MOD_AT) else ()
                    for k in ks[:1]:
                        mod_chunk(ph, i, k)
                    ve.wait_ge(hi_done, i * ph.S + (at + 1))
                    ve.tensor_tensor(wlo[:, at % SPL_N, :], raw[:, at % RAW_N, :], whi[:, at % SPL_N, :].bitcast(F32),
                                     ALU.subtract).then_inc(split_done, 1)
                    for k in ks[1:]:
                        mod_chunk(ph, i, k)
                return f

            def done(ph, n):
                ve.wait_ge(slot_used, n * ph.slots_per_block + (ph.slot0 + ph.slots_per_block + SPL_N))

            def nothing(ph):
                return lambda n, b, k: None

            def conv4(ph):
                def f(n, b, k):
                    c.at(ev_a, n + 1)
                    for j in range(1, DN_TAPS):
                        for hf in range(2):
                            o = ev[:, 0, hf * T + j:(hf + 1) * T]
                            ins = ve.scalar_tensor_tensor(o, b2(b)[:, hf, 0:T - j], conv4_w[:, 8 * k + 4 * hf + 3 - j:8 * k + 4 * hf + 4 - j], o,
                                                          ALU.mult, ALU.add)
                            if j == DN_TAPS - 1 and hf:
                                ins.then_inc(block_free, 1)
                            else:
                                ins.then_inc(dve_step, 1)
                                chain.n += 1
                        if j < DN_TAPS - 1:
                            ve.wait_ge(dve_step, chain.i * chain.per + chain.n)
                return f

            def glu(ph):
                def f(n, b, k):
                    c.at(ev_a, n + 1)
                    ve.tensor_tensor(cin[:, ds(n, 1), CF_TAPS - 1:CF_TAPS - 1 + T], b2(b)[:, 0:1, :],
                                     ev[:, 0, 0:T].rearrange("p (a b) -> p a b", a=1), ALU.mult).then_inc(block_free, 1)
                return f

            def resid(gate=None, squares=False):
                def make(ph):
                    def f(n, b, k):
                        onto(n, b)
                        if squares and not (isinstance(n, int) and n == 0):
                            c.at(res_sq, n)
                            chain(ve.tensor_tensor(stat[:, 1, :], stat[:, 1, :], ev[:, (k - 1) % 2, :], ALU.add))

                    def onto(n, b):
                        done(ph, n)
                        if gate is None:
                            ve.tensor_tensor(h[:, ds(n * 2, 2), :], b2(b), h[:, ds(n * 2, 2), :], ALU.add).then_inc(block_free, 1)
                        else:
                            for hf in range(2):
                                o = h[:, ds(n * 2 + hf, 1), :]
                                ins = ve.scalar_tensor_tensor(o, b2(b)[:, hf:hf + 1, :], modt[:, ds(n * 2 + (gate + hf), 1)], o,
                                                              ALU.mult, ALU.add)
                            ins.then_inc(block_free, 1)
                    return f
                return make

            def relu2(ph):
                def f(n, b, k):
                    c.at(ev_a, n + 1)
                    o = hid[:, 0, ds(n * 2, 2), :]
                    ve.tensor_tensor(hid[:, 1, ds(n * 2, 2), :], ev[:, 1, :].rearrange("p (a b) -> p a b", a=2), o.bitcast(F32),
                                     ALU.subtract).then_inc(ev_v, 1)
                return f

            def gated(first):
                def make(ph):
                    def f(n, b, k):
                        c.at(ev_a, n * 2 + 1)
                        for j, so, do in ((0, slice(0, T - 1), slice(1, T)), (2, slice(1, T), slice(0, T - 1))):
                            for hf in range(2):
                                o = ev[:, 0, hf * T + do.start:hf * T + do.stop]
                                ins = ve.scalar_tensor_tensor(o, b2(b)[:, hf, so], par("ff_conv", n * 6 + (6 * first + 3 * hf + j)), o,
                                                              ALU.mult, ALU.add)
                                if j == 2 and hf:
                                    ins.then_inc(block_free, 1)
                                else:
                                    ins.then_inc(dve_step, 1)
                                    chain.n += 1
                            if j == 0:
                                ve.wait_ge(dve_step, chain.i * chain.per + chain.n)
                        c.at(ev_a, n * 2 + 2)
                        chain(ve.tensor_tensor(ev[:, 1, T:2 * T], ev[:, 1, 0:T], ev[:, 0, T:2 * T], ALU.mult))
                        t = ev[:, 1:2, T:2 * T]
                        chain(ve.tensor_copy(hid[:, 0, ds(n, 1), :], t))
                        ve.tensor_tensor(hid[:, 1, ds(n, 1), :], t, hid[:, 0, ds(n, 1), :].bitcast(F32), ALU.subtract).then_inc(ev_v, 1)
                    return f
                return make

            def phase(name, evac, links=0, extra=None):
                ph = PH[name]
                over(ve, ph, slot, evac(ph), chain, links + (MOD_K // 2 if ph.mod else 0), extra)

            def residual(name, gate=None, extra=None):
                ph = PH[name]
                chain(ve.memset(stat[:, 1, :], 0.0))
                phase(name, resid(gate, True), ph.K, extra)
                c.at(res_sq, ph.nblocks)
                ve.tensor_tensor(stat[:, 1, :], stat[:, 1, :], ev[:, 1, :], ALU.add).then_inc(res_sum, 1)
                c.end(res_sq, ph.nblocks)

            def h_norm(at):
                def f(i, j):
                    if isinstance(i, int) and j == at:
                        c.at(h_sums, 1)
                        ve.tensor_scalar(small[:, H_ROOT:H_ROOT + TT], bank[4][:, 0:TT], 1.0 / D, EPS, ALU.mult, ALU.add).then_inc(h_var, 1)
                    if isinstance(i, int) and j == at + 2:
                        c.at(h_std, 1)
                        ve.reciprocal(small[:, H_ROOT:H_ROOT + TT], small[:, H_ROOT:H_ROOT + TT]).then_inc(h_root, 1)
                        c.end(h_sums, 1)
                        c.end(h_std, 1)
                return f

            def norm(src, gain, chunks=DC, c0=0, shift=None, into=None, ahead=False, b=3):
                if not ahead:
                    c.at(sums, 1)
                    ve.tensor_scalar(small[:, ROOT:ROOT + TT], bank[b][:, 0:TT], 1.0 / (chunks * P), EPS, ALU.mult, ALU.add).then_inc(var, 1)
                    c.at(std, 1)
                    ve.reciprocal(small[:, ROOT:ROOT + TT], small[:, ROOT:ROOT + TT]).then_inc(root, 1)
                    c.end(sums, 1)
                    c.end(std, 1)
                c.at(spread, 1)
                c.end(spread, 1)
                factor = bank[4 if ahead else b][:, T:2 * T]
                dst = tmp if into is None else into

                def lower(q):
                    c.at(norm_hi, q + 1)
                    if shift is None:
                        ks = slice(4 * q, 4 * q + 4)
                        ins = ve.tensor_tensor(act[:, 1, c0 + 4 * q:c0 + 4 * q + 4, :], tmp[:, ks, :],
                                               act[:, 0, c0 + 4 * q:c0 + 4 * q + 4, :].bitcast(F32), ALU.subtract)
                    else:
                        for k in range(4 * q, 4 * q + 4):
                            ins = ve.scalar_tensor_tensor(act[:, 1, k, :], tmp[:, k, :], modt[:, shift + k:shift + k + 1],
                                                          act[:, 0, k, :].bitcast(F32), ALU.add, ALU.subtract)
                    ins.then_inc(act_ready, 1)

                for q in range(chunks // 4):
                    for k in range(4 * q, 4 * q + 4):
                        ins = ve.scalar_tensor_tensor(dst[:, k, :], src[:, k, :], gain(k), factor, ALU.mult, ALU.mult)
                    if into is None:
                        ins.then_inc(normed, 1)
                        if q:
                            lower(q - 1)
                if into is None:
                    lower(chunks // 4 - 1)
                    c.end(norm_hi, chunks // 4)
                return ins

            def g(name):
                return lambda k: par(name, k)

            ve.wait_ge(params_in, 64)
            ve.wait_ge(mod_ready, 1)
            ve.wait_ge(src_in, 16)
            norm(h, g("norm_mix"))
            conv_x, conv_w, conv4_w = modraw[:, 0, 0:T + CF_TAPS - 1], modraw[:, 1, 0:CF_TAPS + 1], modraw[:, 1, 64:64 + 8 * 4]
            conv_mark = {}

            def conv31(ph, i0, stage=False):
                def f(i, j):
                    if stage and j == LAG:
                        chain(ve.tensor_copy(conv4_w, par("dn_conv", i * 8 * ph.K, 8 * ph.K)))
                    chunk = i + i0
                    if isinstance(chunk, int) and chunk < 0:
                        if j == ph.S - 1:
                            c.at(gate_pe, 1)
                        return
                    if j == 0:
                        ve.wait_ge(block_free, chunk + (FREE + 1))
                        ve.tensor_copy(conv_x.rearrange("p (a b) -> p a b", a=1), cin[:, ds(chunk, 1), :])
                        ve.tensor_copy(conv_w[:, 0:CF_TAPS], par("cf_conv", chunk * CF_TAPS, CF_TAPS))
                        chain(ve.tensor_copy(conv_w[:, CF_TAPS:], par("cf_b", chunk)))
                    for t in range(j * CF_TAPS // ph.S, (j + 1) * CF_TAPS // ph.S):
                        acc, x_, w = modacc[:, t % 2, 0:T], conv_x[:, t:t + T], conv_w[:, t:t + 1]
                        if t >= 2:
                            ve.wait_ge(dve_step, conv_mark[t - 2])
                        if t == 0:
                            ins = ve.tensor_scalar(acc, x_, w, conv_w[:, CF_TAPS:], ALU.mult, ALU.add)
                        elif t == 1:
                            ins = ve.tensor_scalar(acc, x_, w, None, ALU.mult)
                        else:
                            ins = ve.scalar_tensor_tensor(acc, x_, w, acc, ALU.mult, ALU.add)
                        chain.tick(ins)
                        conv_mark[t] = chain.now()
                    if j == ph.S - 1:
                        ve.wait_ge(dve_step, conv_mark[CF_TAPS - 1])
                        chain(ve.tensor_tensor(tmp[:, ds(chunk, 1), :], modacc[:, 0:1, 0:T], modacc[:, 1:2, 0:T], ALU.add))
                return f
            CONV_LINKS = 1 + CF_TAPS + 1
            before_qkv = PH["glu"].iters - 1
            phase("glu", glu, CONV_LINKS, conv31(PH["glu"], -1))
            c.end(ev_a, 8)
            phase("qkv", conv4, PH["qkv"].K * 5 + 1 + CONV_LINKS, conv31(PH["qkv"], before_qkv, stage=True))
            c.end(ev_a, 12)
            phase("z", nothing, CONV_LINKS, conv31(PH["z"], before_qkv + PH["qkv"].iters))
            assert before_qkv + PH["qkv"].iters + PH["z"].iters == 8

            ve.memset(small[:, 125:126], 0.0).then_inc(cf_dve, 1)
            for mt in range(TT):
                ins = ve.tensor_tensor(gt[:, A1, 8 * mt:8 * mt + 8], bank[3][:, 16 * mt + 8:16 * mt + 16], par("dt", 0, 8), ALU.add)
            ins.then_inc(gate_dve, 1)
            c.at(gate_act, 1)
            chain(ve.scalar_tensor_tensor(gt[:, GC, :], gt[:, A1, :], 0.0, gt[:, LN1, :], ALU.max, ALU.add))
            for mt in range(TT):
                r = slice(8 * mt, 8 * mt + 8)
                ins = ve.scalar_tensor_tensor(gt[:, G, r], gt[:, GC, r], -1.0, gt[:, EA, 0:8], ALU.mult, ALU.mult)
            ins.then_inc(gate_dve, 1)
            c.at(cf_pe, 1)
            ve.tensor_scalar(stat[:, 0, 0:T], bank[2][:, 0:T], 1.0 / D_CONV, None, ALU.mult).then_inc(cf_dve, 1)
            c.at(cf_dve, 2)
            ve.tensor_tensor(tmp[:, 0:8, :], tmp[:, 0:8, :], stat[:, 0:1, 0:T].to_broadcast([P, 8, T]), ALU.subtract).then_inc(cf_dve, 1)
            c.at(cf_dve, 3)
            c.at(l2_pe, 8)
            c.at(cf_pe, 2)
            ve.tensor_scalar(small[:, L2:L2 + 32], bank[4][:, 0:32], 1.0, EPS, ALU.mult, ALU.add)
            ve.tensor_scalar(small[:, L2 + 32:L2 + 34], bank[4][:, 32:34], 1.0 / D_CONV, EPS, ALU.mult, ALU.add).then_inc(l2_dve, 1)
            c.at(l2_act, 1)
            ve.reciprocal(small[:, L2:L2 + 34], small[:, L2:L2 + 34]).then_inc(l2_dve, 1)
            c.at(gate_act, 2)
            ve.tensor_tensor(gt[:, BEG, :], gt[:, BETA, :], gt[:, EGC, :], ALU.mult)
            for p in range(8):
                c.at(l2_pe, 8 + p + 1)
                o = qkvT[:, 2 * p:2 * p + 2, :]
                ve.scalar_tensor_tensor(o, o, float(P) ** -0.5 if p < 4 else 1.0, b2(4 + p % 4), ALU.mult, ALU.mult).then_inc(l2_dve, 1)
            c.at(cf_pe, 3)
            for q in range(2):
                for k in range(4 * q, 4 * q + 4):
                    ins = ve.scalar_tensor_tensor(tmp[:, k, :], tmp[:, k, :], par("ln_g", k), bank[2][:, 0:T], ALU.mult, ALU.mult)
                ins.then_inc(cf_dve, 1)
            for q in range(2):
                c.at(cf_act, 2 + q)
                ve.tensor_tensor(act[:, 1, 8 + 4 * q:12 + 4 * q, :], tmp[:, 8 + 4 * q:12 + 4 * q, :],
                                 act[:, 0, 8 + 4 * q:12 + 4 * q, :].bitcast(F32), ALU.subtract).then_inc(act_ready, 1)
            ve.memset(small[:, 127:128], 0.0).then_inc(cf_dve, 1)

            c.at(cf_dve, 6)
            c.at(l2_dve, 2 + 8)

            def every(t):
                return t.rearrange("p (a b) -> p a b", a=1).to_broadcast([P, 4, P])
            for ch in CHUNKS:
                tok = slice(ch * P, (ch + 1) * P)

                def p_(hg, name):
                    c.at(dl_pe[hg], step(PE_SIG, ch, name))

                def a(hg, name):
                    c.at(dl_act[hg], step(ACT_SIG, ch, name))

                def mine(hg, name):
                    c.at(dl_dve[hg], step(DVE_SIG, ch, name))
                for hg in GROUPS:
                    if ch:
                        c.at(dl_act[hg], step(ACT_SIG, ch - 1, "oc"))
                        a(hg, "eg")
                    p_(hg, "bc")
                    ve.tensor_tensor(DT[hg], bk(hg, 0), every(cc(CM, "below")), ALU.add).then_inc(dl_dve[hg], 1)
                    if not ch:
                        ve.tensor_tensor(gt[:, KDL, 4 * hg:4 * hg + 4], bk(hg, 0)[:, :, P - 1], gtc(GC, ch, 4 * hg, 4),
                                         ALU.subtract).then_inc(dl_dve[hg], 1)
                    if ch:
                        ve.tensor_tensor(QDT[hg], qkvT[:, 4 * hg:4 * hg + 4, tok], EG[hg], ALU.mult)
                    ve.tensor_tensor(KBT[hg], qkvT[:, 8 + 4 * hg:12 + 4 * hg, tok], bk(hg, 1), ALU.mult).then_inc(dl_dve[hg], 1)
                for hg in GROUPS:
                    p_(hg, "tr")
                    for n in range(4):
                        ins = ve.tensor_scalar(VB[hg][:, n, :], bk(hg, 3)[:, n, :], gtc(BETA, ch, 4 * hg + n), None, ALU.mult)
                    ins.then_inc(dl_dve[hg], 1)
                    p_(hg, "aa")
                    a(hg, "dtx")
                    ve.tensor_copy(X[hg], every(ident[:, :]))
                    ve.tensor_copy(XT[hg], every(ident[:, :]))
                    ve.tensor_tensor(AT[hg], bk(hg, 0), DT[hg], ALU.mult)
                    ve.tensor_tensor(ATT[hg], bk(hg, 1), DT[hg], ALU.mult).then_inc(dl_dve[hg], 1)
                    mine(hg, "aat")

                def masked(hg, lv):
                    ve.tensor_tensor(MT[hg], AT[hg], every(cc(CM, "levels")[:, lv * P:(lv + 1) * P]), ALU.mult).then_inc(dl_dve[hg], 1)
                for hg in GROUPS:
                    masked(hg, 0)
                for lv in range(LEVELS):
                    if lv + 1 < LEVELS:
                        for hg in GROUPS:
                            p_(hg, f"y{lv}")
                            masked(hg, lv + 1)
                    for hg in GROUPS:
                        p_(hg, f"z{lv}")
                        if lv:
                            mine(hg, f"x{lv - 1}")
                        if lv + 1 < LEVELS:
                            ve.tensor_tensor(X[hg], X[hg], bk(hg, 2), ALU.subtract)
                        ve.tensor_tensor(XT[hg], XT[hg], bk(hg, 3), ALU.subtract).then_inc(dl_dve[hg], 1)
                if ch:
                    for hg in GROUPS:
                        p_(hg, "ws")
                        ve.tensor_tensor(VN[hg], U_[hg], bk(hg, 0), ALU.subtract).then_inc(dl_dve[hg], 1)
            c.at(on_pe, 1)
            ve.tensor_scalar(small[:, ON:ON + 16], bank[4][:, 0:16], 1.0 / P, EPS, ALU.mult, ALU.add).then_inc(on_dve, 1)
            c.at(on_act, 2 + 1)
            ve.reciprocal(small[:, ON:ON + 16], small[:, ON:ON + 16]).then_inc(on_dve, 1)
            for p in range(5):
                if p < 4:
                    c.at(on_pe, p + 2)
                    o = qkvT[:, 16 + 2 * p:18 + 2 * p, :]
                    chain(ve.scalar_tensor_tensor(o, o, par("dn_norm"), b2(4 + p), ALU.mult, ALU.mult))
                    ve.tensor_tensor(o, o, zT[:, 2 * p:2 * p + 2, :], ALU.mult).then_inc(on_dve, 1)
                if p:
                    c.at(on_act, 3 + p)
                    ve.tensor_tensor(act[:, 1, 2 * p - 2:2 * p, :], qkvT[:, 14 + 2 * p:16 + 2 * p, :],
                                     act[:, 0, 2 * p - 2:2 * p, :].bitcast(F32), ALU.subtract).then_inc(act_ready, 1)
            ve.memset(small[:, 121:122], 0.0).then_inc(mod_used, MOD_N)
            ve.memset(small[:, 126:127], 0.0).then_inc(mixed, 1)
            def memory_sums(i, j):
                if isinstance(i, int) and j == PH["wout"].S - 1:
                    for q in range(4):
                        c.at(mem_sq, q + 1)
                        ins = ve.tensor_reduce(memK[:, q, :],
                                               tmp[:, 4 * q:4 * q + 4, :].rearrange("p k t -> p t k"), AX.X, ALU.add)
                    ins.then_inc(mem_sum, 1)
            residual("wout", extra=memory_sums)

            norm(memory, g("norm_mem"))
            phase("memk", nothing, 0, h_norm(4))
            phase("memv", nothing)
            norm(h, g("norm_xa"), ahead=True)
            phase("wq", nothing)

            def attention(kind, c0=0):
                units = attention_units(kind)
                nk = key_tiles(kind) * P
                scale = {"cross": XA_SCALE, "mla": MLA_SCALE, "na": 1.0}[kind]
                for u in range(len(units) + 2):
                    if u < len(units):
                        hd, mt = units[u]
                        pb = stat[:, u % 2, 0:nk]
                        b = bank[3 + u % 2]
                        m = SM + 4 * (u % 2)
                        c.at(scores, u + 1)
                        if u >= 2:
                            c.at(probs_t, u - 1)
                        src = b[:, 0:nk]
                        if kind == "na":
                            ve.scalar_tensor_tensor(pb[:, 0:T], b[:, 0:T], NA_SCALE, bias[:, hd, mt, :], ALU.mult, ALU.add)
                            chain(ve.tensor_scalar(pb[:, T:2 * T], b[:, T:2 * T], NA_SCALE, None, ALU.mult))
                            src = pb
                        chain(ve.tensor_reduce(small[:, m:m + 1], src, AX.X, ALU.max))
                        ve.tensor_scalar(small[:, m + 1:m + 2], small[:, m:m + 1], -scale, None, ALU.mult).then_inc(maxes, 1)
                        c.at(exps, u + 1)
                        chain(ve.reciprocal(small[:, m + 3:m + 4], small[:, m + 2:m + 3]))
                        ve.tensor_scalar(pb, pb, small[:, m + 3:m + 4], None, ALU.mult).then_inc(probs, 1)
                    if u >= 3 and u % 2 == 1:
                        hd = (u - 3) // 2
                        c.at(head_hi, hd + 1)
                        if kind == "cross":
                            for k in range(2):
                                ks = slice(XA_CH * hd + 2 * k, XA_CH * hd + 2 * k + 2)
                                ins = ve.tensor_tensor(act[:, 1, ks, :], b2(k), act[:, 0, ks, :].bitcast(F32), ALU.subtract)
                        else:
                            ins = ve.tensor_tensor(act[:, 1, c0 + hd, :], bank[0][:, 0:T], act[:, 0, c0 + hd, :].bitcast(F32),
                                                   ALU.subtract)
                        ins.then_inc(act_ready, 1)
                for s_ in (scores, exps, probs_t):
                    c.end(s_, len(units))
                c.end(head_hi, len(units) // 2)

            attention("cross")
            residual("wo")

            norm(h, g("norm_mlp"))
            for r in range(FF1_ROUNDS):
                phase(f"w1_{r}", relu2)
                c.end(ev_a, PH["w1_0"].nblocks)
                if r == FF1_ROUNDS - 1:
                    residual(f"w2_{r}")
                else:
                    phase(f"w2_{r}", resid())
            chain(mod_store(MOD_BODIES, 1))
            for w, to_, n in ((0, 0, 96), (1, 96, 32)):
                parts = msum[:, w, 0:2 * n].rearrange("p (a b c) -> p a b c", b=2, c=16)
                modt_ = modt[:, to_:to_ + n].rearrange("p (a c) -> p a c", c=16)
                b_ = par("b_mod", 0, n).rearrange("p (a c) -> p a c", c=16)
                chain(ve.tensor_tensor(modt_, parts[:, :, 0, :], b_, ALU.add))
                chain(ve.tensor_tensor(modt_, modt_, parts[:, :, 1, :], ALU.add))
            for to_, sc_at, name in ((GAIN_X, 16, "g_attn"), (GAIN_C, 112, "g_attn"), (GAIN_F, 64, "g_ffn")):
                chain(ve.scalar_tensor_tensor(small[:, to_:to_ + DC], modt[:, sc_at:sc_at + DC], 1.0, par(name, 0, DC), ALU.add, ALU.mult))

            def gs(at):
                return lambda k: small[:, at + k:at + k + 1]
            chain(norm(h, g("norm_final"), into=h, b=5))
            norm(kN[:, :, :, :].rearrange("p a b t -> p (a b) t"), gs(GAIN_C), shift=96)
            for name in ("ckv_c", "nak_c", "nav_c", "kr_c"):
                phase(name, nothing)
            norm(h, gs(GAIN_X), shift=0)
            for name in ("ckv_x", "nak_x", "nav_x", "cq", "naq", "fn", "kr_x"):
                phase(name, nothing)
            ve.wait_ge(bias_in, 32)
            for hd in range(NA_H):
                chain(ve.tensor_tensor(bias[:, hd, :, :], bias[:, hd, :, :], mask[:, :, :], ALU.add))
            attention("na", 8)
            for gg in range(FN_G):
                c.at(head_hi, gg + 1)
                ve.tensor_tensor(act[:, 1, 12 + gg, :], bank[0][:, 0:T], act[:, 0, 12 + gg, :].bitcast(F32), ALU.subtract).then_inc(act_ready, 1)
            c.end(head_hi, FN_G)
            norm(ckv[:, 1, :, :], g("g_kv"), LC)
            phase("kn_c", nothing)
            phase("v_c", nothing)
            norm(ckv[:, 0, :, :], g("g_kv"), LC, 4)
            phase("kn_x", nothing)
            phase("v_x", nothing)
            norm(cq, g("g_q"), LC)
            phase("qn", nothing)
            phase("qr", nothing)
            ve.wait_ge(block_free, FREE + PH["qr"].block0 + PH["qr"].nblocks)
            for n in range(1 + MLA_H // 2):
                x_ = kr[:, 0, :] if n == 0 else qR[:, n - 1, :]
                c.at(rope_pe, n + 1)
                if n:
                    c.at(rope_dve, n)
                ve.tensor_tensor(stat[:, 0, 0:T], x_, cc(CA, "cos"), ALU.mult)
                chain(ve.tensor_tensor(stat[:, 1, 0:T], bank[3 + n][:, 0:T], cc(CA, "sin"), ALU.mult))
                ve.tensor_tensor(x_, stat[:, 0, 0:T], stat[:, 1, 0:T], ALU.add).then_inc(rope_dve, 1)
            attention("mla")
            residual("wout2", 32)
            norm(h, gs(GAIN_F), shift=48)
            first = 0
            for r, n in enumerate(FF2_ROUNDS):
                phase(f"up_{r}", gated(first), 2 * 5)
                c.end(ev_a, 2 * n)
                first += n
                if r == len(FF2_ROUNDS) - 1:
                    residual(f"down_{r}", 80)
                else:
                    phase(f"down_{r}", resid(80))
            norm(h, g("g_final"), into=tmp).then_inc(out_ready, 1)


def slots_of(w, ph, cols=None):
    if cols is not None:
        w = np.concatenate([w[:, a:b] for a, b in cols], axis=1)
    n = ph.nblocks * ph.ncol
    assert w.shape == (ph.chunks * P, n), (ph.name, w.shape)
    w = w.reshape(ph.slots_per_block, ph.per_slot, P, ph.nblocks, ph.ncol)
    return w.transpose(3, 0, 2, 1, 4).reshape(ph.slots, P, SLOT)


def per_partition(v):
    return np.ascontiguousarray(v).reshape(-1, P).T


def feature_major(x):
    return x.reshape(T, -1, P).transpose(2, 1, 0).reshape(P, -1)


def kernel(**a):
    import concourse.bacc as bacc
    from concourse.bass_utils import run_bass_kernel_spmd

    a = {k: np.asarray(v) for k, v in a.items()}
    w_in, w_in2 = a["w_in"][0], a["w_in_2"][0]
    parts = {}
    parts["qkv"] = slots_of(w_in[:, 0:3072], PH["qkv"])
    parts["z"] = slots_of(w_in[:, 3072:4096], PH["z"])
    w_ba = w_in[:, 4096:4112]
    g0 = 4112
    parts["glu"] = slots_of(w_in, PH["glu"], [c for i in range(8) for c in (
        (g0 + P * i, g0 + P * (i + 1)), (g0 + 1024 + P * i, g0 + 1024 + P * (i + 1)))])
    parts["wout"] = slots_of(a["w_out"][0], PH["wout"])
    parts["memk"] = slots_of(a["xa_wk"][0], PH["memk"])
    parts["memv"] = slots_of(a["xa_wv"][0], PH["memv"])
    parts["wq"] = slots_of(a["xa_wq"][0], PH["wq"])
    parts["wo"] = slots_of(a["xa_wo"][0], PH["wo"])
    for r in range(FF1_ROUNDS):
        parts[f"w1_{r}"] = slots_of(a["mlp_w1"][0][:, D * r:D * (r + 1)], PH[f"w1_{r}"])
        parts[f"w2_{r}"] = slots_of(a["mlp_w2"][0][D * r:D * (r + 1), :], PH[f"w2_{r}"])
    at = {}
    o = 0
    for name, n in (("cq", LAT), ("ckv", LAT), ("kr", ROPE), ("naq", 512), ("nak", 512), ("nav", 512), ("fn", 512)):
        at[name] = (o, o + n)
        o += n
    for name in ("ckv", "nak", "nav"):
        for who in "cx":
            parts[f"{name}_{who}"] = slots_of(w_in2, PH[f"{name}_{who}"], [at[name]])
    for who in "cx":
        parts[f"kr_{who}"] = slots_of(w_in2, PH[f"kr_{who}"], [at["kr"], at["kr"]])
    for name in ("cq", "naq", "fn"):
        parts[name] = slots_of(w_in2, PH[name], [at[name]])
    ukv, uq = a["w_ukv_2"][0], a["w_uq_2"][0]
    for who in "cx":
        parts[f"kn_{who}"] = slots_of(ukv, PH[f"kn_{who}"], [(256 * i, 256 * i + 128) for i in range(MLA_H)])
        parts[f"v_{who}"] = slots_of(ukv, PH[f"v_{who}"], [(256 * i + 128, 256 * i + 256) for i in range(MLA_H)])
    parts["qn"] = slots_of(uq, PH["qn"], [(192 * i, 192 * i + 128) for i in range(MLA_H)])
    parts["qr"] = slots_of(uq, PH["qr"], [(192 * i + 128, 192 * i + 192) for i in range(MLA_H)])
    parts["wout2"] = slots_of(a["w_out_2"][0], PH["wout2"])
    first = 0
    for r, n in enumerate(FF2_ROUNDS):
        parts[f"up_{r}"] = slots_of(a["w_up_2"][0], PH[f"up_{r}"], [c for i in range(first, first + n) for c in (
            (P * i, P * (i + 1)), (D_FF2 + P * i, D_FF2 + P * (i + 1)))])
        parts[f"down_{r}"] = slots_of(a["w_down_2"][0][P * first:P * (first + n)], PH[f"down_{r}"])
        first += n
    stream = np.empty((N_SLOTS, P, SLOT), np.float32)
    for name, ph in PH.items():
        stream[ph.slot0:ph.slot0 + ph.slots] = parts.pop(name)
    mods = a["w_mod_2"][0].reshape(2, MOD_K // 2, 2, P, -1, MOD_COL).transpose(0, 4, 1, 3, 2, 5)
    mods = np.stack([mods[half, blk] for half, blk in MOD_ORDER]).reshape(-1, P, SLOT)

    def paired(v):
        v = v.reshape(v.shape[:-1] + (2, D_FF2 // P, P))
        return v.swapaxes(-3, -2).reshape(v.shape[:-3] + (88, P))

    vec = {
        "norm_mix": per_partition(a["norm_mix_g"]), "norm_mem": per_partition(a["norm_mem_g"]),
        "norm_xa": per_partition(a["norm_xa_g"]), "norm_mlp": per_partition(a["norm_mlp_g"]),
        "norm_final": per_partition(a["norm_final_g"]), "g_attn": per_partition(a["g_attn_2"]),
        "g_ffn": per_partition(a["g_ffn_2"]), "g_final": per_partition(a["g_final_2"]),
        "g_q": per_partition(a["g_q_2"]), "g_kv": per_partition(a["g_kv_2"]), "dn_norm": per_partition(a["dn_norm_g"]),
        "cf_b": per_partition(a["cf_dw_b"]), "ln_g": per_partition(a["cf_ln_g"]), "ln_b": per_partition(a["cf_ln_b"]),
        "dn_conv": a["dn_conv_w"][0].reshape(DN_TAPS, 24, P).transpose(2, 1, 0).reshape(P, -1),
        "cf_conv": a["cf_dw_w"][0].reshape(CF_TAPS, 8, P).transpose(2, 1, 0).reshape(P, -1),
        "ff_conv": paired(a["conv_w_2"][0]).transpose(2, 1, 0).reshape(P, -1),
        "ff_b": paired(a["conv_b_2"][0]).T, "b_mod": per_partition(a["b_mod_2"]),
        "c": per_partition(a["c_2"]), "c_ctx": per_partition(a["c_ctx_2"]),
        "a_log": np.broadcast_to(a["dn_a_log"][0], (P, 8)), "dt": np.broadcast_to(a["dn_dt_bias"][0], (P, 8)),
    }
    pvec = np.concatenate([vec[name] for name in PV], axis=1)
    eye = np.concatenate([np.eye(P), np.ones((P, P))], axis=1).astype(np.float32)
    i, j = np.arange(P)[:, None], np.arange(P)[None, :]
    levels = [((i // (2 * s) == j // (2 * s)) & (i % (2 * s) < s) & (j % (2 * s) >= s)).astype(np.float32) for s in (1, 2, 4, 8, 16, 32, 64)]
    upper = (i <= j).astype(np.float32)
    below = np.where(i <= j, 0.0, NEG).astype(np.float32)
    cmix = np.concatenate(levels + [upper, below, w_ba.reshape(DC, P, 16).transpose(1, 0, 2).reshape(P, -1)], axis=1)
    ang = 2 * np.pi * ((i * j) % P) / P
    dft_ch = np.concatenate([np.cos(ang), np.sin(ang)], axis=1)
    tt = np.arange(T)
    ang = 2 * np.pi * ((tt[:, None] * tt[None, :]) % T) / T

    def rows(m):
        return m.reshape(TT, P, T).transpose(1, 0, 2).reshape(P, -1)
    freqs = np.float32(10000.0) ** (-np.arange(16, dtype=np.float32) / 16)
    f = np.arange(P) % ROPE
    pos = np.where(f[:, None] < 32, tt[None, :] // GRID_W, tt[None, :] % GRID_W).astype(np.float32)
    angle = pos * freqs[f % 16][:, None]
    sign = np.where(f % 32 < 16, -1.0, 1.0)[:, None]
    swap = (i == (j ^ 16)).astype(np.float32)
    catt = np.concatenate([dft_ch, rows(np.cos(ang)), rows(-np.sin(ang)), np.cos(angle), sign * np.sin(angle), swap,
                           ], axis=1).astype(np.float32)
    catt = np.concatenate([catt, a["w_fnet_2"][0].transpose(1, 0, 2).reshape(P, -1)], axis=1)
    qr_, qw, kr_, kw = tt[:, None] // GRID_W, tt[:, None] % GRID_W, tt[None, :] // GRID_W, tt[None, :] % GRID_W
    start = np.clip(qw - NA_KW // 2, 0, GRID_W - NA_KW)
    inside = (kw >= start) & (kw < start + NA_KW)
    rel_col = np.clip(kw - qw + NA_KW - 1, 0, 2 * NA_KW - 2)
    table = a["na_rpb_2"][0][:, kr_ - qr_ + NA_KH - 1, rel_col]
    na_bias = table.reshape(NA_H, TT, P, T).transpose(2, 0, 1, 3).reshape(P, -1)
    na_mask = np.where(inside, 0.0, NEG).astype(np.float32).reshape(TT, P, T).transpose(1, 0, 2).reshape(P, -1)

    arrays = {
        "x_t": feature_major(a["x"][0]).reshape(P, DC, T), "mem_t": feature_major(a["mem"][0]), "ctx_t": feature_major(a["ctx_2"][0]),
        "stream": stream, "mods": mods, "pvec": pvec, "eye": eye, "cmix": cmix, "catt": catt, "na_bias": na_bias, "na_mask": na_mask,
    }
    nc = bacc.Bacc("TRN2", target_bir_lowering=False, num_devices=1)
    args = []
    for name, v in arrays.items():
        arrays[name] = np.ascontiguousarray(v)
        args.append(nc.dram_tensor(name, v.shape, mybir.dt.from_np(v.dtype), kind="ExternalInput").ap())
    args.append(nc.dram_tensor("out_t", (P, DC, T), F32, kind="ExternalOutput").ap())
    build(nc, *args)
    got = run_bass_kernel_spmd(nc, [arrays], core_ids=[0]).results[0]["out_t"]
    return got.transpose(2, 1, 0).reshape(1, T, D)
```

```python
import numpy as np
from contextlib import ExitStack

import concourse.bass as bass
from concourse import mybir
from concourse.alu_op_type import AluOpType as ALU

F32 = mybir.dt.float32
F32R = mybir.dt.float32r
ACT = mybir.ActivationFunctionType
AX = mybir.AxisListType
ds = bass.ds

P = 128
D = 2048
T = 256
DC = D // P
TT = T // P
EPS = 1e-6
D_DELTA, D_CONV = 1024, 1024
DN_H, DN_TAPS, CF_TAPS = 8, 4, 31
XA_H = 4
XA_CH = DC // XA_H
XA_SCALE = float(512) ** -0.5
D_FF1, D_FF2 = 8192, 5632
MLA_H, NOPE, ROPE, LAT = 8, 128, 64, 512
LC = LAT // P
MLA_SCALE = float(NOPE + ROPE) ** -0.5
NA_H, NA_KH, NA_KW, GRID_W = 4, 8, 16, 64
NA_SCALE = float(P) ** -0.5
FN_G = 4
FN_SCALE = float(T * P) ** -0.5
NEG = -1e30

SLOT = 1024
RAW_N, SPL_N, MOD_N = 8, 4, 2
NCOL = 256
LAG = 3


class Phase:

    def __init__(self, name, nblocks, chunks, per_body=2, per_slot=4, ncol=NCOL, flip=False, mod=0):
        self.name, self.nblocks, self.chunks, self.flip, self.mod = name, nblocks, chunks, flip, mod
        self.K, self.per_slot, self.ncol = per_body, per_slot, ncol
        self.iters = nblocks // per_body
        self.slots_per_block = -(-chunks // per_slot)
        self.S = self.slots_per_block * per_body
        self.slots = self.slots_per_block * nblocks


FF1_ROUNDS = 4
FF2_ROUNDS = (16, 16, 12)


def phases():
    out = [
        Phase("glu", 8, DC), Phase("qkv", 12, DC, per_body=4), Phase("z_0", 2, DC), Phase("z_1", 2, DC),
        Phase("wout", 8, DC),
        Phase("memk", 8, DC, per_body=4, mod=2), Phase("memv", 8, DC, per_body=4, flip=True, mod=2),
        Phase("wq", 8, DC, per_body=4, mod=2), Phase("wo", 8, DC, per_body=4, mod=2),
    ]
    for r in range(FF1_ROUNDS):
        out += [Phase(f"w1_{r}", 8, DC, per_body=4, mod=1), Phase(f"w2_{r}", 8, DC, per_body=4, mod=1)]
    for who in ("c", "x"):
        out += [Phase("ckv_" + who, 2, DC), Phase("nak_" + who, 2, DC), Phase("nav_" + who, 2, DC, flip=True)]
        if who == "x":
            out += [Phase("cq", 2, DC), Phase("naq", 2, DC), Phase("fn", 2, DC)]
        out += [Phase("kr_" + who, 1, DC, per_body=1, per_slot=8, ncol=P)]
    for who in ("c", "x"):
        out += [Phase("kn_" + who, 4, LC, per_body=4), Phase("v_" + who, 4, LC, per_body=4, flip=True)]
    out += [Phase("qn", 4, LC, per_body=4), Phase("qr", 2, LC, per_body=2)]
    out += [Phase("wout2", 8, DC)]
    for r, n in enumerate(FF2_ROUNDS):
        out += [Phase(f"up_{r}", n, DC, per_body=2 if n % 2 == 0 else 1)]
        out += [Phase(f"down_{r}", 8, n, per_body=2 if n == 16 else 8)]
    slot = block = mod = 0
    for ph in out:
        ph.slot0, ph.block0 = slot, block
        ph.mod0 = mod
        if ph.mod:
            assert (ph.mod == 2) == (mod < MOD_CTX) and ph.S == 2 * RAW_N
        slot += ph.slots
        block += ph.nblocks
        mod += ph.iters if ph.mod else 0
        assert ph.iters == 1 or (ph.S % RAW_N == 0 and ph.K % 2 == 0), ph.name
    return {ph.name: ph for ph in out}, slot


MOD_COL = 512
MOD_BODIES = 24
MOD_CTX = 8
MOD_AT = ((0, 1), (2,), (3,), (4,), (5,), (6,), (7,), (8, 9), (10,), (11,), (12,), (13,), (14,), (15,))
MOD_OUT_AT = 12
PRE = 3
PH, N_SLOTS = phases()


def columns(parts):
    at, out = 0, {}
    for name, n in parts:
        out[name] = (at, at + n)
        at += n
    return out, at


PV, N_PV = columns([
    ("norm_mix", DC), ("norm_mem", DC), ("norm_xa", DC), ("norm_mlp", DC), ("norm_final", DC),
    ("g_attn", DC), ("g_ffn", DC), ("g_final", DC), ("g_q", LC), ("g_kv", LC), ("dn_norm", 1),
    ("cf_b", 8), ("ln_g", 8), ("ln_b", 8), ("dn_conv", 24 * DN_TAPS), ("cf_conv", 8 * CF_TAPS),
    ("ff_conv", 88 * 3), ("ff_b", 88), ("b_mod", 96), ("c", DC), ("c_ctx", DC), ("a_log", 8), ("dt", 8),
])
CM, N_CM = columns([
    ("levels", 7 * P), ("upper", P), ("below", P), ("w_ba", DC * 16)])
CA, N_CA = columns([
    ("dft_ch", 2 * P), ("dft_cos", TT * T), ("dft_sin", TT * T), ("cos", T), ("sin", T), ("swap", P),
    ("w_fnet", FN_G * P)])
N_CZ = max(N_CM, N_CA)



def build(nc, x_t, mem_t, ctx_t, stream, mods, pvec, eye, cmix, catt, na_bias, na_mask, out_t):
    es = ExitStack()
    with es:
        def sb(name, shape, dt=F32, stack=None):
            return (stack or es).enter_context(nc.sbuf_tensor(name, shape, dt))

        def sem(name):
            return es.enter_context(nc.semaphore(name))

        raw = sb("raw", [P, RAW_N, SLOT])
        whi = sb("whi", [P, SPL_N, SLOT], F32R)
        wlo = sb("wlo", [P, SPL_N, SLOT], F32R)
        act = sb("act", [P, 2, DC, T], F32R)
        h = sb("h", [P, DC, T])
        tmp = sb("tmp", [P, DC, T])
        pv = sb("pv", [P, N_PV])
        cz = sb("cz", [P, N_CZ])
        ident = sb("ident", [P, P])
        ones = sb("ones", [P, P])
        stat = sb("stat", [P, 2, 512])
        modt = sb("modt", [P, P])
        msum = sb("msum", [P, 2, MOD_BODIES * 4])
        small = sb("small", [P, 256])
        gt = sb("gt", [P, 12, 16])
        ev = sb("ev", [P, 2, 512])
        with ExitStack() as first:
            modraw = sb("modraw", [P, MOD_N, SLOT], stack=first)
            modacc = sb("modacc", [P, 2, MOD_COL], stack=first)
            with ExitStack() as mixer:
                qkvT = sb("qkvT", [P, 24, T], stack=mixer)
                zT = sb("zT", [P, 8, T], stack=mixer)
                cin = sb("cin", [P, 8, T + CF_TAPS - 1], stack=mixer)
            with ExitStack() as cross:
                memK = sb("memK", [P, DC, T], stack=cross)
                memV = sb("memV", [P, TT, D], stack=cross)
            with ExitStack() as mlp:
                hid = sb("hid", [P, 2, DC, T], F32R, stack=mlp)
        with ExitStack() as second:
            cq = sb("cq", [P, LC, T], stack=second)
            ckv = sb("ckv", [P, 2, LC, T], stack=second)
            kr = sb("kr", [P, 2, T], stack=second)
            with ExitStack() as local:
                naK = sb("naK", [P, NA_H, 2, T], stack=local)
                naV = sb("naV", [P, 2, TT, NA_H * P], stack=local)
                naQ = sb("naQ", [P, NA_H, T], stack=local)
                fT = sb("fT", [P, FN_G, T], stack=local)
                bias = sb("bias", [P, NA_H, TT, T], stack=local)
                mask = sb("mask", [P, TT, T], stack=local)
            with ExitStack() as latent:
                kN = sb("kN", [P, MLA_H, 2, T], stack=latent)
                mlaV = sb("mlaV", [P, 2, TT, MLA_H * P], stack=latent)
                qR = sb("qR", [P, MLA_H // 2, T], stack=latent)
        qN = tmp[:, 8:16, :]
        context_sq = kN[:, :, :, :].rearrange("p a b t -> p (a b) t")
        memory = memV[:, :, :].rearrange("p a (b t) -> p (a b) t", t=T)

        def tiles(t, n):
            flat = t.rearrange("p a b -> p (a b)") if len(t.shape) == 3 else t
            return [flat[:, 512 * k:512 * k + 512].rearrange("p (a b) -> p a b", a=4) for k in range(n)]
        T_TMP, T_CIN, T_EV = tiles(tmp[:, :, :], 8), tiles(cin[:, :, :], 4), tiles(ev[:, :, :], 2)
        T_STAT, T_MOD = tiles(stat[:, :, :], 2), tiles(modraw[:, :, :], 4)
        X, XT, Y, MT = ([T_TMP[4 * hg + k] for hg in range(2)] for k in range(4))
        AT, ATT = ([T_CIN[2 * hg + k] for hg in range(2)] for k in range(2))
        VB, ST = T_EV, T_STAT
        KW, QDT = ([T_MOD[2 * hg + k] for hg in range(2)] for k in range(2))
        KBT, EG, DT = X, Y, MT
        U_, VN, WT = AT, MT, Y

        bank = [es.enter_context(nc.psum_tensor(f"bank{i}", [P, 512], F32)) for i in range(8)]


        def b2(k):
            return bank[k][:, :].rearrange("p (a b) -> p a b", a=2)

        def b4(k):
            return bank[k][:, :].rearrange("p (a b) -> p a b", a=4)

        def par(name, k=0, n=1):
            return pv[:, PV[name][0] + k:PV[name][0] + k + n] if isinstance(k, int) else pv[:, ds(k + PV[name][0], n)]

        def cc(table, name):
            return cz[:, table[name][0]:table[name][1]]

        raw_in = [sem(f"raw_in{k}") for k in range(RAW_N)]
        mod_in = [sem(f"mod_in{k}") for k in range(MOD_N)]
        mod_used = sem("mod_used")
        mod_out = sem("mod_out")
        hi_done = sem("hi_done")
        split_done = sem("split_done")
        slot_used = sem("slot_used")
        block_free = sem("block_free")
        ev_a = sem("ev_a")
        ev_v = sem("ev_v")
        act_step = sem("act_step")
        dve_step = sem("dve_step")
        params_in = sem("params_in")
        ones_in = sem("ones_in")
        late_in = sem("late_in")
        src_in = [sem(f"src_in{q}") for q in range(4)]
        squares = sem("squares")
        parts = sem("parts")
        sums = sem("sums")
        res_sq = sem("res_sq")
        res_sum = sem("res_sum")
        h_sums, h_var, h_std, h_root = sem("h_sums"), sem("h_var"), sem("h_std"), sem("h_root")
        h_normed, h_sq, h_sum = sem("h_normed"), sem("h_sq"), sem("h_sum")
        mem_sq, mem_sum = sem("mem_sq"), sem("mem_sum")
        var = sem("var")
        root = sem("root")
        std = sem("std")
        spread = sem("spread")
        normed = sem("normed")
        norm_hi = sem("norm_hi")
        act_ready = sem("act_ready")
        gate_pe, gate_act, gate_dve = sem("gate_pe"), sem("gate_act"), sem("gate_dve")
        l2_pe, l2_act, l2_dve, l2_sq = sem("l2_pe"), sem("l2_act"), sem("l2_dve"), sem("l2_sq")
        cf_pe, cf_act, cf_dve = sem("cf_pe"), sem("cf_act"), sem("cf_dve")
        dl_pe, dl_act, dl_dve = ([sem(f"dl_{e}{hg}") for hg in range(2)] for e in ("pe", "act", "dve"))
        on_pe, on_act, on_dve = sem("on_pe"), sem("on_act"), sem("on_dve")
        scores, maxes, exps, probs = sem("scores"), sem("maxes"), sem("exps"), sem("probs")
        probs_t, probs_c, heads, head_hi = sem("probs_t"), sem("probs_c"), sem("heads"), sem("head_hi")
        fn_pe, fn_act = sem("fn_pe"), sem("fn_act")
        ctx_in, bias_in, mem_in = sem("ctx_in"), sem("bias_in"), sem("mem_in")
        mixed = sem("mixed")
        rope_pe, rope_dve = sem("rope_pe"), sem("rope_dve")
        mod_ready = sem("mod_ready")
        bias_ready = sem("bias_ready")
        out_ready, stored = sem("out_ready"), sem("stored")
        EV0 = 1
        EV_UP = 1
        FREE = 2

        class Counts:

            def __init__(self, eng):
                self.eng, self.base = eng, {}

            def at(self, s, n):
                v = n + self.base.get(s.name, 0)
                if not isinstance(v, int) or v > 0:
                    self.eng.wait_ge(s, v)

            def end(self, s, n):
                self.base[s.name] = self.base.get(s.name, 0) + n

        class Chain:

            def __init__(self, eng, s):
                self.eng, self.s, self.n, self.i, self.per = eng, s, 0, 0, 0

            def __call__(self, ins):
                ins.then_inc(self.s, 1)
                self.n += 1
                self.eng.wait_ge(self.s, self.i * self.per + self.n)

            def tick(self, ins):
                ins.then_inc(self.s, 1)
                self.n += 1

            def now(self):
                return self.i * self.per + self.n

            def loop(self, i, per):
                self.n, self.i, self.per, self.mark = self.n - per, i, per, self.n

            def end(self, iters):
                assert self.n == self.mark, (self.n, self.mark)
                self.n, self.i, self.per = self.n + self.per * (iters - 1), 0, 0

        block = es.enter_context(nc.Block())

        def over(eng, ph, slot_of, evac_fn, chain, links, extra=None):
            ends = [(k + 1) * ph.slots_per_block - 1 + LAG for k in range(ph.K)]
            order = list(PH.values())
            n = order.index(ph)
            slot_fn = slot_of(ph)

            def body(i, first, done):
                for j in range(ph.S):
                    if j >= done:
                        slot_fn(i, j)
                    if extra:
                        extra(i, j)
                    for k, t in enumerate(ends):
                        if t == j:
                            evac_fn(i * ph.K + k, (ph.block0 + k) % 2, k)
                        elif t - ph.S == j and not first:
                            evac_fn((i - 1) * ph.K + k, (ph.block0 + k) % 2, k)

            body(0, True, min(PRE, ph.S) if n else 0)
            if ph.iters > 1:
                with eng.Fori(1, ph.iters) as i:
                    chain.loop(i, links)
                    body(i, False, 0)
                chain.end(ph.iters)
            after = order[n + 1] if n + 1 < len(order) else None
            for j in range(LAG):
                if after and j < min(PRE, after.S):
                    slot_of(after)(0, j)
                for k, t in enumerate(ends):
                    if t - ph.S == j:
                        evac_fn((ph.iters - 1) * ph.K + k, (ph.block0 + k) % 2, k)

        @block.sync
        def _(sp):
            def load(body, j):
                sp.wait_ge(split_done, body * RAW_N + (j + 1))
                sp.dma_start(raw[:, j, :], stream[ds(body * RAW_N + j, 1), :, :].rearrange("a p n -> (a p) n")
                             ).then_inc(raw_in[j], 16)

            def load_mod(body, q):
                sp.wait_ge(mod_used, body * 4 + (q + 1))
                sp.dma_start(modraw[:, q % MOD_N, :], mods[ds(body * 4 + q, 1), :, :].rearrange("a p n -> (a p) n")
                             ).then_inc(mod_in[q % MOD_N], 16)

            def bodies(first, last, mod=False):
                with sp.Fori(first, last) as b:
                    for j in range(RAW_N):
                        load(b, j)
                        if mod and j % 2:
                            load_mod(b - first, j // 2)

            for q in range(4):
                sp.dma_start(h[:, 4 * q:4 * q + 4, :], x_t[:, 4 * q:4 * q + 4, :]).then_inc(src_in[q], 16)
            with_mod = PH["memk"].slot0 // RAW_N
            bodies(0, with_mod)
            bodies(with_mod, with_mod + 2 * MOD_BODIES, True)
            bodies(with_mod + 2 * MOD_BODIES, N_SLOTS // RAW_N)
            for j in range(N_SLOTS % RAW_N):
                load(N_SLOTS // RAW_N, j)
            for q in range(DC // 4):
                sp.wait_ge(out_ready, q + 1)
                sp.dma_start(out_t[:, 4 * q:4 * q + 4, :], tmp[:, 4 * q:4 * q + 4, :]).then_inc(stored, 16)
            sp.wait_ge(stored, 16 * (DC // 4))

        @block.gpsimd
        def _(pool):
            pool.dma_start(ones[:, :], eye[:, P:2 * P]).then_inc(ones_in, 16)
            for dst, src in ((ident, eye[:, 0:P]), (pv, pvec), (cz[:, 0:N_CM], cmix)):
                pool.dma_start(dst[:, :] if dst is not cz else dst, src).then_inc(params_in, 16)
            pool.wait_ge(mixed, 1)
            pool.dma_start(memV[:, :, :].rearrange("p a b -> p (a b)"), mem_t).then_inc(mem_in, 16)
            pool.dma_start(cz[:, 0:N_CA], catt).then_inc(late_in, 16)
            pool.wait_ge(block_free, FREE + PH["w1_0"].block0 + 1)
            pool.dma_start(tmp[:, :, :].rearrange("p a b -> p (a b)"), ctx_t).then_inc(ctx_in, 16)
            last = PH["w2_3"]
            pool.wait_ge(block_free, FREE + last.block0 + last.nblocks)
            pool.dma_start(bias[:, :, :, :].rearrange("p a b c -> p (a b c)"), na_bias).then_inc(bias_in, 16)
            pool.dma_start(mask[:, :, :].rearrange("p a b -> p (a b)"), na_mask).then_inc(bias_in, 16)

        BETA, A1, LN1, EA, G, GC, NGC, EGC, BEG, KDL, KDS = range(11)
        C_SILU, GAIN_X, GAIN_C, GAIN_F, SM, ROOT, H_ROOT, L2, ON = 0, 32, 48, 64, 96, 104, 110, 128, 176

        def gtc(row, ch, hd, n=1):
            return gt[:, row, ch * 8 + hd:ch * 8 + hd + n]

        LEVELS = 7
        GROUPS, CHUNKS = range(2), range(TT)
        PE_SIG = [["bc", "tr", "aa"] + [f"{a}{l}" for l in range(LEVELS) for a in "yz"] + ["uw"] + ["ws"] * ch + ["o"]
                  for ch in CHUNKS]
        ACT_SIG = [["eg"] * ch + ["dtx"] + ["kds"] * (1 - ch) + ["tok"] + [f"y{l}" for l in range(LEVELS)] + ["uc", "oc"]
                   for ch in CHUNKS]
        DVE_SIG = [["dta"] + ["kdl"] * (1 - ch) + ["kb", "vb", "aat", "m0"] + [a for l in range(LEVELS)
                   for a in ([f"m{l + 1}"] if l + 1 < LEVELS else []) + [f"x{l}"]] + ["vn"] * ch for ch in CHUNKS]

        def step(table, ch, name):
            return sum(len(table[k]) for k in range(ch)) + table[ch].index(name) + 1

        def bk(hg, k):
            return b4(4 * hg + k)

        def attention_units(kind):
            return [(hd, mt) for hd in range({"cross": XA_H, "mla": MLA_H, "na": NA_H}[kind]) for mt in range(TT)]

        def key_tiles(kind):
            return TT if kind == "cross" else 2 * TT

        @block.tensor
        def _(pe):
            c = Counts(pe)

            def phase(ph, src, c0=0, after=None):
                def body(i):
                    for k in range(ph.K):
                        b = bank[(ph.block0 + k) % 2]
                        pe.wait_ge(block_free, i * ph.K + (ph.block0 + k + 1))
                        for sl in range(ph.slots_per_block):
                            j = k * ph.slots_per_block + sl
                            pe.wait_ge(split_done, i * ph.S + (ph.slot0 + j + 1 + RAW_N))
                            if after and k == 0:
                                c.at(after[0], after[1] + (sl + 1) * after[2])
                            buf = (ph.slot0 + j) % SPL_N
                            for ci in range(ph.per_slot):
                                kc = sl * ph.per_slot + ci
                                for hf in range(ph.ncol // P if not ph.flip else TT):
                                    for n, (wx, ax) in enumerate(((whi, 0), (whi, 1), (wlo, 0))):
                                        if ph.flip:
                                            lhs = src[:, ax, c0 + kc, hf * P:(hf + 1) * P]
                                            rhs = wx[:, buf, ci * NCOL:(ci + 1) * NCOL]
                                        else:
                                            lhs = wx[:, buf, ci * ph.ncol + hf * P:ci * ph.ncol + (hf + 1) * P]
                                            rhs = src[:, ax, c0 + kc, :]
                                        mm = pe.matmul(b[:, hf * T:(hf + 1) * T], lhs, rhs,
                                                       start=(kc == 0 and hf == 0 and n == 0),
                                                       stop=(kc == ph.chunks - 1 and n == 2), skip_group_check=True)
                            mm.then_inc(slot_used, 1)
                            if ph.mod and j == MOD_OUT_AT:
                                mod_matmuls(ph, i)
                if ph.iters > 1:
                    with pe.Fori(0, ph.iters) as i:
                        body(i)
                else:
                    body(0)

            def mod_matmuls(ph, i):
                mb = i + ph.mod0
                pe.wait_ge(mod_used, mb * 8 + (8 + MOD_N))
                for w in range(ph.mod):
                    for n in range(MOD_COL // P):
                        mm = pe.matmul(bank[2][:, 4 * w + n:4 * w + n + 1], modacc[:, w, n * P:(n + 1) * P],
                                       ones[:, 0:1], start=True, stop=True, skip_group_check=True)
                mm.then_inc(mod_out, 1)

            def row_sums(out, src, tok, start, stop):
                return pe.matmul(out, src[:, tok], ones[:, 0:1], start=start, stop=stop, skip_group_check=True)

            def over_features(out, col, n, start=True):
                return pe.matmul(out, small[:, col + n:col + n + 1].to_broadcast([P, P]), ident[:, :], start=start, stop=True,
                                 skip_group_check=True)

            def norm_root(b, col, s_):
                c.at(s_, 1)
                c.end(s_, 1)
                for mt in range(TT):
                    mm = over_features(bank[b][:, T + mt * P:T + (mt + 1) * P], col, mt, mt == 0)
                mm.then_inc(spread, 1)

            def part_sums(b, groups):
                q = 0
                for n, size in enumerate(groups):
                    for k in range(size):
                        c.at(parts, q + 1)
                        for mt in range(TT):
                            at = q % 2 * T + mt * P
                            mm = row_sums(bank[b][:, TT * n + mt:TT * n + mt + 1], ev[:, q // 2, :], slice(at, at + P),
                                          k == 0 and mt == 0, k == size - 1)
                        q += 1
                mm.then_inc(sums, 1)
                c.end(parts, q)

            def residual_sums(b, s_):
                c.at(res_sum, 1)
                c.end(res_sum, 1)
                for hf in range(2):
                    for mt in range(TT):
                        mm = row_sums(bank[b][:, mt:mt + 1], stat[:, 1, :], slice(hf * T + mt * P, hf * T + (mt + 1) * P),
                                      hf == 0 and mt == 0, hf == 1)
                mm.then_inc(s_, 1)

            def act_in(n):
                c.at(act_ready, n)
                c.end(act_ready, n)

            def phase_in(name):
                phase(PH[name], act, after=(act_ready, 0, 1))
                c.end(act_ready, DC // 4)

            def phase_out(ph):
                pe.wait_ge(block_free, FREE + ph.block0 + ph.nblocks)

            pe.wait_ge(ones_in, 16)
            part_sums(3, (4,))
            pe.wait_ge(params_in, 48)
            norm_root(3, ROOT, root)
            for q in range(DC // 4):
                c.at(normed, q + 1)
                for k in range(4 * q, 4 * q + 4):
                    for mt in range(TT):
                        mm = pe.matmul(bank[4][:, 16 * mt:16 * mt + 16], tmp[:, k, mt * P:(mt + 1) * P],
                                       cc(CM, "w_ba")[:, 16 * k:16 * k + 16], start=(k == 0 and mt == 0), stop=(k == DC - 1),
                                       skip_group_check=True)
            mm.then_inc(gate_pe, 1)
            phase_in("glu")
            phase(PH["qkv"], act)

            def l2_sums(first):
                for p in range(first, first + 4):
                    c.at(l2_sq, p + 1)
                    for n in range(4):
                        mm = row_sums(bank[5][:, 4 * p + n:4 * p + n + 1], tmp[:, 8 + 2 * (p % 4) + n // 2, :],
                                      slice(n % 2 * P, (n % 2 + 1) * P), True, True)
                mm.then_inc(l2_pe, 1)
            phase(PH["z_0"], act)
            l2_sums(0)
            c.at(gate_dve, 2)
            for mt in range(TT):
                mm = pe.matmul(bank[3][:, 32 + 8 * mt:40 + 8 * mt], cc(CM, "upper"), gtc(G, mt, 0, 8), start=True, stop=True)
            mm.then_inc(gate_pe, 1)
            phase(PH["z_1"], act)
            c.at(cf_dve, 1)
            for k in range(8):
                mm = pe.matmul(bank[2][:, 0:T], ones[:, :], tmp[:, k, :], start=(k == 0), stop=(k == 7))
            mm.then_inc(cf_pe, 1)
            l2_sums(4)
            c.at(cf_dve, 4)
            for mt in range(TT):
                mm = row_sums(bank[5][:, 32 + mt:33 + mt], stat[:, 0, :], slice(mt * P, (mt + 1) * P), True, True)
            mm.then_inc(cf_pe, 1)
            c.at(l2_dve, 2)
            for p in range(8):
                if p >= 4:
                    c.at(l2_dve, p - 1)
                for n in range(4):
                    mm = over_features(bank[4 + p % 4][:, n * P:(n + 1) * P], L2, 4 * p + n, n == 0)
                mm.then_inc(l2_pe, 1)
            for mt in range(TT):
                mm = over_features(bank[2][:, mt * P:(mt + 1) * P], L2, 32 + mt, mt == 0)
            mm.then_inc(cf_pe, 1)
            c.at(cf_dve, 6)
            c.at(l2_dve, 2 + 8)
            for ch in CHUNKS:
                tok = slice(ch * P, (ch + 1) * P)

                def a(hg, name):
                    c.at(dl_act[hg], step(ACT_SIG, ch, name))

                def v(hg, name):
                    c.at(dl_dve[hg], step(DVE_SIG, ch, name))
                for hg in GROUPS:
                    if ch:
                        c.at(dl_act[hg], step(ACT_SIG, ch - 1, "oc"))
                    for n in range(4):
                        pe.matmul(bk(hg, 0)[:, n, :], gtc(G, ch, 4 * hg + n).to_broadcast([P, P]), cc(CM, "upper"), start=True, stop=True)
                    for n in range(4):
                        mm = pe.matmul(bk(hg, 1)[:, n, :], gtc(BETA, ch, 4 * hg + n).to_broadcast([P, P]), ident[:, :], start=True, stop=True)
                    mm.then_inc(dl_pe[hg], 1)
                    for n in range(4):
                        pe.transpose(bk(hg, 2)[:, n, :], qkvT[:, 8 + 4 * hg + n, tok], ident[:, :])
                    for n in range(4):
                        mm = pe.transpose(bk(hg, 3)[:, n, :], qkvT[:, 16 + 4 * hg + n, tok], ident[:, :])
                    mm.then_inc(dl_pe[hg], 1)
                for hg in GROUPS:
                    v(hg, "kb")
                    for n in range(4):
                        pe.matmul(bk(hg, 0)[:, n, :], qkvT[:, 8 + 4 * hg + n, tok], KBT[hg][:, n, :], start=True, stop=True)
                    for n in range(4):
                        mm = pe.matmul(bk(hg, 1)[:, n, :], qkvT[:, 8 + 4 * hg + n, tok], qkvT[:, 4 * hg + n, tok], start=True, stop=True)
                    mm.then_inc(dl_pe[hg], 1)
                for lv in range(LEVELS):
                    for hg in GROUPS:
                        v(hg, f"m{lv}")
                        if lv:
                            v(hg, f"x{lv - 1}")
                        for n in range(4):
                            mm = pe.matmul(bk(hg, 0)[:, n, :], MT[hg][:, n, :], X[hg][:, n, :], start=True, stop=True)
                        mm.then_inc(dl_pe[hg], 1)
                    for hg in GROUPS:
                        a(hg, f"y{lv}")
                        if lv + 1 < LEVELS:
                            for n in range(4):
                                pe.matmul(bk(hg, 2)[:, n, :], XT[hg][:, n, :], Y[hg][:, n, :], start=True, stop=True)
                        for n in range(4):
                            mm = pe.matmul(bk(hg, 3)[:, n, :], Y[hg][:, n, :], XT[hg][:, n, :], start=True, stop=True)
                        mm.then_inc(dl_pe[hg], 1)
                for hg in GROUPS:
                    v(hg, f"x{LEVELS - 1}")
                    for n in range(4):
                        mm = pe.matmul(bk(hg, 1)[:, n, :], XT[hg][:, n, :], VB[hg][:, n, :], start=True, stop=True)
                    if ch:
                        for n in range(4):
                            mm = pe.matmul(bk(hg, 2)[:, n, :], KW[hg][:, n, :], XT[hg][:, n, :], start=True, stop=True)
                    mm.then_inc(dl_pe[hg], 1)
                if ch:
                    for hg in GROUPS:
                        a(hg, "uc")
                        for n in range(4):
                            mm = pe.matmul(bk(hg, 0)[:, n, :], WT[hg][:, n, :], ST[hg][:, n, :], start=True, stop=True)
                        mm.then_inc(dl_pe[hg], 1)
                for hg in GROUPS:
                    if ch:
                        v(hg, "vn")
                    else:
                        a(hg, "uc")
                    for n in range(4):
                        if ch:
                            pe.matmul(bk(hg, 3)[:, n, :], ST[hg][:, n, :], QDT[hg][:, n, :], start=True, stop=False)
                        mm = pe.matmul(bk(hg, 3)[:, n, :], VN[hg][:, n, :], ATT[hg][:, n, :], start=not ch, stop=True)
                    if not ch:
                        for n in range(4):
                            mm = pe.matmul(bk(hg, 2)[:, n, :], KW[hg][:, n, :], VN[hg][:, n, :], start=True, stop=True)
                    mm.then_inc(dl_pe[hg], 1)
            for hd in range(DN_H):
                c.at(on_act, hd // 4 + 1)
                for mt in range(TT):
                    mm = row_sums(bank[4][:, 2 * hd + mt:2 * hd + mt + 1], tmp[:, hd, :], slice(mt * P, (mt + 1) * P), True, True)
            mm.then_inc(on_pe, 1)
            c.at(on_dve, 2)
            for p in range(4):
                for n in range(4):
                    mm = over_features(bank[4 + p][:, n * P:(n + 1) * P], ON, 4 * p + n, n == 0)
                mm.then_inc(on_pe, 1)
            act_in(2 + 4)
            phase(PH["wout"], act)
            pe.wait_ge(mem_sum, 1)
            for q in range(4):
                for mt in range(TT):
                    mm = row_sums(bank[3][:, mt:mt + 1], memK[:, q, :], slice(mt * P, (mt + 1) * P), q == 0 and mt == 0, q == 3)
            mm.then_inc(sums, 1)
            residual_sums(4, h_sums)
            norm_root(3, ROOT, root)
            phase_in("memk")
            norm_root(4, H_ROOT, h_root)
            phase(PH["memv"], act)
            phase_in("wq")

            def attention(kind):
                units = attention_units(kind)
                kt = key_tiles(kind)
                for u in range(len(units) + 2):
                    if u < len(units):
                        hd, mt = units[u]
                        tok = slice(mt * P, (mt + 1) * P)
                        b = bank[3 + u % 2]
                        if kind == "cross":
                            for k in range(XA_CH):
                                mm = pe.matmul(b[:, 0:T], tmp[:, XA_CH * hd + k, tok], memK[:, XA_CH * hd + k, :],
                                               start=(k == 0), stop=(k == XA_CH - 1))
                        elif kind == "na":
                            mm = pe.matmul(b[:, :], naQ[:, hd, tok], naK[:, hd, :, :], start=True, stop=True)
                        else:
                            lo = ROPE * (hd % 2)
                            pe.matmul(b[:, :], qN[:, hd, tok], kN[:, hd, :, :], start=True, stop=False)
                            mm = pe.matmul(b[:, :], qR[lo:lo + ROPE, hd // 2, tok], kr[lo:lo + ROPE, :, :], start=False, stop=True)
                        mm.then_inc(scores, 1)
                    if 1 <= u <= len(units):
                        w = u - 1
                        c.at(probs, w + 1)
                        if w >= 2:
                            c.at(probs_c, w - 1)
                        for k in range(kt):
                            mm = pe.transpose(b4(5 + w % 2)[:, k, :], stat[:, w % 2, k * P:(k + 1) * P], ident[:, :])
                        mm.then_inc(probs_t, 1)
                    if u >= 3 and u % 2 == 1:
                        hd = (u - 3) // 2
                        c.at(probs_c, u - 1)
                        if hd:
                            c.at(act_ready, hd)
                        pt = ev[:, :, :].rearrange("p a (b t) -> p (a b) t", b=2)
                        for cd in range(XA_CH if kind == "cross" else 1):
                            b = bank[cd // 2 if kind == "cross" else 0]
                            for k in range(kt):
                                if kind == "cross":
                                    val = memV[:, k, (XA_CH * hd + cd) * P:(XA_CH * hd + cd + 1) * P]
                                elif kind == "na":
                                    val = naV[:, k // 2, k % 2, hd * P:(hd + 1) * P]
                                else:
                                    val = mlaV[:, k // 2, k % 2, hd * P:(hd + 1) * P]
                                mm = pe.matmul(b[:, T * (cd % 2):T * (cd % 2) + T], val, pt[:, k, :],
                                               start=(k == 0), stop=(k == kt - 1))
                        mm.then_inc(heads, 1)
                c.end(probs, len(units))
                c.end(probs_c, len(units))

            phase_out(PH["wq"])
            attention("cross")
            act_in(XA_H)
            phase(PH["wo"], act)
            residual_sums(3, sums)
            norm_root(3, ROOT, root)
            for r in range(FF1_ROUNDS):
                if r:
                    phase(PH[f"w1_{r}"], act)
                else:
                    phase_in("w1_0")
                phase(PH[f"w2_{r}"], hid, after=(ev_v, PH[f"w1_{r}"].nblocks * r + EV0, 2))
            c.end(ev_v, PH["w1_0"].nblocks * FF1_ROUNDS)
            residual_sums(5, h_sums)
            part_sums(3, (4,))
            norm_root(5, H_ROOT, h_root)
            norm_root(3, ROOT, root)
            phase_in("ckv_c")
            c.at(h_sum, 1)
            for q in range(4):
                for mt in range(TT):
                    mm = row_sums(bank[5][:, mt:mt + 1], ev[:, q // 2, :], slice(q % 2 * T + mt * P, q % 2 * T + (mt + 1) * P),
                                  q == 0 and mt == 0, q == 3)
            mm.then_inc(h_sums, 1)
            phase(PH["nak_c"], act)
            norm_root(5, H_ROOT, h_root)
            phase(PH["nav_c"], act)
            phase(PH["kr_c"], act)
            phase_in("ckv_x")
            for name in ("nak_x", "nav_x", "cq", "naq", "fn", "kr_x"):
                phase(PH[name], act)
            phase_out(PH["kr_x"])
            attention("na")
            act_in(NA_H)
            pe.wait_ge(late_in, 16)
            for g in range(FN_G):
                if g:
                    c.at(fn_act, 2 * g)
                for mt in range(TT):
                    mm = pe.matmul(bank[3][:, mt * T:(mt + 1) * T], fT[:, g, mt * P:(mt + 1) * P], cc(CA, "dft_ch"), start=True, stop=True)
                mm.then_inc(fn_pe, 1)
                c.at(fn_act, 2 * g + 1)
                for n in range(2 * TT):
                    mt, part = n // 2, n % 2
                    mm = pe.matmul(bank[4][:, 0:T], stat[:, 0, mt * T + part * P:mt * T + (part + 1) * P],
                                   cc(CA, ("dft_cos", "dft_sin")[part])[:, mt * T:(mt + 1) * T], start=(n == 0), stop=(n == 3))
                mm.then_inc(fn_pe, 1)
                c.at(fn_act, 2 * g + 2)
                if g:
                    c.at(act_ready, g)
                pe.matmul(bank[0][:, 0:T], cc(CA, "w_fnet")[:, g * P:(g + 1) * P], stat[:, 1, 0:T], start=True, stop=True).then_inc(heads, 1)
            act_in(FN_G)
            part_sums(3, (1, 1, 1))
            c.at(root, 1)
            c.end(root, 1)
            for n in range(3):
                for mt in range(TT):
                    mm = over_features(bank[5 + n][:, mt * P:(mt + 1) * P], ROOT, 2 * n + mt, mt == 0)
                mm.then_inc(spread, 1)
            act_in(1)
            phase(PH["kn_c"], act)
            phase(PH["v_c"], act)
            act_in(1)
            phase(PH["kn_x"], act, 4)
            phase(PH["v_x"], act, 4)
            act_in(1)
            phase(PH["qn"], act)
            phase(PH["qr"], act)
            phase_out(PH["qr"])
            for n in range(1 + MLA_H // 2):
                src = kr[:, 0, :] if n == 0 else qR[:, n - 1, :]
                pe.matmul(bank[3 + n][:, 0:T], cc(CA, "swap"), src, start=True, stop=True).then_inc(rope_pe, 1)
            c.at(rope_dve, 1 + MLA_H // 2)
            attention("mla")
            act_in(MLA_H)
            phase(PH["wout2"], act)
            residual_sums(3, sums)
            norm_root(3, ROOT, root)
            done = 0
            for r, n in enumerate(FF2_ROUNDS):
                if r:
                    phase(PH[f"up_{r}"], act)
                else:
                    phase_in("up_0")
                phase(PH[f"down_{r}"], hid, after=(ev_v, EV_UP * done + EV0, 4 * EV_UP))
                done += n
            residual_sums(3, sums)
            norm_root(3, ROOT, root)

        @block.scalar
        def _(sc):
            c = Counts(sc)
            chain = Chain(sc, act_step)

            def slot(ph):
                def f(i, j):
                    at = ph.slot0 + j
                    sc.wait_ge(raw_in[at % RAW_N], i * (16 * (ph.S // RAW_N)) + 16 * (at // RAW_N + 1))
                    sc.wait_ge(slot_used, i * ph.S + (at + 1))
                    sc.activation(whi[:, at % SPL_N, :], raw[:, at % RAW_N, :], ACT.Copy).then_inc(hi_done, 1)
                return f

            def done(ph, n):
                sc.wait_ge(slot_used, n * ph.slots_per_block + (ph.slot0 + ph.slots_per_block + SPL_N))

            def to(dst, flip=False, func=ACT.Copy):
                def make(ph):
                    def f(n, b, k):
                        done(ph, n)
                        o = dst[:, 0:TT, ds(n * NCOL, NCOL)] if flip else dst[:, ds(n * 2, 2), :]
                        sc.activation(o, b2(b), func).then_inc(block_free, 1)
                    return f
                return make

            def one(dst):
                def make(ph):
                    def f(n, b, k):
                        done(ph, n)
                        sc.activation(dst, bank[b][:, 0:T], ACT.Copy).then_inc(block_free, 1)
                    return f
                return make

            def nothing(ph):
                return lambda n, b, k: None

            def conv4(ph):
                def f(n, b, k):
                    done(ph, n)
                    sc.wait_ge(block_free, n + (FREE + ph.block0))
                    for hf in range(2):
                        ins = sc.activation(ev[:, 0, hf * T:(hf + 1) * T], b2(b)[:, hf, :], ACT.Copy,
                                            scale=par("dn_conv", n * 8 + (4 * hf + 3)))
                    ins.then_inc(ev_a, 1)
                    sc.wait_ge(block_free, n + (FREE + ph.block0 + 1))
                    chain(sc.activation(qkvT[:, ds(n * 2, 2), :], ev[:, 0, :].rearrange("p (a b) -> p a b", a=2), ACT.Silu))
                return f

            def glu(ph):
                def f(n, b, k):
                    done(ph, n)
                    sc.wait_ge(block_free, n + (FREE + ph.block0))
                    sc.activation(ev[:, 0, 0:T], b2(b)[:, 1, :], ACT.Sigmoid).then_inc(ev_a, 1)
                return f

            def relu2(ph):
                def f(n, b, k):
                    done(ph, n)
                    c.at(ev_v, n + EV0)
                    sc.activation(ev[:, 0, :], bank[b][:, :], ACT.Relu).then_inc(block_free, 1)
                    sc.wait_ge(block_free, n + (FREE + ph.block0 + 1))
                    chain(sc.activation(ev[:, 1, :], ev[:, 0, :], ACT.Square))
                    sc.activation(hid[:, 0, ds(n * 2, 2), :], ev[:, 1, :].rearrange("p (a b) -> p a b", a=2),
                                  ACT.Copy).then_inc(ev_a, 1)
                return f

            def gated(first):
                def make(ph):
                    def f(n, b, k):
                        done(ph, n)
                        c.at(ev_v, n * EV_UP + EV0)
                        for hf in range(2):
                            ins = sc.activation(ev[:, 0, hf * T:(hf + 1) * T], b2(b)[:, hf, :], ACT.Identity,
                                                scale=par("ff_conv", n * 6 + (6 * first + 3 * hf + 1)),
                                                bias=par("ff_b", n * 2 + (2 * first + hf)))
                        ins.then_inc(ev_a, 1)
                        sc.wait_ge(block_free, n + (FREE + ph.block0 + 1))
                        sc.activation(ev[:, 1, 0:T], ev[:, 0, 0:T], ACT.Silu).then_inc(ev_a, 1)
                    return f
                return make

            def squared(ph):
                def f(n, b, k):
                    sc.wait_ge(block_free, n + (FREE + ph.block0 + 1))
                    sc.activation(ev[:, k % 2, :].rearrange("p (a b) -> p a b", a=2), h[:, ds(n * 2, 2), :], ACT.Square).then_inc(res_sq, 1)
                return f

            def phase(name, evac, links=0, extra=None):
                over(sc, PH[name], slot, evac(PH[name]), chain, links, extra)

            def before(name):
                sc.wait_ge(block_free, FREE + PH[name].block0)

            def norm(src, shift=None, split=True, rooted=False, first=False, beside=None, into=tmp):
                for q in range(DC // 4 if src is not None else 0):
                    if first:
                        sc.wait_ge(src_in[q], 16)
                    sc.activation(into[:, 4 * q:4 * q + 4, :], src[:, 4 * q:4 * q + 4, :], ACT.Square).then_inc(squares, 1)
                if beside:
                    beside(0, 0)
                if not rooted:
                    c.at(var, 1)
                    sc.activation(small[:, ROOT:ROOT + TT], small[:, ROOT:ROOT + TT], ACT.Sqrt).then_inc(std, 1)
                    c.end(var, 1)
                if split:
                    for q in range(DC // 4):
                        c.at(normed, q + 1)
                        if shift is None:
                            ins = sc.activation(act[:, 0, 4 * q:4 * q + 4, :], tmp[:, 4 * q:4 * q + 4, :], ACT.Copy)
                        else:
                            for k in range(4 * q, 4 * q + 4):
                                ins = sc.activation(act[:, 0, k, :], tmp[:, k, :], ACT.Identity, bias=modt[:, shift + k:shift + k + 1])
                        ins.then_inc(norm_hi, 1)
                    c.end(normed, DC // 4)

            norm(h, first=True)
            sc.wait_ge(params_in, 48)
            sc.activation(small[:, C_SILU:C_SILU + 2 * DC], pv[:, PV["c"][0]:PV["c_ctx"][1]], ACT.Silu).then_inc(mod_ready, 1)
            phase("glu", glu)
            phase("qkv", conv4, PH["qkv"].K)
            def row(r):
                return gt[:, r, :]
            c.at(gate_dve, 1)
            sc.activation(row(BETA).rearrange("p (a b) -> p a b", a=2),
                          bank[4][:, 0:32].rearrange("p (a b) -> p a b", a=2)[:, :, 0:8], ACT.Sigmoid)
            sc.activation(gt[:, EA, 0:8], par("a_log", 0, 8), ACT.Exp)
            chain(sc.activation(row(LN1), row(A1), ACT.Abs))
            chain(sc.activation(row(LN1), row(LN1), ACT.Exp, scale=-1.0))
            sc.activation(row(LN1), row(LN1), ACT.Ln, bias=1.0).then_inc(gate_act, 1)
            sc.wait_ge(act_step, chain.n)
            c.at(gate_pe, 1)

            def l2_squares(first):
                def f(i, j):
                    if j >= 4:
                        if first and j == 4:
                            c.at(l2_pe, 1)
                        p = first + j - 4
                        sc.activation(tmp[:, 2 * j:2 * j + 2, :], qkvT[:, 2 * p:2 * p + 2, :], ACT.Square).then_inc(l2_sq, 1)
                return f
            for n in range(2):
                phase(f"z_{n}", to(zT[:, 4 * n:4 * n + 4, :], func=ACT.Silu), 0, l2_squares(4 * n))

            c.at(gate_pe, 2)
            gc = bank[3][:, 32:48]
            sc.activation(row(GC), gc, ACT.Copy)
            sc.activation(row(NGC), gc, ACT.Copy, scale=-1.0)
            sc.activation(row(EGC), gc, ACT.Exp).then_inc(gate_act, 1)
            c.at(cf_dve, 3)
            c.at(l2_pe, 2)
            sc.activation(tmp[:, 8:16, :], tmp[:, 0:8, :], ACT.Square).then_inc(cf_act, 1)
            c.at(l2_dve, 1)
            sc.activation(small[:, L2:L2 + 34], small[:, L2:L2 + 34], ACT.Sqrt).then_inc(l2_act, 1)
            for q in range(2):
                c.at(cf_dve, 5 + q)
                for k in range(4 * q, 4 * q + 4):
                    ins = sc.activation(tmp[:, 8 + k, :], tmp[:, k, :], ACT.Silu, bias=par("ln_b", k))
                chain(ins)
                sc.activation(act[:, 0, 8 + 4 * q:12 + 4 * q, :], tmp[:, 8 + 4 * q:12 + 4 * q, :], ACT.Copy).then_inc(cf_act, 1)
            c.at(cf_dve, 7)
            for ch in CHUNKS:
                tok = slice(ch * P, (ch + 1) * P)

                def p_(hg, name):
                    c.at(dl_pe[hg], step(PE_SIG, ch, name))

                def v(hg, name):
                    c.at(dl_dve[hg], step(DVE_SIG, ch, name))
                if ch:
                    for hg in GROUPS:
                        p_(hg, "bc")
                        sc.activation(EG[hg], bk(hg, 0), ACT.Exp).then_inc(dl_act[hg], 1)
                for hg in GROUPS:
                    v(hg, "dta")
                    for n in range(4):
                        ins = sc.activation(DT[hg][:, n, :], DT[hg][:, n, :], ACT.Exp, bias=gtc(NGC, ch, 4 * hg + n))
                    ins.then_inc(dl_act[hg], 1)
                    if not ch:
                        v(hg, "kdl")
                        kds = gt[:, KDS, 4 * hg:4 * hg + 4]
                        sc.activation(kds, gt[:, KDL, 4 * hg:4 * hg + 4], ACT.Exp).then_inc(dl_act[hg], 1)
                        c.at(dl_act[hg], step(ACT_SIG, ch, "kds"))
                    p_(hg, "tr")
                    for n in range(4):
                        w = gtc(BEG, ch, 4 * hg + n) if ch else gt[:, KDS, 4 * hg + n:4 * hg + n + 1]
                        ins = sc.activation(KW[hg][:, n, :], bk(hg, 2)[:, n, :], ACT.Copy, scale=w)
                    ins.then_inc(dl_act[hg], 1)
                for lv in range(LEVELS):
                    for hg in GROUPS:
                        p_(hg, f"y{lv}")
                        sc.activation(Y[hg], bk(hg, 0), ACT.Copy).then_inc(dl_act[hg], 1)
                for hg in GROUPS:
                    p_(hg, "uw")
                    if ch:
                        sc.activation(U_[hg], bk(hg, 1), ACT.Copy)
                        sc.activation(WT[hg], bk(hg, 2), ACT.Copy).then_inc(dl_act[hg], 1)
                    else:
                        sc.activation(VN[hg], bk(hg, 1), ACT.Copy).then_inc(dl_act[hg], 1)
                for hg in GROUPS:
                    p_(hg, "o")
                    ins = sc.activation(qkvT[:, 16 + 4 * hg:20 + 4 * hg, tok], bk(hg, 3), ACT.Copy)
                    if not ch:
                        ins = sc.activation(ST[hg], bk(hg, 2), ACT.Copy)
                    ins.then_inc(dl_act[hg], 1)
            for hg in GROUPS:
                c.at(dl_act[hg], step(ACT_SIG, TT - 1, "oc"))
            for q in range(2):
                sc.activation(tmp[:, 4 * q:4 * q + 4, :], qkvT[:, 16 + 4 * q:20 + 4 * q, :], ACT.Square).then_inc(on_act, 1)
            c.at(on_dve, 1)
            sc.activation(small[:, ON:ON + 16], small[:, ON:ON + 16], ACT.Sqrt).then_inc(on_act, 1)
            for p in range(4):
                c.at(on_dve, p + 3)
                sc.activation(act[:, 0, 2 * p:2 * p + 2, :], qkvT[:, 16 + 2 * p:18 + 2 * p, :], ACT.Copy).then_inc(on_act, 1)
            def memory_squares(i, j):
                if isinstance(i, int) and i == 0 and j == LAG + 1:
                    sc.wait_ge(mem_in, 16)
                    for q in range(4):
                        sc.activation(tmp[:, 4 * q:4 * q + 4, :], memory[:, 4 * q:4 * q + 4, :], ACT.Square).then_inc(mem_sq, 1)

            def h_sqrt(at):
                def f(i, j):
                    if isinstance(i, int) and i == 0 and j == at:
                        c.at(h_var, 1)
                        sc.activation(small[:, H_ROOT:H_ROOT + TT], small[:, H_ROOT:H_ROOT + TT], ACT.Sqrt).then_inc(h_std, 1)
                        c.end(h_var, 1)
                return f
            phase("wout", squared, 0, memory_squares)
            before("memk")
            norm(None)
            phase("memk", to(memK), 0, h_sqrt(6))
            phase("memv", to(memV, flip=True))
            before("wq")
            norm(None, rooted=True)
            phase("wq", to(tmp))

            def attention(kind, c0=0):
                units = attention_units(kind)
                kt = key_tiles(kind)
                nk = kt * P
                scale = {"cross": XA_SCALE, "mla": MLA_SCALE, "na": 1.0}[kind]
                for u in range(len(units) + 2):
                    if u < len(units):
                        pb = stat[:, u % 2, 0:nk]
                        c.at(maxes, u + 1)
                        sc.activation(pb, pb if kind == "na" else bank[3 + u % 2][:, 0:nk], ACT.Exp, scale=scale,
                                      bias=small[:, SM + 4 * (u % 2) + 1:SM + 4 * (u % 2) + 2],
                                      accum_out=small[:, SM + 4 * (u % 2) + 2:SM + 4 * (u % 2) + 3]).then_inc(exps, 1)
                    if 1 <= u <= len(units):
                        w = u - 1
                        hd, mt = units[w]
                        c.at(probs_t, w + 1)
                        if mt == 0 and hd:
                            c.at(heads, hd)
                        sc.activation(ev[:, :, :].rearrange("p a (b t) -> p (a b) t", b=2)[:, 0:kt, mt * P:(mt + 1) * P],
                                      b4(5 + w % 2)[:, 0:kt, :], ACT.Copy).then_inc(probs_c, 1)
                    if u >= 3 and u % 2 == 1:
                        hd = (u - 3) // 2
                        c.at(heads, hd + 1)
                        if kind == "cross":
                            for k in range(2):
                                ins = sc.activation(act[:, 0, XA_CH * hd + 2 * k:XA_CH * hd + 2 * k + 2, :], b2(k), ACT.Copy)
                        else:
                            ins = sc.activation(act[:, 0, c0 + hd, :], bank[0][:, 0:T], ACT.Copy)
                        ins.then_inc(head_hi, 1)
                c.end(maxes, len(units))
                c.end(probs_t, len(units))
                c.end(heads, len(units) // 2)

            before("wo")
            attention("cross")
            phase("wo", squared)
            before("w1_0")
            norm(None)
            for r in range(FF1_ROUNDS):
                phase(f"w1_{r}", relu2, PH["w1_0"].K)
                c.end(ev_v, PH["w1_0"].nblocks)
                phase(f"w2_{r}", squared if r == FF1_ROUNDS - 1 else nothing)
            before("ckv_c")
            sc.wait_ge(ctx_in, 16)
            norm(tmp, shift=96, beside=h_sqrt(0), into=context_sq)

            def h_squares(i, j):
                if 1 <= j <= 4:
                    c.at(h_normed, j)
                    sc.activation(tmp[:, 4 * j - 4:4 * j, :], h[:, 4 * j - 4:4 * j, :], ACT.Square).then_inc(h_sq, 1)
            phase("ckv_c", to(ckv[:, 1, :, :]), 0, h_squares)
            phase("nak_c", to(naK[:, :, 1, :]), 0, h_sqrt(6))
            phase("nav_c", to(naV[:, 1, :, :], flip=True))
            phase("kr_c", one(kr[:, 1, :]))
            norm(None, shift=0, rooted=True)
            phase("ckv_x", to(ckv[:, 0, :, :]))
            phase("nak_x", to(naK[:, :, 0, :]))
            phase("nav_x", to(naV[:, 0, :, :], flip=True))
            phase("cq", to(cq))
            phase("naq", to(naQ))
            phase("fn", to(fT))
            phase("kr_x", one(kr[:, 0, :]))
            attention("na", 8)
            for g in range(FN_G):
                c.at(fn_pe, 2 * g + 1)
                if g:
                    c.at(heads, g)
                sc.activation(stat[:, 0, :], bank[3][:, :], ACT.Copy).then_inc(fn_act, 1)
                c.at(fn_pe, 2 * g + 2)
                sc.activation(stat[:, 1, 0:T], bank[4][:, 0:T], ACT.Copy, scale=FN_SCALE).then_inc(fn_act, 1)
                c.at(heads, g + 1)
                sc.activation(act[:, 0, 12 + g, :], bank[0][:, 0:T], ACT.Copy).then_inc(head_hi, 1)
            c.end(heads, FN_G)
            for n, src in enumerate((ckv[:, 1, :, :], ckv[:, 0, :, :], cq[:, :, :])):
                sc.activation(tmp[:, LC * n:LC * (n + 1), :], src, ACT.Square).then_inc(squares, 1)
            c.at(var, 1)
            sc.activation(small[:, ROOT:ROOT + 6], small[:, ROOT:ROOT + 6], ACT.Sqrt).then_inc(std, 1)
            c.end(var, 1)

            def latent_upper(n, c0):
                c.at(normed, n + 1)
                sc.activation(act[:, 0, c0:c0 + LC, :], tmp[:, LC * n:LC * (n + 1), :], ACT.Copy).then_inc(norm_hi, 1)
            latent_upper(0, 0)
            latent_upper(1, LC)
            phase("kn_c", to(kN[:, :, 1, :]))
            phase("v_c", to(mlaV[:, 1, :, :], flip=True))
            latent_upper(2, 0)
            c.end(normed, 3)
            phase("kn_x", to(kN[:, :, 0, :]))
            phase("v_x", to(mlaV[:, 0, :, :], flip=True))
            phase("qn", to(qN))
            phase("qr", to(qR))
            attention("mla")
            phase("wout2", squared)
            before("up_0")
            norm(None, shift=48)
            first = 0
            for r, n in enumerate(FF2_ROUNDS):
                phase(f"up_{r}", gated(first))
                c.end(ev_v, n * EV_UP)
                first += n
                phase(f"down_{r}", squared if r == len(FF2_ROUNDS) - 1 else nothing)
            norm(None, split=False)

        @block.vector
        def _(ve):
            c = Counts(ve)
            chain = Chain(ve, dve_step)
            ve.memset(cin[:, :, 0:CF_TAPS - 1], 0.0).then_inc(split_done, RAW_N)
            ve.memset(small[:, 120:121], 0.0).then_inc(slot_used, SPL_N)
            ve.memset(small[:, 122:123], 0.0).then_inc(block_free, FREE)
            ve.memset(small[:, 123:124], 0.0).then_inc(ev_v, EV0)

            mod_mark = {}

            def mod_store(n, both):
                ve.wait_ge(mod_out, n)
                return ve.tensor_copy(msum[:, 0:both, ds(n * 4 - 4, 4)], bank[2][:, 0:4 * both].rearrange("p (a b) -> p a b", a=both))

            def mod_chunk(ph, i, k):
                mb = i + ph.mod0
                q = k // 2
                if k % 2 == 0:
                    ve.wait_ge(mod_in[q % MOD_N], mb * 64 + 16 * (q // MOD_N + 1))
                if k == 0:
                    if not isinstance(mb, int):
                        mod_store(mb, ph.mod)
                    elif mb:
                        mod_store(mb, 2 if mb <= MOD_CTX else 1)
                elif k % 2 == 0:
                    ve.wait_ge(mod_used, mb * 8 + (k // 2 + MOD_N))
                else:
                    ve.wait_ge(dve_step, mod_mark[k - 1])
                for w in range(ph.mod):
                    wt = modraw[:, q % MOD_N, (k % 2) * MOD_COL:(k % 2 + 1) * MOD_COL]
                    at = C_SILU + DC * w + k
                    col = small[:, at:at + 1]
                    acc = modacc[:, w, :]
                    if k == 0:
                        ins = ve.tensor_scalar(acc, wt, col, None, ALU.mult)
                    else:
                        ins = ve.scalar_tensor_tensor(acc, wt, col, acc, ALU.mult, ALU.add)
                if k % 2:
                    ins.then_inc(mod_used, 1)
                else:
                    chain.tick(ins)
                    mod_mark[k] = chain.now()

            def slot(ph):
                def f(i, j):
                    at = ph.slot0 + j
                    ks = MOD_AT[j] if ph.mod and j < len(MOD_AT) else ()
                    for k in ks[:1]:
                        mod_chunk(ph, i, k)
                    ve.wait_ge(hi_done, i * ph.S + (at + 1))
                    ve.tensor_tensor(wlo[:, at % SPL_N, :], raw[:, at % RAW_N, :], whi[:, at % SPL_N, :].bitcast(F32),
                                     ALU.subtract).then_inc(split_done, 1)
                    for k in ks[1:]:
                        mod_chunk(ph, i, k)
                return f

            def done(ph, n):
                ve.wait_ge(slot_used, n * ph.slots_per_block + (ph.slot0 + ph.slots_per_block + SPL_N))

            def nothing(ph):
                return lambda n, b, k: None

            def conv4(ph):
                def f(n, b, k):
                    c.at(ev_a, n + 1)
                    for j in range(1, DN_TAPS):
                        for hf in range(2):
                            o = ev[:, 0, hf * T + j:(hf + 1) * T]
                            ins = ve.scalar_tensor_tensor(o, b2(b)[:, hf, 0:T - j], conv4_w[:, 8 * k + 4 * hf + 3 - j:8 * k + 4 * hf + 4 - j], o,
                                                          ALU.mult, ALU.add)
                            if j == DN_TAPS - 1 and hf:
                                ins.then_inc(block_free, 1)
                            else:
                                ins.then_inc(dve_step, 1)
                                chain.n += 1
                        if j < DN_TAPS - 1:
                            ve.wait_ge(dve_step, chain.i * chain.per + chain.n)
                return f

            def glu(ph):
                def f(n, b, k):
                    c.at(ev_a, n + 1)
                    ve.tensor_tensor(cin[:, ds(n, 1), CF_TAPS - 1:CF_TAPS - 1 + T], b2(b)[:, 0:1, :],
                                     ev[:, 0, 0:T].rearrange("p (a b) -> p a b", a=1), ALU.mult).then_inc(block_free, 1)
                return f

            def resid(gate=None, squares=False):
                def make(ph):
                    def f(n, b, k):
                        onto(n, b)
                        if squares and not (isinstance(n, int) and n == 0):
                            c.at(res_sq, n)
                            chain(ve.tensor_tensor(stat[:, 1, :], stat[:, 1, :], ev[:, (k - 1) % 2, :], ALU.add))

                    def onto(n, b):
                        done(ph, n)
                        if gate is None:
                            ve.tensor_tensor(h[:, ds(n * 2, 2), :], b2(b), h[:, ds(n * 2, 2), :], ALU.add).then_inc(block_free, 1)
                        else:
                            for hf in range(2):
                                o = h[:, ds(n * 2 + hf, 1), :]
                                ins = ve.scalar_tensor_tensor(o, b2(b)[:, hf:hf + 1, :], modt[:, ds(n * 2 + (gate + hf), 1)], o,
                                                              ALU.mult, ALU.add)
                            ins.then_inc(block_free, 1)
                    return f
                return make

            def relu2(ph):
                def f(n, b, k):
                    c.at(ev_a, n + 1)
                    o = hid[:, 0, ds(n * 2, 2), :]
                    ve.tensor_tensor(hid[:, 1, ds(n * 2, 2), :], ev[:, 1, :].rearrange("p (a b) -> p a b", a=2), o.bitcast(F32),
                                     ALU.subtract).then_inc(ev_v, 1)
                return f

            def gated(first):
                def make(ph):
                    def f(n, b, k):
                        c.at(ev_a, n * 2 + 1)
                        for j, so, do in ((0, slice(0, T - 1), slice(1, T)), (2, slice(1, T), slice(0, T - 1))):
                            for hf in range(2):
                                o = ev[:, 0, hf * T + do.start:hf * T + do.stop]
                                ins = ve.scalar_tensor_tensor(o, b2(b)[:, hf, so], par("ff_conv", n * 6 + (6 * first + 3 * hf + j)), o,
                                                              ALU.mult, ALU.add)
                                if j == 2 and hf:
                                    ins.then_inc(block_free, 1)
                                else:
                                    ins.then_inc(dve_step, 1)
                                    chain.n += 1
                            if j == 0:
                                ve.wait_ge(dve_step, chain.i * chain.per + chain.n)
                        c.at(ev_a, n * 2 + 2)
                        chain(ve.tensor_tensor(ev[:, 1, T:2 * T], ev[:, 1, 0:T], ev[:, 0, T:2 * T], ALU.mult))
                        t = ev[:, 1:2, T:2 * T]
                        chain(ve.tensor_copy(hid[:, 0, ds(n, 1), :], t))
                        ve.tensor_tensor(hid[:, 1, ds(n, 1), :], t, hid[:, 0, ds(n, 1), :].bitcast(F32), ALU.subtract).then_inc(ev_v, 1)
                    return f
                return make

            def phase(name, evac, links=0, extra=None):
                ph = PH[name]
                over(ve, ph, slot, evac(ph), chain, links + (DC // 2 if ph.mod else 0), extra)

            def residual(name, gate=None, extra=None):
                ph = PH[name]
                chain(ve.memset(stat[:, 1, :], 0.0))
                phase(name, resid(gate, True), ph.K, extra)
                c.at(res_sq, ph.nblocks)
                ve.tensor_tensor(stat[:, 1, :], stat[:, 1, :], ev[:, 1, :], ALU.add).then_inc(res_sum, 1)
                c.end(res_sq, ph.nblocks)

            def h_norm(at, b=4):
                def f(i, j):
                    if isinstance(i, int) and i == 0 and j == at:
                        c.at(h_sums, 1)
                        ve.tensor_scalar(small[:, H_ROOT:H_ROOT + TT], bank[b][:, 0:TT], 1.0 / D, EPS, ALU.mult, ALU.add).then_inc(h_var, 1)
                    if isinstance(i, int) and i == 0 and j == at + 2:
                        c.at(h_std, 1)
                        ve.reciprocal(small[:, H_ROOT:H_ROOT + TT], small[:, H_ROOT:H_ROOT + TT]).then_inc(h_root, 1)
                        c.end(h_sums, 1)
                        c.end(h_std, 1)
                return f

            def part_squares(src, n):
                for q in range(n):
                    c.at(squares, q + 1)
                    ve.tensor_reduce(ev[:, q // 2, q % 2 * T:(q % 2 + 1) * T], src[:, 4 * q:4 * q + 4, :].rearrange("p k t -> p t k"),
                                     AX.X, ALU.add).then_inc(parts, 1)
                c.end(squares, n)

            def norm(src, gain, shift=None, into=None, ahead=False, scaled=False, b=3):
                if not ahead and not scaled:
                    c.at(sums, 1)
                    ve.tensor_scalar(small[:, ROOT:ROOT + TT], bank[b][:, 0:TT], 1.0 / D, EPS, ALU.mult, ALU.add).then_inc(var, 1)
                    c.at(std, 1)
                    ve.reciprocal(small[:, ROOT:ROOT + TT], small[:, ROOT:ROOT + TT]).then_inc(root, 1)
                    c.end(sums, 1)
                    c.end(std, 1)
                if not scaled:
                    c.at(spread, 1)
                    c.end(spread, 1)
                factor = bank[4 if ahead else b][:, T:2 * T]
                dst = tmp if into is None else into

                def lower(q):
                    c.at(norm_hi, q + 1)
                    if shift is None:
                        ks = slice(4 * q, 4 * q + 4)
                        ins = ve.tensor_tensor(act[:, 1, 4 * q:4 * q + 4, :], tmp[:, ks, :],
                                               act[:, 0, 4 * q:4 * q + 4, :].bitcast(F32), ALU.subtract)
                    else:
                        for k in range(4 * q, 4 * q + 4):
                            ins = ve.scalar_tensor_tensor(act[:, 1, k, :], tmp[:, k, :], modt[:, shift + k:shift + k + 1],
                                                          act[:, 0, k, :].bitcast(F32), ALU.add, ALU.subtract)
                    ins.then_inc(act_ready, 1)

                for q in range(DC // 4):
                    for k in range(4 * q, 4 * q + 4 if not scaled else 0):
                        ins = ve.scalar_tensor_tensor(dst[:, k, :], src[:, k, :], gain(k), factor, ALU.mult, ALU.mult)
                    if into is not None:
                        ins.then_inc(out_ready, 1)
                    elif not scaled:
                        ins.then_inc(normed, 1)
                    if into is None:
                        if q:
                            lower(q - 1)
                if into is None:
                    lower(DC // 4 - 1)
                    c.end(norm_hi, DC // 4)

            def g(name):
                return lambda k: par(name, k)

            for q in range(4):
                ve.wait_ge(src_in[q], 16)
            part_squares(tmp, 4)
            ve.wait_ge(params_in, 48)
            norm(h, g("norm_mix"))
            ve.wait_ge(mod_ready, 1)
            conv_x, conv_w, conv4_w = modraw[:, 0, 0:T + CF_TAPS - 1], modraw[:, 1, 0:CF_TAPS + 1], modraw[:, 1, 64:64 + 8 * 4]
            conv_mark = {}

            def conv31(ph, i0, stage=False):
                def f(i, j):
                    if stage and j == LAG:
                        chain(ve.tensor_copy(conv4_w, par("dn_conv", i * 8 * ph.K, 8 * ph.K)))
                    chunk = i + i0
                    if isinstance(chunk, int) and chunk < 0:
                        if j == ph.S - 1:
                            c.at(gate_pe, 1)
                        return
                    if j == 0:
                        ve.wait_ge(block_free, chunk + (FREE + 1))
                        ve.tensor_copy(conv_x.rearrange("p (a b) -> p a b", a=1), cin[:, ds(chunk, 1), :])
                        ve.tensor_copy(conv_w[:, 0:CF_TAPS], par("cf_conv", chunk * CF_TAPS, CF_TAPS))
                        chain(ve.tensor_copy(conv_w[:, CF_TAPS:], par("cf_b", chunk)))
                    for t in range(j * CF_TAPS // ph.S, (j + 1) * CF_TAPS // ph.S):
                        acc, x_, w = modacc[:, t % 2, 0:T], conv_x[:, t:t + T], conv_w[:, t:t + 1]
                        if t >= 2:
                            ve.wait_ge(dve_step, conv_mark[t - 2])
                        if t == 0:
                            ins = ve.tensor_scalar(acc, x_, w, conv_w[:, CF_TAPS:], ALU.mult, ALU.add)
                        elif t == 1:
                            ins = ve.tensor_scalar(acc, x_, w, None, ALU.mult)
                        else:
                            ins = ve.scalar_tensor_tensor(acc, x_, w, acc, ALU.mult, ALU.add)
                        chain.tick(ins)
                        conv_mark[t] = chain.now()
                    if j == ph.S - 1:
                        ve.wait_ge(dve_step, conv_mark[CF_TAPS - 1])
                        chain(ve.tensor_tensor(tmp[:, ds(chunk, 1), :], modacc[:, 0:1, 0:T], modacc[:, 1:2, 0:T], ALU.add))
                return f
            CONV_LINKS = 1 + CF_TAPS + 1
            before_qkv = PH["glu"].iters - 1
            phase("glu", glu, CONV_LINKS, conv31(PH["glu"], -1))
            c.end(ev_a, 8)
            phase("qkv", conv4, PH["qkv"].K * 5 + 1 + CONV_LINKS, conv31(PH["qkv"], before_qkv, stage=True))
            c.end(ev_a, 12)
            for mt in range(TT):
                ins = ve.tensor_tensor(gt[:, A1, 8 * mt:8 * mt + 8], bank[4][:, 16 * mt + 8:16 * mt + 16], par("dt", 0, 8), ALU.add)
            ins.then_inc(gate_dve, 1)
            phase("z_0", nothing, 0, conv31(PH["z_0"], before_qkv + PH["qkv"].iters))
            c.at(gate_act, 1)
            chain(ve.scalar_tensor_tensor(gt[:, GC, :], gt[:, A1, :], 0.0, gt[:, LN1, :], ALU.max, ALU.add))
            for mt in range(TT):
                r = slice(8 * mt, 8 * mt + 8)
                ins = ve.scalar_tensor_tensor(gt[:, G, r], gt[:, GC, r], -1.0, gt[:, EA, 0:8], ALU.mult, ALU.mult)
            ins.then_inc(gate_dve, 1)
            phase("z_1", nothing, 0, conv31(PH["z_1"], before_qkv + PH["qkv"].iters + 1))
            assert before_qkv + PH["qkv"].iters + 2 == 8
            ve.memset(small[:, 125:126], 0.0).then_inc(cf_dve, 1)
            c.at(cf_pe, 1)
            ve.tensor_scalar(stat[:, 0, 0:T], bank[2][:, 0:T], 1.0 / D_CONV, None, ALU.mult).then_inc(cf_dve, 1)
            c.at(cf_dve, 2)
            ve.tensor_tensor(tmp[:, 0:8, :], tmp[:, 0:8, :], stat[:, 0:1, 0:T].to_broadcast([P, 8, T]), ALU.subtract).then_inc(cf_dve, 1)
            c.at(cf_dve, 3)
            c.at(cf_act, 1)
            ve.tensor_reduce(stat[:, 0, 0:T], tmp[:, 8:16, :].rearrange("p k t -> p t k"), AX.X, ALU.add).then_inc(cf_dve, 1)
            c.at(l2_pe, 2)
            c.at(cf_pe, 2)
            ve.tensor_scalar(small[:, L2:L2 + 32], bank[5][:, 0:32], 1.0, EPS, ALU.mult, ALU.add)
            ve.tensor_scalar(small[:, L2 + 32:L2 + 34], bank[5][:, 32:34], 1.0 / D_CONV, EPS, ALU.mult, ALU.add).then_inc(l2_dve, 1)
            c.at(l2_act, 1)
            ve.reciprocal(small[:, L2:L2 + 34], small[:, L2:L2 + 34]).then_inc(l2_dve, 1)
            c.at(gate_act, 2)
            ve.tensor_tensor(gt[:, BEG, :], gt[:, BETA, :], gt[:, EGC, :], ALU.mult)
            for p in range(8):
                c.at(l2_pe, 2 + p + 1)
                o = qkvT[:, 2 * p:2 * p + 2, :]
                ve.scalar_tensor_tensor(o, o, float(P) ** -0.5 if p < 4 else 1.0, b2(4 + p % 4), ALU.mult, ALU.mult).then_inc(l2_dve, 1)
            c.at(cf_pe, 3)
            for q in range(2):
                for k in range(4 * q, 4 * q + 4):
                    ins = ve.scalar_tensor_tensor(tmp[:, k, :], tmp[:, k, :], par("ln_g", k), bank[2][:, 0:T], ALU.mult, ALU.mult)
                ins.then_inc(cf_dve, 1)
            for q in range(2):
                c.at(cf_act, 2 + q)
                ve.tensor_tensor(act[:, 1, 8 + 4 * q:12 + 4 * q, :], tmp[:, 8 + 4 * q:12 + 4 * q, :],
                                 act[:, 0, 8 + 4 * q:12 + 4 * q, :].bitcast(F32), ALU.subtract).then_inc(act_ready, 1)
            ve.memset(small[:, 127:128], 0.0).then_inc(cf_dve, 1)

            c.at(cf_dve, 7)
            c.at(l2_dve, 2 + 8)

            def every(t):
                return t.rearrange("p (a b) -> p a b", a=1).to_broadcast([P, 4, P])
            for ch in CHUNKS:
                tok = slice(ch * P, (ch + 1) * P)

                def p_(hg, name):
                    c.at(dl_pe[hg], step(PE_SIG, ch, name))

                def a(hg, name):
                    c.at(dl_act[hg], step(ACT_SIG, ch, name))

                def mine(hg, name):
                    c.at(dl_dve[hg], step(DVE_SIG, ch, name))
                for hg in GROUPS:
                    if ch:
                        c.at(dl_act[hg], step(ACT_SIG, ch - 1, "oc"))
                        a(hg, "eg")
                    p_(hg, "bc")
                    ve.tensor_tensor(DT[hg], bk(hg, 0), every(cc(CM, "below")), ALU.add).then_inc(dl_dve[hg], 1)
                    if not ch:
                        ve.tensor_tensor(gt[:, KDL, 4 * hg:4 * hg + 4], bk(hg, 0)[:, :, P - 1], gtc(GC, ch, 4 * hg, 4),
                                         ALU.subtract).then_inc(dl_dve[hg], 1)
                    if ch:
                        ve.tensor_tensor(QDT[hg], qkvT[:, 4 * hg:4 * hg + 4, tok], EG[hg], ALU.mult)
                    ve.tensor_tensor(KBT[hg], qkvT[:, 8 + 4 * hg:12 + 4 * hg, tok], bk(hg, 1), ALU.mult).then_inc(dl_dve[hg], 1)
                for hg in GROUPS:
                    p_(hg, "tr")
                    for n in range(4):
                        ins = ve.tensor_scalar(VB[hg][:, n, :], bk(hg, 3)[:, n, :], gtc(BETA, ch, 4 * hg + n), None, ALU.mult)
                    ins.then_inc(dl_dve[hg], 1)
                    p_(hg, "aa")
                    a(hg, "dtx")
                    ve.tensor_copy(X[hg], every(ident[:, :]))
                    ve.tensor_copy(XT[hg], every(ident[:, :]))
                    ve.tensor_tensor(AT[hg], bk(hg, 0), DT[hg], ALU.mult)
                    ve.tensor_tensor(ATT[hg], bk(hg, 1), DT[hg], ALU.mult).then_inc(dl_dve[hg], 1)
                    mine(hg, "aat")

                def masked(hg, lv):
                    ve.tensor_tensor(MT[hg], AT[hg], every(cc(CM, "levels")[:, lv * P:(lv + 1) * P]), ALU.mult).then_inc(dl_dve[hg], 1)
                for hg in GROUPS:
                    masked(hg, 0)
                for lv in range(LEVELS):
                    if lv + 1 < LEVELS:
                        for hg in GROUPS:
                            p_(hg, f"y{lv}")
                            masked(hg, lv + 1)
                    for hg in GROUPS:
                        p_(hg, f"z{lv}")
                        if lv:
                            mine(hg, f"x{lv - 1}")
                        if lv + 1 < LEVELS:
                            ve.tensor_tensor(X[hg], X[hg], bk(hg, 2), ALU.subtract)
                        ve.tensor_tensor(XT[hg], XT[hg], bk(hg, 3), ALU.subtract).then_inc(dl_dve[hg], 1)
                if ch:
                    for hg in GROUPS:
                        p_(hg, "ws")
                        ve.tensor_tensor(VN[hg], U_[hg], bk(hg, 0), ALU.subtract).then_inc(dl_dve[hg], 1)
            c.at(on_pe, 1)
            ve.tensor_scalar(small[:, ON:ON + 16], bank[4][:, 0:16], 1.0 / P, EPS, ALU.mult, ALU.add).then_inc(on_dve, 1)
            c.at(on_act, 2 + 1)
            ve.reciprocal(small[:, ON:ON + 16], small[:, ON:ON + 16]).then_inc(on_dve, 1)
            for p in range(5):
                if p < 4:
                    c.at(on_pe, p + 2)
                    o = qkvT[:, 16 + 2 * p:18 + 2 * p, :]
                    chain(ve.scalar_tensor_tensor(o, o, par("dn_norm"), b2(4 + p), ALU.mult, ALU.mult))
                    ve.tensor_tensor(o, o, zT[:, 2 * p:2 * p + 2, :], ALU.mult).then_inc(on_dve, 1)
                if p:
                    c.at(on_act, 3 + p)
                    ve.tensor_tensor(act[:, 1, 2 * p - 2:2 * p, :], qkvT[:, 14 + 2 * p:16 + 2 * p, :],
                                     act[:, 0, 2 * p - 2:2 * p, :].bitcast(F32), ALU.subtract).then_inc(act_ready, 1)
            ve.memset(small[:, 121:122], 0.0).then_inc(mod_used, MOD_N)
            ve.memset(small[:, 126:127], 0.0).then_inc(mixed, 1)
            def memory_sums(i, j):
                if isinstance(i, int) and i == 0 and j == PH["wout"].S - 1:
                    for q in range(4):
                        c.at(mem_sq, q + 1)
                        ins = ve.tensor_reduce(memK[:, q, :],
                                               tmp[:, 4 * q:4 * q + 4, :].rearrange("p k t -> p t k"), AX.X, ALU.add)
                    ins.then_inc(mem_sum, 1)
            residual("wout", extra=memory_sums)

            norm(memory, g("norm_mem"))
            phase("memk", nothing, 0, h_norm(4))
            phase("memv", nothing)
            norm(h, g("norm_xa"), ahead=True)
            phase("wq", nothing)

            def attention(kind, c0=0):
                units = attention_units(kind)
                nk = key_tiles(kind) * P
                scale = {"cross": XA_SCALE, "mla": MLA_SCALE, "na": 1.0}[kind]
                for u in range(len(units) + 2):
                    if u < len(units):
                        hd, mt = units[u]
                        pb = stat[:, u % 2, 0:nk]
                        b = bank[3 + u % 2]
                        m = SM + 4 * (u % 2)
                        c.at(scores, u + 1)
                        if u >= 2:
                            c.at(probs_t, u - 1)
                        src = b[:, 0:nk]
                        if kind == "na":
                            ve.scalar_tensor_tensor(pb[:, 0:T], b[:, 0:T], NA_SCALE, bias[:, hd, mt, :], ALU.mult, ALU.add)
                            chain(ve.tensor_scalar(pb[:, T:2 * T], b[:, T:2 * T], NA_SCALE, None, ALU.mult))
                            src = pb
                        chain(ve.tensor_reduce(small[:, m:m + 1], src, AX.X, ALU.max))
                        ve.tensor_scalar(small[:, m + 1:m + 2], small[:, m:m + 1], -scale, None, ALU.mult).then_inc(maxes, 1)
                        c.at(exps, u + 1)
                        chain(ve.reciprocal(small[:, m + 3:m + 4], small[:, m + 2:m + 3]))
                        ve.tensor_scalar(pb, pb, small[:, m + 3:m + 4], None, ALU.mult).then_inc(probs, 1)
                    if u >= 3 and u % 2 == 1:
                        hd = (u - 3) // 2
                        c.at(head_hi, hd + 1)
                        if kind == "cross":
                            for k in range(2):
                                ks = slice(XA_CH * hd + 2 * k, XA_CH * hd + 2 * k + 2)
                                ins = ve.tensor_tensor(act[:, 1, ks, :], b2(k), act[:, 0, ks, :].bitcast(F32), ALU.subtract)
                        else:
                            ins = ve.tensor_tensor(act[:, 1, c0 + hd, :], bank[0][:, 0:T], act[:, 0, c0 + hd, :].bitcast(F32),
                                                   ALU.subtract)
                        ins.then_inc(act_ready, 1)
                for s_ in (scores, exps, probs_t):
                    c.end(s_, len(units))
                c.end(head_hi, len(units) // 2)

            attention("cross")
            residual("wo")

            norm(h, g("norm_mlp"))
            for r in range(FF1_ROUNDS):
                phase(f"w1_{r}", relu2)
                c.end(ev_a, PH["w1_0"].nblocks)
                if r == FF1_ROUNDS - 1:
                    residual(f"w2_{r}")
                else:
                    phase(f"w2_{r}", resid())
            chain(mod_store(MOD_BODIES, 1))
            for w, to_, n in ((0, 0, 96), (1, 96, 32)):
                ins = ve.tensor_tensor(modt[:, to_:to_ + n], msum[:, w, 0:n], par("b_mod", 0, n), ALU.add)
            chain(ins)
            for to_, sc_at, name in ((GAIN_X, 16, "g_attn"), (GAIN_C, 112, "g_attn"), (GAIN_F, 64, "g_ffn")):
                chain(ve.scalar_tensor_tensor(small[:, to_:to_ + DC], modt[:, sc_at:sc_at + DC], 1.0, par(name, 0, DC), ALU.add, ALU.mult))

            def gs(at):
                return lambda k: small[:, at + k:at + k + 1]
            h_norm(0, 5)(0, 0)
            part_squares(context_sq, 4)
            h_norm(-2, 5)(0, 0)
            c.end(spread, 1)
            norm(tmp, gs(GAIN_C), shift=96)

            def block_norm(i, j):
                if j < 4:
                    for k in range(4 * j, 4 * j + 4):
                        ins = ve.scalar_tensor_tensor(h[:, k, :], h[:, k, :], par("norm_final", k), bank[5][:, T:2 * T], ALU.mult, ALU.mult)
                    ins.then_inc(h_normed, 1)
                else:
                    q = j - 4
                    c.at(h_sq, q + 1)
                    ins = ve.tensor_reduce(ev[:, q // 2, q % 2 * T:(q % 2 + 1) * T],
                                           tmp[:, 4 * q:4 * q + 4, :].rearrange("p k t -> p t k"), AX.X, ALU.add)
                    if q == 3:
                        ins.then_inc(h_sum, 1)

            def next_norm(i, j):
                if j >= 4:
                    c.at(spread, 1)
                    for k in range(4 * j - 16, 4 * j - 12):
                        ins = ve.scalar_tensor_tensor(tmp[:, k, :], h[:, k, :], gs(GAIN_X)(k), bank[5][:, T:2 * T], ALU.mult, ALU.mult)
                    ins.then_inc(normed, 1)
            phase("ckv_c", nothing, 0, block_norm)
            phase("nak_c", nothing, 0, h_norm(4, 5))
            phase("nav_c", nothing, 0, next_norm)
            c.end(spread, 1)
            phase("kr_c", nothing)
            norm(h, gs(GAIN_X), shift=0, scaled=True)
            for name in ("ckv_x", "nak_x", "nav_x", "cq", "naq", "fn", "kr_x"):
                phase(name, nothing)
            ve.wait_ge(bias_in, 32)
            for hd in range(NA_H):
                chain(ve.tensor_tensor(bias[:, hd, :, :], bias[:, hd, :, :], mask[:, :, :], ALU.add))
            attention("na", 8)
            for gg in range(FN_G):
                c.at(head_hi, gg + 1)
                ve.tensor_tensor(act[:, 1, 12 + gg, :], bank[0][:, 0:T], act[:, 0, 12 + gg, :].bitcast(F32), ALU.subtract).then_inc(act_ready, 1)
            c.end(head_hi, FN_G)
            part_squares(tmp, 3)
            c.at(sums, 1)
            ve.tensor_scalar(small[:, ROOT:ROOT + 6], bank[3][:, 0:6], 1.0 / LAT, EPS, ALU.mult, ALU.add).then_inc(var, 1)
            c.at(std, 1)
            ve.reciprocal(small[:, ROOT:ROOT + 6], small[:, ROOT:ROOT + 6]).then_inc(root, 1)
            c.end(sums, 1)
            c.end(std, 1)

            def latent_lower(n, c0):
                c.at(norm_hi, n + 1)
                ve.tensor_tensor(act[:, 1, c0:c0 + LC, :], tmp[:, LC * n:LC * (n + 1), :],
                                 act[:, 0, c0:c0 + LC, :].bitcast(F32), ALU.subtract).then_inc(act_ready, 1)
            for n, (src, gain) in enumerate(((ckv[:, 1, :, :], "g_kv"), (ckv[:, 0, :, :], "g_kv"), (cq[:, :, :], "g_q"))):
                c.at(spread, n + 1)
                for k in range(LC):
                    ins = ve.scalar_tensor_tensor(tmp[:, LC * n + k, :], src[:, k, :], par(gain, k), bank[5 + n][:, 0:T],
                                                  ALU.mult, ALU.mult)
                ins.then_inc(normed, 1)
                if n:
                    latent_lower(n - 1, LC * (n - 1))
            c.end(spread, 3)
            phase("kn_c", nothing)
            phase("v_c", nothing)
            latent_lower(2, 0)
            c.end(norm_hi, 3)
            phase("kn_x", nothing)
            phase("v_x", nothing)
            phase("qn", nothing)
            phase("qr", nothing)
            ve.wait_ge(block_free, FREE + PH["qr"].block0 + PH["qr"].nblocks)
            ve.wait_ge(late_in, 16)
            for n in range(1 + MLA_H // 2):
                x_ = kr[:, 0, :] if n == 0 else qR[:, n - 1, :]
                c.at(rope_pe, n + 1)
                if n:
                    c.at(rope_dve, n)
                ve.tensor_tensor(stat[:, 0, 0:T], x_, cc(CA, "cos"), ALU.mult)
                chain(ve.tensor_tensor(stat[:, 1, 0:T], bank[3 + n][:, 0:T], cc(CA, "sin"), ALU.mult))
                ve.tensor_tensor(x_, stat[:, 0, 0:T], stat[:, 1, 0:T], ALU.add).then_inc(rope_dve, 1)
            attention("mla")
            residual("wout2", 32)
            norm(h, gs(GAIN_F), shift=48)
            first = 0
            for r, n in enumerate(FF2_ROUNDS):
                phase(f"up_{r}", gated(first), 2 * 5)
                c.end(ev_a, 2 * n)
                first += n
                if r == len(FF2_ROUNDS) - 1:
                    residual(f"down_{r}", 80)
                else:
                    phase(f"down_{r}", resid(80))
            norm(h, g("g_final"), into=tmp)


def slots_of(w, ph, cols=None):
    if cols is not None:
        w = np.concatenate([w[:, a:b] for a, b in cols], axis=1)
    n = ph.nblocks * ph.ncol
    assert w.shape == (ph.chunks * P, n), (ph.name, w.shape)
    w = w.reshape(ph.slots_per_block, ph.per_slot, P, ph.nblocks, ph.ncol)
    return w.transpose(3, 0, 2, 1, 4).reshape(ph.slots, P, SLOT)


def per_partition(v):
    return np.ascontiguousarray(v).reshape(-1, P).T


def feature_major(x):
    return x.reshape(T, -1, P).transpose(2, 1, 0).reshape(P, -1)


def kernel(**a):
    import concourse.bacc as bacc
    from concourse.bass_utils import run_bass_kernel_spmd

    a = {k: np.asarray(v) for k, v in a.items()}
    w_in, w_in2 = a["w_in"][0], a["w_in_2"][0]
    parts = {}
    parts["qkv"] = slots_of(w_in[:, 0:3072], PH["qkv"])
    for n in range(2):
        parts[f"z_{n}"] = slots_of(w_in[:, 3072 + 512 * n:3584 + 512 * n], PH[f"z_{n}"])
    w_ba = w_in[:, 4096:4112]
    g0 = 4112
    parts["glu"] = slots_of(w_in, PH["glu"], [c for i in range(8) for c in (
        (g0 + P * i, g0 + P * (i + 1)), (g0 + 1024 + P * i, g0 + 1024 + P * (i + 1)))])
    parts["wout"] = slots_of(a["w_out"][0], PH["wout"])
    parts["memk"] = slots_of(a["xa_wk"][0], PH["memk"])
    parts["memv"] = slots_of(a["xa_wv"][0], PH["memv"])
    parts["wq"] = slots_of(a["xa_wq"][0], PH["wq"])
    parts["wo"] = slots_of(a["xa_wo"][0], PH["wo"])
    for r in range(FF1_ROUNDS):
        parts[f"w1_{r}"] = slots_of(a["mlp_w1"][0][:, D * r:D * (r + 1)], PH[f"w1_{r}"])
        parts[f"w2_{r}"] = slots_of(a["mlp_w2"][0][D * r:D * (r + 1), :], PH[f"w2_{r}"])
    at = {}
    o = 0
    for name, n in (("cq", LAT), ("ckv", LAT), ("kr", ROPE), ("naq", 512), ("nak", 512), ("nav", 512), ("fn", 512)):
        at[name] = (o, o + n)
        o += n
    for name in ("ckv", "nak", "nav"):
        for who in "cx":
            parts[f"{name}_{who}"] = slots_of(w_in2, PH[f"{name}_{who}"], [at[name]])
    for who in "cx":
        parts[f"kr_{who}"] = slots_of(w_in2, PH[f"kr_{who}"], [at["kr"], at["kr"]])
    for name in ("cq", "naq", "fn"):
        parts[name] = slots_of(w_in2, PH[name], [at[name]])
    ukv, uq = a["w_ukv_2"][0], a["w_uq_2"][0]
    for who in "cx":
        parts[f"kn_{who}"] = slots_of(ukv, PH[f"kn_{who}"], [(256 * i, 256 * i + 128) for i in range(MLA_H)])
        parts[f"v_{who}"] = slots_of(ukv, PH[f"v_{who}"], [(256 * i + 128, 256 * i + 256) for i in range(MLA_H)])
    parts["qn"] = slots_of(uq, PH["qn"], [(192 * i, 192 * i + 128) for i in range(MLA_H)])
    parts["qr"] = slots_of(uq, PH["qr"], [(192 * i + 128, 192 * i + 192) for i in range(MLA_H)])
    parts["wout2"] = slots_of(a["w_out_2"][0], PH["wout2"])
    first = 0
    for r, n in enumerate(FF2_ROUNDS):
        parts[f"up_{r}"] = slots_of(a["w_up_2"][0], PH[f"up_{r}"], [c for i in range(first, first + n) for c in (
            (P * i, P * (i + 1)), (D_FF2 + P * i, D_FF2 + P * (i + 1)))])
        parts[f"down_{r}"] = slots_of(a["w_down_2"][0][P * first:P * (first + n)], PH[f"down_{r}"])
        first += n
    stream = np.empty((N_SLOTS, P, SLOT), np.float32)
    for name, ph in PH.items():
        stream[ph.slot0:ph.slot0 + ph.slots] = parts.pop(name)
    mods = a["w_mod_2"][0].reshape(DC // 2, 2, P, MOD_BODIES, MOD_COL).transpose(3, 0, 2, 1, 4).reshape(-1, P, SLOT)

    def paired(v):
        v = v.reshape(v.shape[:-1] + (2, D_FF2 // P, P))
        return v.swapaxes(-3, -2).reshape(v.shape[:-3] + (88, P))

    vec = {
        "norm_mix": per_partition(a["norm_mix_g"]), "norm_mem": per_partition(a["norm_mem_g"]),
        "norm_xa": per_partition(a["norm_xa_g"]), "norm_mlp": per_partition(a["norm_mlp_g"]),
        "norm_final": per_partition(a["norm_final_g"]), "g_attn": per_partition(a["g_attn_2"]),
        "g_ffn": per_partition(a["g_ffn_2"]), "g_final": per_partition(a["g_final_2"]),
        "g_q": per_partition(a["g_q_2"]), "g_kv": per_partition(a["g_kv_2"]), "dn_norm": per_partition(a["dn_norm_g"]),
        "cf_b": per_partition(a["cf_dw_b"]), "ln_g": per_partition(a["cf_ln_g"]), "ln_b": per_partition(a["cf_ln_b"]),
        "dn_conv": a["dn_conv_w"][0].reshape(DN_TAPS, 24, P).transpose(2, 1, 0).reshape(P, -1),
        "cf_conv": a["cf_dw_w"][0].reshape(CF_TAPS, 8, P).transpose(2, 1, 0).reshape(P, -1),
        "ff_conv": paired(a["conv_w_2"][0]).transpose(2, 1, 0).reshape(P, -1),
        "ff_b": paired(a["conv_b_2"][0]).T, "b_mod": per_partition(a["b_mod_2"]),
        "c": per_partition(a["c_2"]), "c_ctx": per_partition(a["c_ctx_2"]),
        "a_log": np.broadcast_to(a["dn_a_log"][0], (P, 8)), "dt": np.broadcast_to(a["dn_dt_bias"][0], (P, 8)),
    }
    pvec = np.concatenate([vec[name] for name in PV], axis=1)
    eye = np.concatenate([np.eye(P), np.ones((P, P))], axis=1).astype(np.float32)
    i, j = np.arange(P)[:, None], np.arange(P)[None, :]
    levels = [((i // (2 * s) == j // (2 * s)) & (i % (2 * s) < s) & (j % (2 * s) >= s)).astype(np.float32) for s in (1, 2, 4, 8, 16, 32, 64)]
    upper = (i <= j).astype(np.float32)
    below = np.where(i <= j, 0.0, NEG).astype(np.float32)
    cmix = np.concatenate(levels + [upper, below, w_ba.reshape(DC, P, 16).transpose(1, 0, 2).reshape(P, -1)], axis=1)
    ang = 2 * np.pi * ((i * j) % P) / P
    dft_ch = np.concatenate([np.cos(ang), np.sin(ang)], axis=1)
    tt = np.arange(T)
    ang = 2 * np.pi * ((tt[:, None] * tt[None, :]) % T) / T

    def rows(m):
        return m.reshape(TT, P, T).transpose(1, 0, 2).reshape(P, -1)
    freqs = np.float32(10000.0) ** (-np.arange(16, dtype=np.float32) / 16)
    f = np.arange(P) % ROPE
    pos = np.where(f[:, None] < 32, tt[None, :] // GRID_W, tt[None, :] % GRID_W).astype(np.float32)
    angle = pos * freqs[f % 16][:, None]
    sign = np.where(f % 32 < 16, -1.0, 1.0)[:, None]
    swap = (i == (j ^ 16)).astype(np.float32)
    catt = np.concatenate([dft_ch, rows(np.cos(ang)), rows(-np.sin(ang)), np.cos(angle), sign * np.sin(angle), swap,
                           ], axis=1).astype(np.float32)
    catt = np.concatenate([catt, a["w_fnet_2"][0].transpose(1, 0, 2).reshape(P, -1)], axis=1)
    qr_, qw, kr_, kw = tt[:, None] // GRID_W, tt[:, None] % GRID_W, tt[None, :] // GRID_W, tt[None, :] % GRID_W
    start = np.clip(qw - NA_KW // 2, 0, GRID_W - NA_KW)
    inside = (kw >= start) & (kw < start + NA_KW)
    rel_col = np.clip(kw - qw + NA_KW - 1, 0, 2 * NA_KW - 2)
    table = a["na_rpb_2"][0][:, kr_ - qr_ + NA_KH - 1, rel_col]
    na_bias = table.reshape(NA_H, TT, P, T).transpose(2, 0, 1, 3).reshape(P, -1)
    na_mask = np.where(inside, 0.0, NEG).astype(np.float32).reshape(TT, P, T).transpose(1, 0, 2).reshape(P, -1)

    arrays = {
        "x_t": feature_major(a["x"][0]).reshape(P, DC, T), "mem_t": feature_major(a["mem"][0]), "ctx_t": feature_major(a["ctx_2"][0]),
        "stream": stream, "mods": mods, "pvec": pvec, "eye": eye, "cmix": cmix, "catt": catt, "na_bias": na_bias, "na_mask": na_mask,
    }
    nc = bacc.Bacc("TRN2", target_bir_lowering=False, num_devices=1)
    args = []
    for name, v in arrays.items():
        arrays[name] = np.ascontiguousarray(v)
        args.append(nc.dram_tensor(name, v.shape, mybir.dt.from_np(v.dtype), kind="ExternalInput").ap())
    args.append(nc.dram_tensor("out_t", (P, DC, T), F32, kind="ExternalOutput").ap())
    build(nc, *args)
    got = run_bass_kernel_spmd(nc, [arrays], core_ids=[0]).results[0]["out_t"]
    return got.transpose(2, 1, 0).reshape(1, T, D)
```
